# Optimizing a Trainium2 kernel written in Bass

```python
import math
import jax, jax.numpy as jnp
from jax import lax
import numpy as np

D_MODEL = 1024
BATCH = 1
SEQ = 1024
DEPTH = 2

CHUNK = 64
Q_BLOCK = 128
N_MIXERS = 2
BRANCH_WIDTH = D_MODEL
IN_WIDTH = 4 * BRANCH_WIDTH
SB_HEADS = 16
SB_HEAD_DIM = BRANCH_WIDTH // SB_HEADS
DIFF_HEADS = 8
DIFF_HEAD_DIM = BRANCH_WIDTH // (2 * DIFF_HEADS)
N_DIFF_LAYERS = DEPTH // N_MIXERS
ALIBI_MAX_EXP = 8.0
RMS_EPS = 1e-6
NEG_INF = -1e30

kernel_name = "hybrid_stickbreak_diffattn_adaln_trunk"

def rms_norm(x, g):
    xf = x.astype(jnp.float32)
    y = xf * lax.rsqrt(jnp.mean(xf * xf, axis=-1, keepdims=True) + RMS_EPS)
    return (y * g.astype(jnp.float32)).astype(x.dtype)

def split_query_blocks(t):
    s, e = t.shape[-2], t.shape[-1]
    t = t.reshape(t.shape[:-2] + (s // Q_BLOCK, Q_BLOCK, e))
    return jnp.moveaxis(t, -3, 0)

def merge_query_blocks(t):
    nb, b, h, q, e = t.shape
    t = jnp.moveaxis(t, 0, 2).reshape(b, h, nb * q, e)
    return t.transpose(0, 2, 1, 3).reshape(b, nb * q, h * e)

def alibi_slopes(n_heads):
    exps = jnp.arange(1, n_heads + 1, dtype=jnp.float32) * (ALIBI_MAX_EXP / n_heads)
    return jnp.exp2(-exps)

def stick_breaking_attention(qkv):
    b, s, _ = qkv.shape
    q, k, v = jnp.split(qkv, 3, axis=-1)
    heads = lambda t: t.reshape(b, s, SB_HEADS, SB_HEAD_DIM).transpose(0, 2, 1, 3)
    q, k, v = heads(q), heads(k), heads(v)
    key_pos = jnp.arange(s)
    scale = SB_HEAD_DIM ** -0.5

    def block(args):
        qb, blk = args
        q_pos = blk * Q_BLOCK + jnp.arange(Q_BLOCK)
        strict = key_pos[None, :] < q_pos[:, None]
        logits = jnp.einsum('bhqd,bhsd->bhqs', qb, k).astype(jnp.float32) * scale
        log_beta = jax.nn.log_sigmoid(logits)
        log_keep = jnp.where(strict, log_beta - logits, 0.0)
        between = lax.cumsum(log_keep, axis=3, reverse=True) - log_keep
        weights = jnp.where(strict, jnp.exp(log_beta + between), 0.0)
        return jnp.einsum('bhqs,bhsd->bhqd', weights.astype(v.dtype), v)

    out = lax.map(block, (split_query_blocks(q), jnp.arange(s // Q_BLOCK)))
    return merge_query_blocks(out)

def diff_attention(qkv, lam, g_sub, lam_init):
    b, s, _ = qkv.shape
    q, k, v = jnp.split(qkv, 3, axis=-1)
    qk_heads = lambda t: t.reshape(b, s, DIFF_HEADS, 2, DIFF_HEAD_DIM).transpose(3, 0, 2, 1, 4)
    q, k = qk_heads(q), qk_heads(k)
    v = v.reshape(b, s, DIFF_HEADS, 2 * DIFF_HEAD_DIM).transpose(0, 2, 1, 3)
    lamf = lam.astype(jnp.float32)
    lam_full = jnp.exp(jnp.sum(lamf[0] * lamf[1])) - jnp.exp(jnp.sum(lamf[2] * lamf[3])) + lam_init
    slopes = alibi_slopes(DIFF_HEADS)
    key_pos = jnp.arange(s)
    key_chunk = key_pos // CHUNK
    scale = DIFF_HEAD_DIM ** -0.5

    def block(args):
        qb, blk = args
        q_pos = blk * Q_BLOCK + jnp.arange(Q_BLOCK)
        visible = key_chunk[None, :] <= (q_pos // CHUNK)[:, None]
        dist = jnp.abs(q_pos[:, None] - key_pos[None, :]).astype(jnp.float32)
        bias = jnp.where(visible[None], -slopes[:, None, None] * dist[None], NEG_INF)
        logits = jnp.einsum('nbhqd,nbhsd->nbhqs', qb, k).astype(jnp.float32) * scale + bias[None, None]
        probs = jax.nn.softmax(logits, axis=-1)
        weights = probs[0] - lam_full * probs[1]
        return jnp.einsum('bhqs,bhse->bhqe', weights.astype(v.dtype), v)

    out = lax.map(block, (split_query_blocks(q), jnp.arange(s // Q_BLOCK)))
    out = merge_query_blocks(out).reshape(b, s, DIFF_HEADS, 2 * DIFF_HEAD_DIM)
    out = rms_norm(out, g_sub) * (1.0 - lam_init)
    return out.reshape(b, s, BRANCH_WIDTH)

def diff_lambda_init(layer_idx):
    return 0.8 - 0.6 * math.exp(-0.3 * layer_idx)

def setup_inputs(seed: int = 0) -> dict:
    key = jax.random.key(seed)
    ks = jax.random.split(key, 12)
    d = D_MODEL
    f = jnp.float32
    x = jax.random.normal(ks[0], (BATCH, SEQ, d), f)
    c = jax.random.normal(ks[1], (BATCH, d), f)
    w_ada = jax.random.normal(ks[2], (DEPTH, d, 3 * d), f) * (0.5 * d ** -0.5)
    b_ada = jax.random.normal(ks[3], (DEPTH, 3 * d), f) * 0.01
    g_pre = 1.0 + 0.1 * jax.random.normal(ks[4], (DEPTH, d), f)
    g_post = 1.0 + 0.1 * jax.random.normal(ks[5], (DEPTH, d), f)
    w_in = jax.random.normal(ks[6], (DEPTH, d, IN_WIDTH), f) * d ** -0.5
    w_out = jax.random.normal(ks[7], (DEPTH, BRANCH_WIDTH, d), f) * BRANCH_WIDTH ** -0.5
    diff_lambda = 0.1 * jax.random.normal(ks[8], (N_DIFF_LAYERS, 4, DIFF_HEAD_DIM), f)
    diff_subln = 1.0 + 0.1 * jax.random.normal(ks[9], (N_DIFF_LAYERS, 2 * DIFF_HEAD_DIM), f)
    return {"x": x, "c": c, "w_ada": w_ada, "b_ada": b_ada, "g_pre": g_pre, "g_post": g_post,
            "w_in": w_in, "w_out": w_out, "diff_lambda": diff_lambda, "diff_subln": diff_subln}

def reference(x, c, w_ada, b_ada, g_pre, g_post, w_in, w_out, diff_lambda, diff_subln):
    cond = jax.nn.silu(c)
    for i in range(DEPTH):
        ada = cond @ w_ada[i] + b_ada[i]
        shift, scale, gate = jnp.split(ada[:, None, :], 3, axis=-1)
        h = rms_norm(x, g_pre[i]) * (1.0 + scale) + shift
        u = h @ w_in[i]
        mix_in, z = u[..., :3 * BRANCH_WIDTH], u[..., 3 * BRANCH_WIDTH:]
        if i % N_MIXERS == 0:
            y = stick_breaking_attention(mix_in)
        else:
            j = i // N_MIXERS
            y = diff_attention(mix_in, diff_lambda[j], diff_subln[j], diff_lambda_init(i))
        y = (y * jax.nn.silu(z)) @ w_out[i]
        x = x + gate * rms_norm(y, g_post[i])
    return x


_drawn_inputs = setup_inputs


def setup_inputs(seed=0):
    import zlib

    import numpy as np

    out = dict(_drawn_inputs(seed))
    spreads = {}
    factors = {'b_ada': 3.234}
    for name, (base, spread) in spreads.items():
        noise = np.random.default_rng([zlib.crc32(name.encode()), seed]).standard_normal(out[name].shape)
        drawn = base * np.exp(spread * noise) if base else spread * noise
        out[name] = __import__('jax').numpy.asarray(drawn.astype(out[name].dtype))
    for name, factor in factors.items():
        out[name] = (out[name] * factor).astype(out[name].dtype)
    return out
```

```python
import math

import concourse.bass as bass
from concourse import mybir

F32 = mybir.dt.float32
F32R = mybir.dt.float32r
BF16 = mybir.dt.bfloat16
I32 = mybir.dt.int32
ALU = mybir.AluOpType
ACT = mybir.ActivationFunctionType
AX = mybir.AxisListType

P = 128
D = 1024
S = 1024
KT = D // P
NT = S // P
HALF = 512
PAIRS = D // P
HD = 64
GW = 2 * P
NG = NT // 2
SCALE = HD ** -0.5
CHUNK = 64
EPS = 1e-6
NEG = -1e30
DEPTH = 2
CREDIT = 32
MULS = 3
GROUP = MULS * KT
KB = 1024


def done(n):
    return CREDIT + 1 + n


def widths(i):
    w = P * (i + 1)
    return [(c, min(HALF, w - c)) for c in range(0, w, HALF)]


def shares(total, weights):
    whole, acc, cut = sum(weights), 0, [0]
    for w in weights:
        acc += w
        cut.append(round(total * acc / whole))
    return list(zip(cut[:-1], cut[1:]))


def trunk(nc, x, c, w_ada, b_ada, g_pre, g_post, w_in, w_out, diff_lambda, diff_subln, out):
    base = (nc.sbuf_base + 63) // 64 * 64
    placed = {}

    def sb(name, shape, dtype, kb):
        placed[name] = nc.alloc_sbuf_tensor_at(name, shape, dtype, offset=base + int(kb * KB))
        return placed[name]

    x1 = nc.dram_tensor("x_between", [S, D], F32, kind="Internal").ap()
    gate_rows = nc.dram_tensor("gate_rows", [DEPTH, D], F32, kind="Internal").ap()

    m = {}
    m["h_hi"] = sb("h_hi", [P, KT, S], F32R, 0)
    m["h_lo"] = sb("h_lo", [P, KT, S], F32R, 32)
    m["ada_w"] = sb("ada_w", [P, KT, 3 * D], F32, 0)
    m["wo_hi"] = sb("wo_hi", [P, KT, D], F32R, 0)
    m["wo_raw"] = sb("wo_raw", [P, KT, D], F32, 32)
    m["wo_lo"] = sb("wo_lo", [P, KT, D], F32R, 32)
    m["y"] = sb("y", [P, KT, S], F32, 64)
    m["w_hi"] = [sb(f"w_hi{s}", [P, KT, P], F32R, 96 + 8 * s) for s in range(2)]
    m["w_raw"] = [sb(f"w_raw{s}", [P, KT, P], F32, 100 + 8 * s) for s in range(2)]
    m["w_lo"] = [sb(f"w_lo{s}", [P, KT, P], F32R, 100 + 8 * s) for s in range(2)]
    m["uq"] = sb("uq", [P, S], F32, 112)
    m["uk"] = sb("uk", [P, S], F32, 116)
    m["uv"] = sb("uv", [P, S], F32, 120)
    m["sz"] = sb("sz", [P, S], F32, 124)
    m["q"] = [sb(f"q{h}", [P, S], F32R, 128 + 4 * h) for h in range(2)]
    m["k_hi"] = [sb(f"k_hi{h}", [P, S], F32R, 136 + 4 * h) for h in range(2)]
    m["k_lo"] = [sb(f"k_lo{h}", [P, S], F32R, 144 + 4 * h) for h in range(2)]
    m["v"] = [sb(f"v{h}", [P, NT, P], F32R, 152 + 4 * h) for h in range(2)]
    m["a"] = [sb(f"a{r}", [P, S], F32, 160 + 4 * r) for r in range(3)]
    m["b"] = [sb(f"b{r}", [P, S], F32, 172 + 4 * r) for r in range(2)]
    m["stick"] = [sb(f"stick{r}", [P, S + 1], F32, 180 + 4.0625 * r) for r in range(2)]
    m["bias"] = sb("bias", [P, S], F32, 180)
    m["sub_sq"] = [sb(f"sub_sq{r}", [P, GW], F32, 184 + r) for r in range(2)]
    m["sub_rs"] = [sb(f"sub_rs{r}", [P, GW], F32, 186 + r) for r in range(2)]
    m["dist"] = sb("dist", [P, S], I32, 160)
    m["wt_hi"] = sb("wt_hi", [P, NT, GW], F32R, 188.125)
    m["wt_lo"] = sb("wt_lo", [P, NT, GW], F32R, 196.125)
    at = [204.125]

    def small(name, shape, dtype, nbytes):
        t = sb(name, shape, dtype, at[0])
        at[0] += (nbytes + 63) // 64 * 64 / KB
        return t

    m["o_part"] = small("o_part", [P, GW], F32, 4 * GW)
    m["ident"] = small("ident", [P, P], F32, 4 * P)
    m["ones"] = small("ones", [P, P], F32, 4 * P)
    m["ident_b"] = small("ident_b", [P, P], BF16, 2 * P)
    m["mask_b"] = small("mask_b", [P, P], BF16, 2 * P)
    m["mul_col"] = [small(f"mul_col{l}", [P, KT], F32, 4 * KT) for l in range(DEPTH)]
    m["add_col"] = [small(f"add_col{l}", [P, KT], F32, 4 * KT) for l in range(DEPTH)]
    m["lam"] = small("lam", [P, 8], F32, 32)
    m["eps"] = small("eps", [P, 1], F32, 4)
    m["stat"] = small("stat", [P, 32], F32, 128)
    m["pm"] = [nc.alloc_psum_tensor(f"bank{i}", [P, HALF], F32) for i in range(8)]
    assert base + at[0] * KB <= nc.sbuf_usable_end, (base + at[0] * KB, nc.sbuf_usable_end)

    condition(nc, m, sb, c, w_ada, b_ada, g_pre, g_post, diff_lambda, diff_subln, gate_rows)
    for layer in range(DEPTH):
        source, target = (x, x1) if layer == 0 else (x1, out)
        normalise(nc, m, sb, layer, source)
        if layer % 2 == 0:
            stick_breaking(nc, m, w_in[layer], w_out[layer])
        else:
            differential(nc, m, w_in[layer], w_out[layer])
        project_out(nc, m, sb, layer, source, target, gate_rows)


def condition(nc, m, sb, c, w_ada, b_ada, g_pre, g_post, diff_lambda, diff_subln, gate_rows):
    n = {}

    def sem(name):
        n[name] = nc.alloc_semaphore("c_" + name)
        return n[name]

    cond = sb("cond", [P, KT], F32, 128)
    cond_sig = sb("cond_sig", [P, KT], F32, 128.25)
    cond_act = sb("cond_act", [P, KT], F32, 128.5)
    b_cols = sb("b_cols", [P, DEPTH, 2 * KT], F32, 129)
    g_cols = sb("g_cols", [P, DEPTH, KT], F32, 130)
    row_b = sb("row_b", [1, DEPTH, D], F32, 132)
    row_g = sb("row_g", [1, DEPTH, D], F32, 140)
    row = sb("row", [1, DEPTH, D], F32, 148)
    scale1 = sb("scale1", [P, DEPTH, KT], F32, 156)
    lam_in = sb("lam_in", [P, 4, HD], F32, 157)
    lam_prod = sb("lam_prod", [P, 2, HD], F32, 158)
    lam_sums = sb("lam_sums", [P, 4], F32, 159)
    PIECE = 2 * P
    NP_ = 3 * D // PIECE
    small_in = sem("small_loaded")
    ada_in = [sem(f"ada_loaded{i}") for i in range(NP_)]
    cond_sig_done, cond_done = sem("cond_sig_done"), sem("cond_done")
    cols_done, cols_used, row_done, row_used = sem("cols_done"), sem("cols_used"), sem("row_done"), sem("row_used")
    row_stored = sem("row_stored")
    zeroed, consts, chain = sem("zeroed"), sem("consts"), sem("vector_chain")
    lam_exp, lam_sum = sem("lam_exp"), sem("lam_sum")
    lam_init = 0.8 - 0.6 * math.exp(-0.3 * 1)
    bank = m["pm"]

    with nc.Block() as block:

        @block.sync
        def _(sp):
            with nc.allow_non_contiguous_dma(reason="small vectors, feature on the partition"):
                sp.dma_start(cond[:, :], c.rearrange("b (k p) -> p (b k)", p=P)).then_inc(small_in, 16)
                for layer in range(DEPTH):
                    sp.dma_start(b_cols[:, layer, :],
                                 b_ada[layer, 0:2 * D].rearrange("(k p) -> p k", p=P)).then_inc(small_in, 16)
                    sp.dma_start(g_cols[:, layer, :],
                                 g_pre[layer, :].rearrange("(k p) -> p k", p=P)).then_inc(small_in, 16)
                    sp.dma_start(row_b[0:1, layer, :], b_ada[layer:layer + 1, 2 * D:3 * D]).then_inc(small_in, 16)
                    sp.dma_start(row_g[0:1, layer, :], g_post[layer:layer + 1, :]).then_inc(small_in, 16)
                sp.dma_start(lam_in[:, :, :], diff_lambda[0:1, :, :].broadcast_to([P, 4, HD])).then_inc(small_in, 16)
                sp.dma_start(m["lam"][:, 1:2], diff_subln.rearrange("a d -> d a")).then_inc(small_in, 16)
            for layer in range(DEPTH):
                for i in range(NP_):
                    if layer:
                        (sp.wait_ge(cols_done, 1) if i < 2 * D // PIECE else sp.wait_ge(row_done, 1))
                    sp.dma_start(m["ada_w"][:, :, i * PIECE:(i + 1) * PIECE],
                                 w_ada[layer, :, i * PIECE:(i + 1) * PIECE]
                                 .rearrange("(k p) f -> p k f", p=P)).then_inc(ada_in[i], 16)
            for layer in range(DEPTH):
                sp.wait_ge(row_used, layer + 1)
                sp.dma_start(gate_rows[layer:layer + 1, :], row[0:1, layer, :]).then_inc(row_stored, 16)
            sp.wait_ge(row_stored, 16 * DEPTH)

        @block.gpsimd
        def _(pool):
            nc.gpsimd.memset(m["ident"][:, :], 0.0).then_inc(zeroed, 1)
            nc.gpsimd.memset(m["mask_b"][:, :], 0.0).then_inc(zeroed, 1)
            nc.gpsimd.memset(m["ones"][:, :], 1.0).then_inc(zeroed, 1)
            nc.gpsimd.memset(m["ident_b"][:, :], 0.0).then_inc(zeroed, 1)
            nc.gpsimd.memset(m["eps"][:, :], EPS).then_inc(zeroed, 1)
            pool.wait_ge(zeroed, 5)
            for t in (m["ident"], m["ident_b"]):
                nc.gpsimd.affine_select(out=t[:, :], in_=t[:, :], compare_op=ALU.not_equal, fill=1.0, base=0,
                                        pattern=[[-1, P]], channel_multiplier=1).then_inc(consts, 1)
            nc.gpsimd.affine_select(out=m["mask_b"][:, :], in_=m["mask_b"][:, :], compare_op=ALU.is_gt, fill=NEG,
                                    base=0, pattern=[[-1, P]], channel_multiplier=1).then_inc(consts, 1)

        @block.scalar
        def _(act):
            act.wait_ge(small_in, 16 * (3 + 4 * DEPTH))
            nc.scalar.activation(cond_sig[:, :], cond[:, :], ACT.Sigmoid).then_inc(cond_sig_done, 1)
            act.wait_ge(lam_sum, 2)
            nc.scalar.activation(lam_sums[:, 2:4], lam_sums[:, 0:2], ACT.Exp).then_inc(lam_exp, 1)

        @block.vector
        def _(dve):
            def link(instruction, n=[0]):
                n[0] += 1
                instruction.then_inc(chain, 1)
                dve.wait_ge(chain, n[0])

            dve.wait_ge(small_in, 16 * (3 + 4 * DEPTH))
            dve.wait_ge(cond_sig_done, 1)
            nc.vector.tensor_tensor(cond_act[:, :], cond[:, :], cond_sig[:, :], ALU.mult).then_inc(cond_done, 1)
            for j in range(2):
                nc.vector.tensor_tensor_reduce(out=lam_prod[:, j, :], in0=lam_in[:, 2 * j, :],
                                               in1=lam_in[:, 2 * j + 1, :], scale=1.0, scalar=0.0, op0=ALU.mult,
                                               op1=ALU.add, accum_out=lam_sums[:, j:j + 1]).then_inc(lam_sum, 1)
            dve.wait_ge(lam_exp, 1)
            link(nc.vector.tensor_tensor(m["lam"][:, 0:1], lam_sums[:, 3:4], lam_sums[:, 2:3], ALU.subtract))
            link(nc.vector.tensor_scalar(m["lam"][:, 2:3], m["lam"][:, 0:1], -lam_init, None, ALU.add))
            link(nc.vector.tensor_scalar(m["lam"][:, 3:4], m["lam"][:, 1:2], 1.0 - lam_init, None, ALU.mult))
            for layer in range(DEPTH):
                dve.wait_ge(cols_done, layer + 1)
                link(nc.vector.tensor_tensor(m["add_col"][layer][:, :], bank[0][:, 0:KT], b_cols[:, layer, 0:KT],
                                             ALU.add))
                link(nc.vector.tensor_tensor(scale1[:, layer, :], bank[0][:, KT:2 * KT], b_cols[:, layer, KT:2 * KT],
                                             ALU.add))
                nc.vector.scalar_tensor_tensor(out=m["mul_col"][layer][:, :], in0=scale1[:, layer, :], scalar=1.0,
                                               in1=g_cols[:, layer, :], op0=ALU.add,
                                               op1=ALU.mult).then_inc(cols_used, 1)
                dve.wait_ge(row_done, layer + 1)
                for h in range(2):
                    cols = slice(h * HALF, (h + 1) * HALF)
                    link(nc.vector.tensor_tensor(row[0:1, layer, cols], bank[1 + h][0:1, :], row_b[0:1, layer, cols],
                                                 ALU.add))
                last = nc.vector.tensor_tensor(row[0:1, layer, :], row[0:1, layer, :], row_g[0:1, layer, :], ALU.mult)
                last.then_inc(row_used, 1)

        @block.tensor
        def _(pe):
            pe.wait_ge(cond_done, 1)
            for layer in range(DEPTH):
                if layer:
                    pe.wait_ge(cols_used, layer)
                for f in range(2 * KT):
                    if f % (PIECE // P) == 0:
                        pe.wait_ge(ada_in[f * P // PIECE], 16 * (layer + 1))
                    for k in range(KT):
                        last = nc.tensor.matmul(bank[0][:, f:f + 1], m["ada_w"][:, k, f * P:(f + 1) * P],
                                                cond_act[:, k:k + 1], start=(k == 0), stop=(k == KT - 1))
                last.then_inc(cols_done, 1)
                if layer:
                    pe.wait_ge(row_used, layer)
                for i in range(2 * D // PIECE, NP_):
                    pe.wait_ge(ada_in[i], 16 * (layer + 1))
                for h in range(2):
                    for k in range(KT):
                        last = nc.tensor.matmul(bank[1 + h][0:1, :], cond_act[:, k:k + 1],
                                                m["ada_w"][:, k, 2 * D + h * HALF:2 * D + (h + 1) * HALF],
                                                start=(k == 0), stop=(k == KT - 1))
                last.then_inc(row_done, 1)


def normalise(nc, m, sb, layer, source):
    def sem(name):
        return nc.alloc_semaphore(f"n{layer}_{name}")

    xt = [sb(f"n{layer}_x{s}", [P, D], F32, 160 + 4 * s) for s in range(2)]
    xn = [sb(f"n{layer}_xn{s}", [P, D], F32, 168 + 4 * s) for s in range(2)]
    h32 = [sb(f"n{layer}_h32_{s}", [P, 4, P], F32, 180 + 2 * s) for s in range(4)]
    st = m["stat"]
    loaded = [sem(f"x_loaded{s}") for s in range(2)]
    squares, mean_done, root_done, rstd_done = sem("squares"), sem("mean_done"), sem("root_done"), sem("rstd_done")
    scaled, turned, modulated, hi_done, lo_done = sem("scaled"), sem("turned"), sem("modulated"), sem("hi_done"), sem("lo_done")
    T2 = 2
    ROUNDS = NT // T2

    with nc.Block() as block:

        @block.sync
        def _(sp):
            with sp.Fori(0, ROUNDS) as r:
                for s in range(T2):
                    sp.wait_ge(scaled, done(T2 * r + s - T2))
                    sp.dma_start(xt[s][:, :], source[bass.ds((T2 * r + s) * P, P), :]).then_inc(loaded[s], 16)

        @block.scalar
        def _(act):
            act.sem_inc(squares, CREDIT)
            act.sem_inc(hi_done, CREDIT)
            act.sem_inc(root_done, CREDIT)
            with act.Fori(0, ROUNDS) as r:
                for s in range(T2):
                    t = T2 * r + s
                    act.wait_ge(loaded[s], 16 * r + 16)
                    act.wait_ge(turned, done(2 * (t - T2) + 1))
                    nc.scalar.activation(xn[s][:, :], xt[s][:, :], ACT.Square,
                                         accum_out=st[:, 4 * s:4 * s + 1]).then_inc(squares, 1)
                    act.wait_ge(mean_done, done(t))
                    nc.scalar.activation(st[:, 4 * s + 2:4 * s + 3], st[:, 4 * s + 1:4 * s + 2],
                                         ACT.Sqrt).then_inc(root_done, 1)
                    for b in range(2):
                        act.wait_ge(modulated, done(2 * t + b))
                        nc.scalar.activation(m["h_hi"][:, 4 * b:4 * b + 4, bass.ds(t * P, P)],
                                             h32[2 * s + b][:, :, :], ACT.Copy).then_inc(hi_done, 1)

        @block.vector
        def _(dve):
            for q in (scaled, mean_done, rstd_done, modulated):
                dve.sem_inc(q, CREDIT)
            with dve.Fori(0, ROUNDS) as r:
                for s in range(T2):
                    t = T2 * r + s
                    dve.wait_ge(squares, done(t))
                    nc.vector.tensor_scalar(st[:, 4 * s + 1:4 * s + 2], st[:, 4 * s:4 * s + 1], 1.0 / D, EPS,
                                            ALU.mult, ALU.add).then_inc(mean_done, 1)
                    dve.wait_ge(root_done, done(t))
                    nc.vector.reciprocal(st[:, 4 * s + 3:4 * s + 4],
                                         st[:, 4 * s + 2:4 * s + 3]).then_inc(rstd_done, 1)
                    dve.wait_ge(rstd_done, done(t))
                    nc.vector.tensor_scalar(xn[s][:, :], xt[s][:, :], st[:, 4 * s + 3:4 * s + 4], None,
                                            ALU.mult).then_inc(scaled, 1)
                    for b in range(2):
                        dve.wait_ge(turned, done(2 * t + b))
                        dve.wait_ge(lo_done, done(2 * (t - T2) + b))
                        for k in range(4):
                            kk = 4 * b + k
                            last = nc.vector.tensor_scalar(
                                h32[2 * s + b][:, k, :], m["pm"][2 * s + b][:, k * P:(k + 1) * P],
                                m["mul_col"][layer][:, kk:kk + 1], m["add_col"][layer][:, kk:kk + 1],
                                ALU.mult, ALU.add)
                        last.then_inc(modulated, 1)

        @block.gpsimd
        def _(pool):
            pool.sem_inc(lo_done, CREDIT)
            with pool.Fori(0, ROUNDS) as r:
                for s in range(T2):
                    t = T2 * r + s
                    for b in range(2):
                        pool.wait_ge(hi_done, done(2 * t + b))
                        dst = m["h_lo"][:, 4 * b:4 * b + 4, bass.ds(t * P, P)]
                        hi = m["h_hi"][:, 4 * b:4 * b + 4, bass.ds(t * P, P)]
                        nc.gpsimd.tensor_tensor(dst, h32[2 * s + b][:, :, :], hi.bitcast(F32),
                                                ALU.subtract).then_inc(lo_done, 1)

        @block.tensor
        def _(pe):
            pe.sem_inc(turned, CREDIT)
            with pe.Fori(0, ROUNDS) as r:
                for s in range(T2):
                    t = T2 * r + s
                    pe.wait_ge(scaled, done(t))
                    for b in range(2):
                        pe.wait_ge(modulated, done(2 * (t - T2) + b))
                        for k in range(4):
                            last = nc.tensor.transpose(m["pm"][2 * s + b][:, k * P:(k + 1) * P],
                                                       xn[s][:, (4 * b + k) * P:(4 * b + k + 1) * P],
                                                       m["ident"][:, :])
                        last.then_inc(turned, 1)


class Projection:

    def __init__(self, nc, m, w_in, tag):
        self.nc, self.m, self.w_in = nc, m, w_in
        self.bank = m["pm"][6:8]
        self.loaded = [nc.alloc_semaphore(f"{tag}_w_loaded{s}") for s in range(2)]
        self.hi_done = nc.alloc_semaphore(f"{tag}_w_hi_done")
        self.lo_done = nc.alloc_semaphore(f"{tag}_w_lo_done")
        self.group_done = nc.alloc_semaphore(f"{tag}_group_done")
        self.u_done = nc.alloc_semaphore(f"{tag}_u_done")
        self.sz_done = nc.alloc_semaphore(f"{tag}_sz_done")

    def load(self, sp, pair, kind):
        s = kind % 2
        sp.wait_ge(self.group_done, done(8 * pair + 2 * (kind - 2) + 1))
        sp.dma_start(self.m["w_raw"][s][:, :, :],
                     self.w_in[:, bass.ds(kind * D + pair * P, P)].rearrange("(k p) f -> p k f", p=P)
                     ).then_inc(self.loaded[s], 16)

    def split_hi(self, act, pair, kind):
        s = kind % 2
        act.wait_ge(self.loaded[s], 32 * pair + 16 * (kind // 2) + 16)
        act.wait_ge(self.group_done, done(8 * pair + 2 * (kind - 2) + 1))
        self.nc.scalar.activation(self.m["w_hi"][s][:, :, :], self.m["w_raw"][s][:, :, :],
                                  ACT.Copy).then_inc(self.hi_done, 1)

    def split_lo(self, pool, pair, kind):
        s = kind % 2
        pool.wait_ge(self.hi_done, done(4 * pair + kind))
        self.nc.gpsimd.tensor_tensor(self.m["w_lo"][s][:, :, :], self.m["w_raw"][s][:, :, :],
                                     self.m["w_hi"][s][:, :, :].bitcast(F32), ALU.subtract).then_inc(self.lo_done, 1)

    def multiply(self, pe, pair, first, last):
        m, nc = self.m, self.nc
        for n in range(first, last):
            group, i = divmod(n, GROUP)
            kind, half = divmod(group, 2)
            k, part = divmod(i, MULS)
            s = kind % 2
            if i == 0:
                if half == 0:
                    pe.wait_ge(self.hi_done, done(4 * pair + kind))
                    pe.wait_ge(self.lo_done, done(4 * pair + kind))
                if kind == 0:
                    pe.wait_ge(self.sz_done, done(2 * (pair - 1) + half))
                else:
                    pe.wait_ge(self.u_done, done(6 * pair + 2 * (kind - 1) + half))
            w = (m["w_hi"], m["w_hi"], m["w_lo"])[part][s]
            h = (m["h_hi"], m["h_lo"], m["h_hi"])[part]
            mm = nc.tensor.matmul(self.bank[half][:, :], w[:, k, :], h[:, k, half * HALF:(half + 1) * HALF],
                                  start=(i == 0), stop=(i == GROUP - 1))
            if i == GROUP - 1:
                mm.then_inc(self.group_done, 1)

    def keep(self, dve, pair, kind, half):
        dve.wait_ge(self.group_done, done(8 * pair + 2 * kind + half))
        dst = (self.m["uq"], self.m["uk"], self.m["uv"])[kind]
        self.nc.vector.tensor_copy(dst[:, half * HALF:(half + 1) * HALF],
                                   self.bank[half][:, :]).then_inc(self.u_done, 1)


class Packing:

    def __init__(self, nc, m, tag):
        self.nc, self.m = nc, m
        self.hi_done = nc.alloc_semaphore(f"{tag}_pack_hi_done")
        self.lo_done = nc.alloc_semaphore(f"{tag}_pack_lo_done")

    def hi(self, act, pair, n):
        h = n % 2
        src = self.m["uq" if n < 2 else "uk"]
        dst = self.m["q" if n < 2 else "k_hi"][h]
        rows = slice(HD * h, HD * h + HD)
        self.nc.scalar.activation(dst[rows, :], src[rows, :], ACT.Copy).then_inc(self.hi_done, 1)

    def lo(self, dve, pair, n):
        h = n % 2
        own, other = slice(HD * h, HD * h + HD), slice(HD - HD * h, 2 * HD - HD * h)
        m, v = self.m, self.nc.vector
        dve.wait_ge(self.hi_done, done(4 * pair + n))
        if n < 2:
            v.tensor_tensor(m["q"][h][other, :], m["uq"][own, :], m["q"][h][own, :].bitcast(F32),
                            ALU.subtract).then_inc(self.lo_done, 1)
        else:
            v.tensor_tensor(m["k_lo"][h][own, :], m["uk"][own, :], m["k_hi"][h][own, :].bitcast(F32),
                            ALU.subtract).then_inc(self.lo_done, 1)
            v.tensor_copy(m["k_hi"][h][other, :], m["k_hi"][h][own, :].bitcast(F32)).then_inc(self.lo_done, 1)
            dve.wait_ge(self.lo_done, done(8 * pair + 2 + 3 * (n - 2)))
            v.tensor_copy(m["k_lo"][h][other, :], m["k_lo"][h][own, :].bitcast(F32)).then_inc(self.lo_done, 1)


def load_out_weights(sp, m, w_out, loaded):
    for k in range(KT):
        sp.dma_start(m["wo_raw"][:, k, :], w_out[k * P:(k + 1) * P, :]).then_inc(loaded[k], 16)


def stick_breaking(nc, m, w_in, w_out):
    TILES = 2 * NT
    CH = [len(widths(t % NT)) for t in range(TILES)]
    CAT = [sum(CH[:t]) for t in range(TILES)]
    NCH = sum(CH)
    NB = NCH + 2
    LAG = 2
    STEPS = TILES + LAG + 1
    GROUPS = 2 * NG
    L, T, O = m["pm"][0:3], m["pm"][3:5], m["pm"][5]
    assert NCH % 3 == 0 and NB % 2 == 0
    RA = 3

    def ring(t):
        return t % RA

    QKV = shares(6 * GROUP, [0] + [2 + t % NT for t in range(1, TILES)] + [0] * (STEPS - TILES))
    ZED = shares(2 * GROUP, [0] * TILES + [1] * (STEPS - TILES))

    SPLIT_AT = (0, 2, 7, 13)

    def slot(s):
        return [QKV[s], tuple(6 * GROUP + z for z in ZED[s])]

    def sem(name):
        return nc.alloc_semaphore("s_" + name)

    logits, gates, scanned, weighted = sem("logits"), sem("gates"), sem("scanned"), sem("weighted")
    turned, hi_done, lo_done = sem("turned"), sem("hi_done"), sem("lo_done")
    o_done, part_done, y_done, gated = sem("o_done"), sem("part_done"), sem("y_done"), sem("gated")
    zsig, one_set = sem("zsig"), sem("one_set")
    wo_in = [sem(f"wo_loaded{k}") for k in range(KT)]
    wo_hi_done = sem("wo_hi_done")
    proj = Projection(nc, m, w_in, "s")
    pack = Packing(nc, m, "s")

    def last_batch_before(p, t):
        if t >= RA:
            return NB * p + 2 + CAT[t - RA] + CH[t - RA] - 1
        prev = max(u for u in range(TILES) if ring(u) == ring(t))
        return NB * (p - 1) + 2 + CAT[prev] + CH[prev] - 1

    with nc.Block() as block:

        @block.sync
        def _(sp):
            for kind in range(4):
                proj.load(sp, 0, kind)
            with sp.Fori(0, PAIRS - 1) as p:
                for kind in range(4):
                    proj.load(sp, p + 1, kind)
            sp.wait_ge(proj.group_done, done(8 * PAIRS - 1))
            load_out_weights(sp, m, w_out, wo_in)

        @block.tensor
        def _(pe):
            for q in (proj.group_done, logits, turned, o_done):
                pe.sem_inc(q, CREDIT)

            def score(p, t):
                h, i = divmod(t, NT)
                qs = m["q"][h][:, i * P:(i + 1) * P]
                if t == 0:
                    pe.wait_ge(pack.lo_done, done(8 * p + 7))
                for n, (k0, w) in enumerate(widths(i)):
                    ch = CAT[t] + n
                    bank = L[ch % 3]
                    pe.wait_ge(gates, done(NCH * p + ch - 3))
                    diag = k0 + w == P * (i + 1)
                    nc.tensor.matmul(bank[:, 0:w], qs, m["k_hi"][h][:, k0:k0 + w], start=True, stop=False)
                    mm = nc.tensor.matmul(bank[:, 0:w], qs, m["k_lo"][h][:, k0:k0 + w], start=False, stop=not diag)
                    if diag:
                        mm = nc.tensor.matmul(bank[:, w - P:w], m["ident_b"][:, :], m["mask_b"][:, :],
                                              start=False, stop=True)
                    mm.then_inc(logits, 1)

            def turn(p, t):
                i = t % NT
                pe.wait_ge(weighted, done(TILES * p + t))
                a = m["a"][ring(t)]
                for n, (k0, w) in enumerate(widths(i)):
                    b = 2 + CAT[t] + n
                    pe.wait_ge(lo_done, done(NB * p + b - 2))
                    for j in range(w // P):
                        at = S - P * (i + 1) + k0 + j * P
                        mm = nc.tensor.transpose(T[b % 2][:, j * P:(j + 1) * P], a[:, at:at + P], m["ident"][:, :])
                    mm.then_inc(turned, 1)

            def values(p, g):
                h, gg = divmod(g, NG)
                pe.wait_ge(lo_done, done(NB * p + 2 + CAT[2 * g + 1] + CH[2 * g + 1] - 1))
                pe.wait_ge(y_done, done(GROUPS * p + g - 1))
                tiles = 2 * gg + 2
                for j in range(tiles):
                    c0 = P if j == tiles - 1 else 0
                    for w in (m["wt_hi"], m["wt_lo"]):
                        mm = nc.tensor.matmul(O[:, c0:GW], m["v"][h][:, j, :], w[:, j, c0:GW],
                                              start=(j == 0 and w is m["wt_hi"]),
                                              stop=(j == tiles - 1 and w is m["wt_lo"]))
                mm.then_inc(o_done, 1)

            def turn_values(p):
                for b in range(2):
                    pe.wait_ge(proj.u_done, done(6 * p + 4 + b))
                    pe.wait_ge(lo_done, done(NB * p + b - 2))
                    for j in range(4):
                        at = (4 * b + j) * P
                        mm = nc.tensor.transpose(T[b][:, j * P:(j + 1) * P], m["uv"][:, at:at + P], m["ident"][:, :])
                    mm.then_inc(turned, 1)

            def pair(p, project):
                for s in range(STEPS):
                    if s < TILES:
                        score(p, s)
                    if project:
                        for f, l in slot(s):
                            proj.multiply(pe, p + 1, f, f + (l - f) // 2)
                    if s >= 4 and s % 2 == 0:
                        values(p, s // 2 - 2)
                    if LAG <= s < TILES + LAG:
                        turn(p, s - LAG)
                    if project:
                        for f, l in slot(s):
                            proj.multiply(pe, p + 1, f + (l - f) // 2, l)
                if project:
                    turn_values(p + 1)

            proj.multiply(pe, 0, 0, 8 * GROUP)
            turn_values(0)
            with pe.Fori(0, PAIRS - 1) as p:
                pair(p, True)
            pair(PAIRS - 1, False)

        @block.scalar
        def _(act):
            for q in (proj.hi_done, pack.hi_done, gates, hi_done, part_done, zsig):
                act.sem_inc(q, CREDIT)

            def sigmoids(p, t):
                i = t % NT
                for n, (k0, w) in enumerate(widths(i)):
                    ch = CAT[t] + n
                    at = S - P * (i + 1) + k0
                    act.wait_ge(logits, done(NCH * p + ch))
                    if n == 0:
                        act.wait_ge(turned, done(last_batch_before(p, t)))
                        act.wait_ge(scanned, done(TILES * p + t - 2))
                    nc.scalar.activation(m["a"][ring(t)][:, at:at + w], L[ch % 3][:, 0:w], ACT.Sigmoid, scale=SCALE)
                    nc.scalar.activation(m["b"][t % 2][:, at:at + w], L[ch % 3][:, 0:w], ACT.Sigmoid,
                                         scale=-SCALE).then_inc(gates, 1)

            def weights_hi(p, t):
                i = t % NT
                for n, (k0, w) in enumerate(widths(i)):
                    b = 2 + CAT[t] + n
                    act.wait_ge(turned, done(NB * p + b))
                    if n == 0:
                        act.wait_ge(o_done, done(GROUPS * p + t // 2 - 1))
                    c0 = (t % 2) * P
                    dst = m["wt_hi"][:, k0 // P:(k0 + w) // P, c0:c0 + P]
                    nc.scalar.activation(dst, T[b % 2][:, 0:w].rearrange("p (j q) -> p j q", q=P),
                                         ACT.Copy).then_inc(hi_done, 1)

            def other_part(p, g):
                h = g // NG
                own, other = slice(HD * h, HD * h + HD), slice(HD - HD * h, 2 * HD - HD * h)
                act.wait_ge(o_done, done(GROUPS * p + g))
                act.wait_ge(y_done, done(GROUPS * p + g - 1))
                nc.scalar.activation(m["o_part"][own, :], O[other, 0:GW], ACT.Copy).then_inc(part_done, 1)

            def z_gate(p):
                for half in range(2):
                    act.wait_ge(proj.group_done, done(8 * p + 6 + half))
                    act.wait_ge(gated, done(p - 1))
                    nc.scalar.activation(m["sz"][:, half * HALF:(half + 1) * HALF], proj.bank[half][:, :],
                                         ACT.Sigmoid).then_inc(zsig, 1)

            def values_hi(p):
                for b in range(2):
                    act.wait_ge(turned, done(NB * p + b))
                    act.wait_ge(o_done, done(GROUPS * p - 1))
                    t3 = T[b][:, :].rearrange("p (j d) -> p j d", d=P)
                    nc.scalar.activation(m["v"][0][:, 4 * b:4 * b + 4, 0:HD], t3[:, :, 0:HD], ACT.Copy)
                    nc.scalar.activation(m["v"][1][:, 4 * b:4 * b + 4, HD:P], t3[:, :, HD:P],
                                         ACT.Copy).then_inc(hi_done, 1)

            def pack_hi(p):
                for n in range(4):
                    if n % 2 == 0:
                        act.wait_ge(proj.u_done, done(6 * p + n + 1))
                    act.wait_ge(logits, done(NCH * p - 1))
                    pack.hi(act, p, n)

            def pair(p, project):
                for s in range(STEPS):
                    if project and s in SPLIT_AT:
                        proj.split_hi(act, p + 1, SPLIT_AT.index(s))
                    if s < TILES:
                        sigmoids(p, s)
                    if s >= 4 and s % 2 == 0:
                        other_part(p, s // 2 - 2)
                    if LAG <= s < TILES + LAG:
                        weights_hi(p, s - LAG)
                    if s == TILES and project:
                        pack_hi(p + 1)
                if project:
                    values_hi(p + 1)
                    z_gate(p + 1)

            for kind in range(4):
                proj.split_hi(act, 0, kind)
            pack_hi(0)
            values_hi(0)
            z_gate(0)
            with act.Fori(0, PAIRS - 1) as p:
                pair(p, True)
            pair(PAIRS - 1, False)

        @block.vector
        def _(dve):
            for q in (proj.u_done, proj.sz_done, pack.lo_done, scanned, lo_done, y_done):
                dve.sem_inc(q, CREDIT)
            for r in range(2):
                nc.vector.memset(m["stick"][r][:, S:S + 1], 1.0).then_inc(one_set, 1)

            def scan(p, t):
                i = t % NT
                at = S - P * (i + 1)
                dve.wait_ge(gates, done(NCH * p + CAT[t] + CH[t] - 1))
                dve.wait_ge(weighted, done(TILES * p + t - 2))
                keep = m["b"][t % 2][:, at:S][:, ::-1]
                nc.vector.tensor_tensor_scan(m["stick"][t % 2][:, at:S][:, ::-1], keep, keep, 1.0, ALU.mult,
                                             ALU.bypass).then_inc(scanned, 1)

            def weights_lo(p, t):
                i = t % NT
                for n, (k0, w) in enumerate(widths(i)):
                    b = 2 + CAT[t] + n
                    dve.wait_ge(hi_done, done(NB * p + b))
                    c0 = (t % 2) * P
                    js = slice(k0 // P, (k0 + w) // P)
                    nc.vector.tensor_tensor(m["wt_lo"][:, js, c0:c0 + P],
                                            T[b % 2][:, 0:w].rearrange("p (j q) -> p j q", q=P),
                                            m["wt_hi"][:, js, c0:c0 + P].bitcast(F32),
                                            ALU.subtract).then_inc(lo_done, 1)

            def add_parts(p, g):
                h, gg = divmod(g, NG)
                own = slice(HD * h, HD * h + HD)
                dve.wait_ge(part_done, done(GROUPS * p + g))
                y = m["y"][own, :, :].rearrange("r k t -> r (k t)")
                nc.vector.tensor_tensor(y[:, bass.ds(p * S + gg * GW, GW)], O[own, 0:GW], m["o_part"][own, :],
                                        ALU.add).then_inc(y_done, 1)

            def z_gate(p):
                for half in range(2):
                    cols = slice(half * HALF, (half + 1) * HALF)
                    dve.wait_ge(zsig, done(2 * p + half))
                    nc.vector.tensor_tensor(m["sz"][:, cols], proj.bank[half][:, :], m["sz"][:, cols],
                                            ALU.mult).then_inc(proj.sz_done, 1)

            def values_lo(p):
                for b in range(2):
                    dve.wait_ge(hi_done, done(NB * p + b))
                    t3 = T[b][:, :].rearrange("p (j d) -> p j d", d=P)
                    js = slice(4 * b, 4 * b + 4)
                    nc.vector.tensor_tensor(m["v"][0][:, js, HD:P], t3[:, :, 0:HD],
                                            m["v"][0][:, js, 0:HD].bitcast(F32), ALU.subtract)
                    nc.vector.tensor_tensor(m["v"][1][:, js, 0:HD], t3[:, :, HD:P],
                                            m["v"][1][:, js, HD:P].bitcast(F32), ALU.subtract).then_inc(lo_done, 1)

            def keep_u(p, kind, half):
                if kind == 2:
                    dve.wait_ge(turned, done(NB * (p - 1) + half))
                proj.keep(dve, p, kind, half)

            ends = {}
            for s in range(STEPS):
                for g in range(6):
                    if QKV[s][0] < (g + 1) * GROUP <= QKV[s][1]:
                        ends.setdefault(s, []).append(divmod(g, 2))

            def pair(p, project):
                for s in range(STEPS):
                    if s >= 4 and s % 2 == 0:
                        add_parts(p, s // 2 - 2)
                    if LAG <= s < TILES + LAG:
                        weights_lo(p, s - LAG)
                    if s < TILES:
                        scan(p, s)
                    if project:
                        for kind, half in ends.get(s, []):
                            keep_u(p + 1, kind, half)
                        if s == TILES:
                            for n in range(4):
                                pack.lo(dve, p + 1, n)
                if project:
                    values_lo(p + 1)
                    z_gate(p + 1)

            for kind in range(3):
                for half in range(2):
                    proj.keep(dve, 0, kind, half)
            for n in range(4):
                pack.lo(dve, 0, n)
            values_lo(0)
            z_gate(0)
            with dve.Fori(0, PAIRS - 1) as p:
                pair(p, True)
            pair(PAIRS - 1, False)
            for k in range(KT):
                dve.wait_ge(wo_in[k], 16)
                nc.vector.tensor_copy(m["wo_hi"][:, k, :], m["wo_raw"][:, k, :]).then_inc(wo_hi_done, 1)

        @block.gpsimd
        def _(pool):
            for q in (proj.lo_done, weighted, gated):
                pool.sem_inc(q, CREDIT)
            pool.wait_ge(one_set, 2)

            def weigh(p, t):
                i = t % NT
                at = S - P * (i + 1)
                pool.wait_ge(scanned, done(TILES * p + t))
                a = m["a"][ring(t)]
                nc.gpsimd.tensor_tensor(a[:, at:S], a[:, at:S], m["stick"][t % 2][:, at + 1:S + 1],
                                        ALU.mult).then_inc(weighted, 1)

            def pair(p, project):
                for s in range(TILES):
                    if project and s in SPLIT_AT:
                        proj.split_lo(pool, p + 1, SPLIT_AT.index(s))
                    weigh(p, s)
                pool.wait_ge(y_done, done(GROUPS * p + GROUPS - 1))
                pool.wait_ge(proj.sz_done, done(2 * p + 1))
                y = m["y"][:, :, :].rearrange("r k t -> r (k t)")[:, bass.ds(p * S, S)]
                nc.gpsimd.tensor_tensor(y, y, m["sz"][:, :], ALU.mult).then_inc(gated, 1)

            for kind in range(4):
                proj.split_lo(pool, 0, kind)
            with pool.Fori(0, PAIRS - 1) as p:
                pair(p, True)
            pair(PAIRS - 1, False)
            for k in range(KT):
                pool.wait_ge(wo_hi_done, k + 1)
                nc.gpsimd.tensor_tensor(m["wo_lo"][:, k, :], m["wo_raw"][:, k, :],
                                        m["wo_hi"][:, k, :].bitcast(F32), ALU.subtract)

def differential(nc, m, w_in, w_out):
    MAPS = 2
    BCH = [len(widths(t)) for t in range(NT)]
    BAT = [sum(BCH[:t]) for t in range(NT)]
    CAT = [MAPS * b for b in BAT]
    NCH = MAPS * sum(BCH)
    NB = sum(BCH) + 2
    LAG = 2
    STEPS = NT + LAG + 1
    L, T, O = m["pm"][0:3], m["pm"][3:5], m["pm"][5]
    RA = 3
    assert NCH % 3 == 0 and NB % 2 == 0

    def ring(t):
        return t % RA

    QKV = shares(6 * GROUP, [0] + [2 + t for t in range(1, NT)] + [0] * (STEPS - NT))
    ZED = shares(2 * GROUP, [0] * NT + [1] * (STEPS - NT))
    SPLIT_AT = (0, 1, 5, 8)

    def slot(s):
        return [QKV[s], tuple(6 * GROUP + z for z in ZED[s])]

    def sem(name):
        return nc.alloc_semaphore("d_" + name)

    logits, biased, negmax, expd = sem("logits"), sem("biased"), sem("negmax"), sem("expd")
    inverse, inverse_lam, second_scaled, weighted = (sem("inverse"), sem("inverse_lam"), sem("second_scaled"),
                                                     sem("weighted"))
    turned, hi_done, lo_done = sem("turned"), sem("hi_done"), sem("lo_done")
    o_done, o_kept, o_squared, sum_done = sem("o_done"), sem("o_kept"), sem("o_squared"), sem("sum_done")
    log_done, rs_done, y_done, gated = sem("log_done"), sem("rs_done"), sem("y_done"), sem("gated")
    zexp, zplus, zrec = sem("zexp"), sem("zplus"), sem("zrec")
    dist_done, table = sem("dist_done"), sem("table")
    halved, seen = sem("halved"), sem("seen")
    wo_in = [sem(f"wo_loaded{k}") for k in range(KT)]
    wo_hi_done = sem("wo_hi_done")
    proj = Projection(nc, m, w_in, "d")
    pack = Packing(nc, m, "d")
    dist = m["dist"]
    st = m["stat"]

    def col(t, name, n=0):
        at = {"max": 0, "neg": 4, "sum": 6, "inv": 8, "lam": 10}[name]
        return 16 * (t % 2) + at + n

    def last_batch_before(p, t):
        if t >= RA:
            return NB * p + 2 + BAT[t - RA] + BCH[t - RA] - 1
        prev = max(u for u in range(NT) if ring(u) == ring(t))
        return NB * (p - 1) + 2 + BAT[prev] + BCH[prev] - 1

    with nc.Block() as block:

        @block.sync
        def _(sp):
            for kind in range(4):
                proj.load(sp, 0, kind)
            with sp.Fori(0, PAIRS - 1) as p:
                for kind in range(4):
                    proj.load(sp, p + 1, kind)
            sp.wait_ge(proj.group_done, done(8 * PAIRS - 1))
            load_out_weights(sp, m, w_out, wo_in)

        @block.tensor
        def _(pe):
            for q in (proj.group_done, logits, turned, o_done, sum_done):
                pe.sem_inc(q, CREDIT)

            def score(p, t):
                if t == 0:
                    pe.wait_ge(pack.lo_done, done(8 * p + 7))
                for n in range(MAPS):
                    qs = m["q"][n][:, t * P:(t + 1) * P]
                    for c, (k0, w) in enumerate(widths(t)):
                        ch = CAT[t] + n * BCH[t] + c
                        bank = L[ch % 3]
                        pe.wait_ge(biased, done(NCH * p + ch - 3))
                        nc.tensor.matmul(bank[:, 0:w], qs, m["k_hi"][n][:, k0:k0 + w], start=True, stop=False)
                        nc.tensor.matmul(bank[:, 0:w], qs, m["k_lo"][n][:, k0:k0 + w], start=False,
                                         stop=True).then_inc(logits, 1)

            def turn(p, t):
                pe.wait_ge(weighted, done(NT * p + t))
                a = m["a"][ring(t)]
                for n, (k0, w) in enumerate(widths(t)):
                    b = 2 + BAT[t] + n
                    pe.wait_ge(lo_done, done(NB * p + b - 2))
                    for j in range(w // P):
                        at = S - P * (t + 1) + k0 + j * P
                        mm = nc.tensor.transpose(T[b % 2][:, j * P:(j + 1) * P], a[:, at:at + P], m["ident"][:, :])
                    mm.then_inc(turned, 1)

            def values(p, g):
                pe.wait_ge(lo_done, done(NB * p + 2 + BAT[2 * g + 1] + BCH[2 * g + 1] - 1))
                pe.wait_ge(log_done, done(NG * p + g - 1))
                tiles = 2 * g + 2
                for j in range(tiles):
                    c0 = P if j == tiles - 1 else 0
                    for i, (v, w) in enumerate(((0, "wt_hi"), (0, "wt_lo"), (1, "wt_hi"))):
                        mm = nc.tensor.matmul(O[:, c0:GW], m["v"][v][:, j, :], m[w][:, j, c0:GW],
                                              start=(j == 0 and i == 0), stop=(j == tiles - 1 and i == MULS - 1))
                mm.then_inc(o_done, 1)

            def sum_squares(p, g):
                pe.wait_ge(o_squared, done(NG * p + g))
                pe.wait_ge(o_kept, done(NG * p + g))
                nc.tensor.matmul(O[:, GW:2 * GW], m["ones"][:, :], m["sub_sq"][g % 2][:, :], start=True,
                                 stop=True).then_inc(sum_done, 1)

            def turn_values(p):
                for b in range(2):
                    pe.wait_ge(proj.u_done, done(6 * p + 4 + b))
                    pe.wait_ge(lo_done, done(NB * p + b - 2))
                    for j in range(4):
                        at = (4 * b + j) * P
                        mm = nc.tensor.transpose(T[b][:, j * P:(j + 1) * P], m["uv"][:, at:at + P], m["ident"][:, :])
                    mm.then_inc(turned, 1)

            def pair(p, project):
                for s in range(STEPS):
                    if s < NT:
                        score(p, s)
                    if project:
                        for f, l in slot(s):
                            proj.multiply(pe, p + 1, f, f + (l - f) // 2)
                    if s >= 4 and s % 2 == 0:
                        values(p, s // 2 - 2)
                    if LAG <= s < NT + LAG:
                        turn(p, s - LAG)
                    if project:
                        for f, l in slot(s):
                            proj.multiply(pe, p + 1, f + (l - f) // 2, l)
                    if s >= 4 and s % 2 == 0:
                        sum_squares(p, s // 2 - 2)
                if project:
                    turn_values(p + 1)

            proj.multiply(pe, 0, 0, 8 * GROUP)
            turn_values(0)
            with pe.Fori(0, PAIRS - 1) as p:
                pair(p, True)
            pair(PAIRS - 1, False)

        @block.scalar
        def _(act):
            for q in (proj.hi_done, pack.hi_done, expd, hi_done, o_kept, o_squared, log_done, rs_done, zexp):
                act.sem_inc(q, CREDIT)
            act.preload_act_table_set("natural_log_exp_and_others")

            def exponentials(p, t):
                at = S - P * (t + 1)
                for n in range(MAPS):
                    e = (m["a"][ring(t)], m["b"][t % 2])[n]
                    neg, total = col(t, "neg", n), col(t, "sum", n)
                    act.wait_ge(negmax, done(MAPS * (NT * p + t) + n))
                    nc.scalar.activation(e[:, at:S], e[:, at:S], ACT.Exp, bias=st[:, neg:neg + 1], scale=SCALE,
                                         accum_out=st[:, total:total + 1]).then_inc(expd, 1)

            def weights_hi(p, t):
                for n, (k0, w) in enumerate(widths(t)):
                    b = 2 + BAT[t] + n
                    act.wait_ge(turned, done(NB * p + b))
                    if n == 0:
                        act.wait_ge(o_done, done(NG * p + t // 2 - 1))
                    c0 = (t % 2) * P
                    dst = m["wt_hi"][:, k0 // P:(k0 + w) // P, c0:c0 + P]
                    nc.scalar.activation(dst, T[b % 2][:, 0:w].rearrange("p (j q) -> p j q", q=P),
                                         ACT.Copy).then_inc(hi_done, 1)

            def keep_output(p, g):
                act.wait_ge(o_done, done(NG * p + g))
                act.wait_ge(sum_done, done(NG * p + g - 2))
                nc.scalar.activation(m["sub_sq"][g % 2][:, :], O[:, 0:GW], ACT.Square).then_inc(o_squared, 1)
                y = m["y"][:, :, :].rearrange("r k t -> r (k t)")
                nc.scalar.activation(y[:, bass.ds(p * S + g * GW, GW)], O[:, 0:GW], ACT.Copy).then_inc(o_kept, 1)

            def inverse_root(p, g):
                act.wait_ge(sum_done, done(NG * p + g))
                nc.scalar.activation(m["sub_rs"][0][:, :], O[:, GW:2 * GW], ACT.Ln, scale=1.0 / P,
                                     bias=m["eps"][:, 0:1]).then_inc(log_done, 1)
                act.wait_ge(log_done, done(NG * p + g))
                act.wait_ge(y_done, done(NG * p + g - 1))
                nc.scalar.activation(m["sub_rs"][1][:, :], m["sub_rs"][0][:, :], ACT.Exp,
                                     scale=-0.5).then_inc(rs_done, 1)

            def z_gate(p):
                for half in range(2):
                    act.wait_ge(proj.group_done, done(8 * p + 6 + half))
                    act.wait_ge(gated, done(p - 1))
                    nc.scalar.activation(m["sz"][:, half * HALF:(half + 1) * HALF], proj.bank[half][:, :],
                                         ACT.Exp, scale=-1.0).then_inc(zexp, 1)

            def values_hi(p):
                for b in range(2):
                    act.wait_ge(turned, done(NB * p + b))
                    act.wait_ge(o_done, done(NG * p - 1))
                    t3 = T[b][:, :].rearrange("p (j d) -> p j d", d=P)
                    nc.scalar.activation(m["v"][0][:, 4 * b:4 * b + 4, :], t3, ACT.Copy).then_inc(hi_done, 1)

            def pack_hi(p):
                for n in range(4):
                    if n % 2 == 0:
                        act.wait_ge(proj.u_done, done(6 * p + n + 1))
                    act.wait_ge(logits, done(NCH * p - 1))
                    pack.hi(act, p, n)

            def pair(p, project):
                for s in range(STEPS):
                    if project and s in SPLIT_AT:
                        proj.split_hi(act, p + 1, SPLIT_AT.index(s))
                    if s >= 5 and s % 2 == 1:
                        inverse_root(p, (s - 5) // 2)
                    if s < NT:
                        exponentials(p, s)
                    if s >= 4 and s % 2 == 0:
                        keep_output(p, s // 2 - 2)
                    if LAG <= s < NT + LAG:
                        weights_hi(p, s - LAG)
                    if s == NT and project:
                        pack_hi(p + 1)
                inverse_root(p, NG - 1)
                if project:
                    values_hi(p + 1)
                    z_gate(p + 1)

            for kind in range(4):
                proj.split_hi(act, 0, kind)
            pack_hi(0)
            values_hi(0)
            z_gate(0)
            with act.Fori(0, PAIRS - 1) as p:
                pair(p, True)
            pair(PAIRS - 1, False)

        @block.vector
        def _(dve):
            for q in (proj.u_done, proj.sz_done, pack.lo_done, biased, negmax, inverse, inverse_lam, second_scaled,
                      weighted, lo_done, y_done, zplus, zrec, halved):
                dve.sem_inc(q, CREDIT)
            slope8 = 8.0 * 2.0 ** (-8.0 / PAIRS)
            dve.wait_ge(dist_done, 1)
            nc.vector.tensor_scalar(m["bias"][:, :], dist[:, :], -slope8, None, ALU.mult).then_inc(table, 1)
            nc.vector.tensor_scalar(m["a"][1][:, :], dist[:, :], slope8, None, ALU.mult).then_inc(table, 1)
            dve.wait_ge(table, 2)
            nc.vector.tensor_tensor(m["bias"][:, :], m["bias"][:, :], m["a"][1][:, :], ALU.min).then_inc(table, 1)
            dve.wait_ge(table, 3)
            nc.vector.memset(m["bias"][0:CHUNK, S - CHUNK:S], NEG).then_inc(table, 1)
            dve.wait_ge(table, 4)

            def add_bias(p, t):
                if t == 0:
                    dve.wait_ge(halved, done(p - 1))
                for n in range(MAPS):
                    x = (m["a"][ring(t)], m["b"][t % 2])[n]
                    if n == 0:
                        dve.wait_ge(turned, done(last_batch_before(p, t)))
                    for c, (k0, w) in enumerate(widths(t)):
                        ch = CAT[t] + n * BCH[t] + c
                        at = S - P * (t + 1) + k0
                        mx = col(t, "max", 2 * n + c)
                        dve.wait_ge(logits, done(NCH * p + ch))
                        dve.sem_inc(seen, 1)
                        nc.vector.tensor_tensor_reduce(
                            out=x[:, at:at + w], in0=L[ch % 3][:, 0:w], in1=m["bias"][:, at:at + w], scale=1.0,
                            scalar=-3e38, op0=ALU.add, op1=ALU.max, accum_out=st[:, mx:mx + 1]).then_inc(biased, 1)
                    dve.wait_ge(biased, done(NCH * p + ch))
                    mx, neg = col(t, "max", 2 * n), col(t, "neg", n)
                    if BCH[t] == 2:
                        ins = nc.vector.tensor_scalar(st[:, neg:neg + 1], st[:, mx:mx + 1], st[:, mx + 1:mx + 2],
                                                      -SCALE, ALU.max, ALU.mult)
                    else:
                        ins = nc.vector.tensor_scalar(st[:, neg:neg + 1], st[:, mx:mx + 1], -SCALE, None, ALU.mult)
                    ins.then_inc(negmax, 1)
                if t == NT - 1:
                    nc.vector.tensor_scalar(m["bias"][:, :], m["bias"][:, :], 0.5, None, ALU.mult).then_inc(halved, 1)

            def combine(p, t):
                at = S - P * (t + 1)
                a, b = m["a"][ring(t)], m["b"][t % 2]
                total, inv, lam = col(t, "sum"), col(t, "inv"), col(t, "lam")
                dve.wait_ge(expd, done(MAPS * (NT * p + t) + 1))
                nc.vector.reciprocal(st[:, inv:inv + 2], st[:, total:total + 2]).then_inc(inverse, 1)
                dve.wait_ge(inverse, done(NT * p + t))
                nc.vector.tensor_scalar(st[:, lam:lam + 1], st[:, inv + 1:inv + 2], m["lam"][:, 2:3], None,
                                        ALU.mult).then_inc(inverse_lam, 1)
                dve.wait_ge(inverse_lam, done(NT * p + t))
                nc.vector.tensor_scalar(b[:, at:S], b[:, at:S], st[:, lam:lam + 1], None,
                                        ALU.mult).then_inc(second_scaled, 1)
                dve.wait_ge(second_scaled, done(NT * p + t))
                nc.vector.scalar_tensor_tensor(out=a[:, at:S], in0=a[:, at:S], scalar=st[:, inv:inv + 1],
                                               in1=b[:, at:S], op0=ALU.mult, op1=ALU.add).then_inc(weighted, 1)

            def weights_lo(p, t):
                for n, (k0, w) in enumerate(widths(t)):
                    b = 2 + BAT[t] + n
                    dve.wait_ge(hi_done, done(NB * p + b))
                    c0 = (t % 2) * P
                    js = slice(k0 // P, (k0 + w) // P)
                    nc.vector.tensor_tensor(m["wt_lo"][:, js, c0:c0 + P],
                                            T[b % 2][:, 0:w].rearrange("p (j q) -> p j q", q=P),
                                            m["wt_hi"][:, js, c0:c0 + P].bitcast(F32),
                                            ALU.subtract).then_inc(lo_done, 1)

            def norm_output(p, g):
                dve.wait_ge(rs_done, done(NG * p + g))
                dve.wait_ge(o_kept, done(NG * p + g))
                y = m["y"][:, :, :].rearrange("r k t -> r (k t)")[:, bass.ds(p * S + g * GW, GW)]
                nc.vector.tensor_tensor(y, y, m["sub_rs"][1][:, :], ALU.mult).then_inc(y_done, 1)

            def z_gate(p):
                for half in range(2):
                    cols = slice(half * HALF, (half + 1) * HALF)
                    sz = m["sz"][:, cols]
                    dve.wait_ge(zexp, done(2 * p + half))
                    nc.vector.tensor_scalar(sz, sz, 1.0, None, ALU.add).then_inc(zplus, 1)
                    dve.wait_ge(zplus, done(2 * p + half))
                    nc.vector.reciprocal(sz, sz).then_inc(zrec, 1)
                    dve.wait_ge(zrec, done(2 * p + half))
                    nc.vector.scalar_tensor_tensor(out=sz, in0=proj.bank[half][:, :], scalar=m["lam"][:, 3:4],
                                                   in1=sz, op0=ALU.mult, op1=ALU.mult).then_inc(proj.sz_done, 1)

            def values_lo(p):
                for b in range(2):
                    dve.wait_ge(hi_done, done(NB * p + b))
                    t3 = T[b][:, :].rearrange("p (j d) -> p j d", d=P)
                    js = slice(4 * b, 4 * b + 4)
                    nc.vector.tensor_tensor(m["v"][1][:, js, :], t3, m["v"][0][:, js, :].bitcast(F32),
                                            ALU.subtract).then_inc(lo_done, 1)

            def keep_u(p, kind, half):
                if kind == 2:
                    dve.wait_ge(turned, done(NB * (p - 1) + half))
                proj.keep(dve, p, kind, half)

            ends = {}
            for s in range(STEPS):
                for g in range(6):
                    if QKV[s][0] < (g + 1) * GROUP <= QKV[s][1]:
                        ends.setdefault(s, []).append(divmod(g, 2))

            def pair(p, project):
                for s in range(STEPS):
                    if 1 <= s <= NT:
                        combine(p, s - 1)
                    if s >= 5 and s % 2 == 1:
                        norm_output(p, (s - 5) // 2)
                    if s < NT:
                        add_bias(p, s)
                    if LAG <= s < NT + LAG:
                        weights_lo(p, s - LAG)
                    if project:
                        for kind, half in ends.get(s, []):
                            keep_u(p + 1, kind, half)
                        if s == NT:
                            for n in range(4):
                                pack.lo(dve, p + 1, n)
                norm_output(p, NG - 1)
                if project:
                    values_lo(p + 1)
                    z_gate(p + 1)

            for kind in range(3):
                for half in range(2):
                    proj.keep(dve, 0, kind, half)
            for n in range(4):
                pack.lo(dve, 0, n)
            values_lo(0)
            z_gate(0)
            with dve.Fori(0, PAIRS - 1) as p:
                pair(p, True)
            pair(PAIRS - 1, False)
            for k in range(KT):
                dve.wait_ge(wo_in[k], 16)
                nc.vector.tensor_copy(m["wo_hi"][:, k, :], m["wo_raw"][:, k, :]).then_inc(wo_hi_done, 1)

        @block.gpsimd
        def _(pool):
            for q in (proj.lo_done, gated):
                pool.sem_inc(q, CREDIT)
            nc.gpsimd.iota(dist[:, :], pattern=[[-1, S]], base=S - P, channel_multiplier=1).then_inc(dist_done, 1)

            def pair(p, project):
                if project:
                    for kind in range(4):
                        proj.split_lo(pool, p + 1, kind)
                pool.wait_ge(y_done, done(NG * p + NG - 1))
                pool.wait_ge(proj.sz_done, done(2 * p + 1))
                y = m["y"][:, :, :].rearrange("r k t -> r (k t)")[:, bass.ds(p * S, S)]
                nc.gpsimd.tensor_tensor(y, y, m["sz"][:, :], ALU.mult).then_inc(gated, 1)

            for kind in range(4):
                proj.split_lo(pool, 0, kind)
            with pool.Fori(0, PAIRS - 1) as p:
                pair(p, True)
            pair(PAIRS - 1, False)
            for k in range(KT):
                pool.wait_ge(wo_hi_done, k + 1)
                nc.gpsimd.tensor_tensor(m["wo_lo"][:, k, :], m["wo_raw"][:, k, :],
                                        m["wo_hi"][:, k, :].bitcast(F32), ALU.subtract)


def project_out(nc, m, sb, layer, source, target, gate_rows):
    def sem(name):
        return nc.alloc_semaphore(f"o{layer}_{name}")

    T2 = 2
    ROUNDS = NT // T2
    y_hi = [sb(f"o{layer}_y_hi{s}", [P, KT, P], F32R, 112 + 4 * s) for s in range(2)]
    y_lo = [sb(f"o{layer}_y_lo{s}", [P, KT, P], F32R, 120 + 4 * s) for s in range(2)]
    xt = [sb(f"o{layer}_x{s}", [P, D], F32, 128 + 4 * s) for s in range(2)]
    res = [sb(f"o{layer}_res{s}", [P, D], F32, 136 + 4 * s) for s in range(2)]
    gate = sb(f"o{layer}_gate", [P, D], F32, 144)
    st = m["stat"]
    bank = m["pm"]
    gate_in = sem("gate_loaded")
    loaded = [sem(f"x_loaded{s}") for s in range(2)]
    stored = [sem(f"stored{s}") for s in range(2)]
    hi_done, lo_done, product = sem("hi_done"), sem("lo_done"), sem("product")
    squares, summed, mean_done, root_done, rstd_done = (sem("squares"), sem("summed"), sem("mean_done"),
                                                        sem("root_done"), sem("rstd_done"))
    scaled, added = sem("scaled"), sem("added")

    with nc.Block() as block:

        @block.sync
        def _(sp):
            sp.dma_start(gate[:, :], gate_rows[layer:layer + 1, :].broadcast_to([P, D])).then_inc(gate_in, 16)
            for s in range(T2):
                sp.dma_start(xt[s][:, :], source[s * P:(s + 1) * P, :]).then_inc(loaded[s], 16)
            with sp.Fori(0, ROUNDS - 1) as r:
                for s in range(T2):
                    t = T2 * r + s
                    sp.wait_ge(added, done(t))
                    sp.dma_start(target[bass.ds(t * P, P), :], res[s][:, :]).then_inc(stored[s], 16)
                    sp.dma_start(xt[s][:, :], source[bass.ds((t + T2) * P, P), :]).then_inc(loaded[s], 16)
            for s in range(T2):
                sp.wait_ge(added, done(NT - T2 + s))
                sp.dma_start(target[(NT - T2 + s) * P:(NT - T2 + s + 1) * P, :], res[s][:, :]).then_inc(stored[s], 16)
            for s in range(T2):
                sp.wait_ge(stored[s], 16 + 16 * ROUNDS)

        @block.scalar
        def _(act):
            for q in (hi_done, squares, root_done):
                act.sem_inc(q, CREDIT)
            for s in range(T2):
                act.sem_inc(stored[s], 16)

            def split(t, s):
                act.wait_ge(product, done(2 * (t - T2) + 1))
                nc.scalar.activation(y_hi[s][:, :, :], m["y"][:, :, bass.ds(t * P, P)], ACT.Copy).then_inc(hi_done, 1)

            def finish(t, s, r):
                for h in range(2):
                    act.wait_ge(product, done(2 * t + h))
                    if h == 0:
                        act.wait_ge(stored[s], 16 + 16 * r)
                    nc.scalar.activation(res[s][:, h * HALF:(h + 1) * HALF], bank[2 * s + h][:, :], ACT.Square,
                                         accum_out=st[:, 8 * s + h:8 * s + h + 1]).then_inc(squares, 1)
                act.wait_ge(mean_done, done(t))
                nc.scalar.activation(st[:, 8 * s + 4:8 * s + 5], st[:, 8 * s + 3:8 * s + 4],
                                     ACT.Sqrt).then_inc(root_done, 1)

            split(0, 0)
            with act.Fori(0, ROUNDS - 1) as r:
                split(T2 * r + 1, 1)
                for s in range(T2):
                    finish(T2 * r + s, s, r)
                    if s == 0:
                        split(T2 * r + 2, 0)
            split(NT - 1, 1)
            finish(NT - 2, 0, ROUNDS - 1)
            finish(NT - 1, 1, ROUNDS - 1)

        @block.vector
        def _(dve):
            for q in (lo_done, summed, mean_done, rstd_done, scaled):
                dve.sem_inc(q, CREDIT)
            dve.wait_ge(gate_in, 16)

            def split(t, s):
                dve.wait_ge(hi_done, done(t))
                nc.vector.tensor_tensor(y_lo[s][:, :, :], m["y"][:, :, bass.ds(t * P, P)],
                                        y_hi[s][:, :, :].bitcast(F32), ALU.subtract).then_inc(lo_done, 1)

            def finish(t, s, r):
                dve.wait_ge(squares, done(2 * t + 1))
                o = 8 * s
                nc.vector.tensor_tensor(st[:, o + 2:o + 3], st[:, o:o + 1], st[:, o + 1:o + 2],
                                        ALU.add).then_inc(summed, 1)
                dve.wait_ge(summed, done(t))
                nc.vector.tensor_scalar(st[:, o + 3:o + 4], st[:, o + 2:o + 3], 1.0 / D, EPS, ALU.mult,
                                        ALU.add).then_inc(mean_done, 1)
                dve.wait_ge(root_done, done(t))
                nc.vector.reciprocal(st[:, o + 5:o + 6], st[:, o + 4:o + 5]).then_inc(rstd_done, 1)
                dve.wait_ge(rstd_done, done(t))
                for h in range(2):
                    cols = slice(h * HALF, (h + 1) * HALF)
                    nc.vector.scalar_tensor_tensor(out=res[s][:, cols], in0=bank[2 * s + h][:, :],
                                                   scalar=st[:, o + 5:o + 6], in1=gate[:, cols], op0=ALU.mult,
                                                   op1=ALU.mult).then_inc(scaled, 1)

            split(0, 0)
            with dve.Fori(0, ROUNDS - 1) as r:
                split(T2 * r + 1, 1)
                for s in range(T2):
                    finish(T2 * r + s, s, r)
                    if s == 0:
                        split(T2 * r + 2, 0)
            split(NT - 1, 1)
            finish(NT - 2, 0, ROUNDS - 1)
            finish(NT - 1, 1, ROUNDS - 1)

        @block.gpsimd
        def _(pool):
            pool.sem_inc(added, CREDIT)
            with pool.Fori(0, ROUNDS) as r:
                for s in range(T2):
                    t = T2 * r + s
                    pool.wait_ge(scaled, done(2 * t + 1))
                    pool.wait_ge(loaded[s], 16 * r + 16)
                    nc.gpsimd.tensor_tensor(res[s][:, :], res[s][:, :], xt[s][:, :], ALU.add).then_inc(added, 1)

        @block.tensor
        def _(pe):
            pe.sem_inc(product, CREDIT)
            with pe.Fori(0, ROUNDS) as r:
                for s in range(T2):
                    t = T2 * r + s
                    pe.wait_ge(lo_done, done(t))
                    for h in range(2):
                        pe.wait_ge(scaled, done(2 * (t - T2) + h))
                        for k in range(KT):
                            for i, (y, w) in enumerate(((y_hi, m["wo_hi"]), (y_hi, m["wo_lo"]), (y_lo, m["wo_hi"]))):
                                mm = nc.tensor.matmul(bank[2 * s + h][:, :], y[s][:, k, :],
                                                      w[:, k, h * HALF:(h + 1) * HALF],
                                                      start=(k == 0 and i == 0), stop=(k == KT - 1 and i == MULS - 1))
                        mm.then_inc(product, 1)

_INS = ["x", "c", "w_ada", "b_ada", "g_pre", "g_post", "w_in", "w_out", "diff_lambda", "diff_subln"]


def kernel(**inputs):
    import numpy as np
    import concourse.bacc as bacc
    from concourse.bass_utils import run_bass_kernel_spmd

    nc = bacc.Bacc("TRN2", target_bir_lowering=False, num_devices=1)
    arrays, args = {}, {}
    for name in _INS:
        a = np.ascontiguousarray(inputs[name])
        if name == "x":
            a = a.reshape(S, D)
        arrays[f"in_{name}_dram"] = a
        args[name] = nc.dram_tensor(f"in_{name}_dram", a.shape, mybir.dt.from_np(a.dtype), kind="ExternalInput").ap()
    args["out"] = nc.dram_tensor("out_dram", [S, D], F32, kind="ExternalOutput").ap()
    trunk(nc, **args)
    r = run_bass_kernel_spmd(nc, [arrays], core_ids=[0])
    return r.results[0]["out_dram"].reshape(1, S, D)
```

```python
import math

import concourse.bass as bass
from concourse import mybir

F32 = mybir.dt.float32
F32R = mybir.dt.float32r
BF16 = mybir.dt.bfloat16
I32 = mybir.dt.int32
ALU = mybir.AluOpType
ACT = mybir.ActivationFunctionType
AX = mybir.AxisListType

P = 128
D = 1024
S = 1024
KT = D // P
NT = S // P
HALF = 512
PAIRS = D // P
HD = 64
GW = 2 * P
NG = NT // 2
SCALE = HD ** -0.5
CHUNK = 64
EPS = 1e-6
NEG = -1e30
DEPTH = 2
CREDIT = 32
MULS = 3
GROUP = MULS * KT
KB = 1024


def done(n):
    return CREDIT + 1 + n


def widths(i):
    w = P * (i + 1)
    return [(c, min(HALF, w - c)) for c in range(0, w, HALF)]


def shares(total, weights):
    whole, acc, cut = sum(weights), 0, [0]
    for w in weights:
        acc += w
        cut.append(round(total * acc / whole))
    return list(zip(cut[:-1], cut[1:]))


def schedule(z, qk, v, lag):
    steps = range(len(z))

    def end(parts, group):
        return next(s for s in steps if parts[s][1] >= (group + 1) * GROUP)

    z_end = [end(z, half) for half in range(2)]
    u_end = [end(qk, g) for g in range(4)] + [end(v, half) for half in range(2)]
    split = [0, z_end[1] + lag, u_end[1] + lag, u_end[3] + lag]
    return ([[half for half in range(2) if z_end[half] == s] for s in steps],
            [[divmod(g, 2) for g in range(6) if u_end[g] == s] for s in steps],
            [[kind for kind in range(4) if split[kind] == s] for s in steps])


def trunk(nc, x, c, w_ada, b_ada, g_pre, g_post, w_in, w_out, diff_lambda, diff_subln, out):
    base = (nc.sbuf_base + 63) // 64 * 64
    placed = {}

    def sb(name, shape, dtype, kb):
        placed[name] = nc.alloc_sbuf_tensor_at(name, shape, dtype, offset=base + int(kb * KB))
        return placed[name]

    x1 = nc.dram_tensor("x_between", [S, D], F32, kind="Internal").ap()
    gate_rows = nc.dram_tensor("gate_rows", [DEPTH, D], F32, kind="Internal").ap()

    m = {}
    m["h_hi"] = sb("h_hi", [P, KT, S], F32R, 0)
    m["h_lo"] = sb("h_lo", [P, KT, S], F32R, 32)
    m["ada_w"] = sb("ada_w", [P, KT, 2 * D], F32, 0)
    m["wo_hi"] = sb("wo_hi", [P, KT, D], F32R, 0)
    m["wo_raw"] = sb("wo_raw", [P, KT, D], F32, 32)
    m["wo_lo"] = sb("wo_lo", [P, KT, D], F32R, 32)
    m["y"] = sb("y", [P, KT, S], F32, 64)
    m["w_hi"] = [sb(f"w_hi{s}", [P, KT, P], F32R, 96 + 8 * s) for s in range(2)]
    m["w_raw"] = [sb(f"w_raw{s}", [P, KT, P], F32, 100 + 8 * s) for s in range(2)]
    m["w_lo"] = [sb(f"w_lo{s}", [P, KT, P], F32R, 100 + 8 * s) for s in range(2)]
    m["uq"] = sb("uq", [P, S], F32, 112)
    m["uk"] = sb("uk", [P, S], F32, 116)
    m["uv"] = sb("uv", [P, S], F32, 120)
    m["ada_piece"] = sb("ada_piece", [P, KT, P], F32, 124)
    m["sub_o"] = [sb(f"sub_o{r}", [P, GW], F32, 124 + r) for r in range(2)]
    m["z_sig"] = sb("z_sig", [P, S], F32, 124)
    m["h32"] = [sb(f"h32_{r}", [P, S], F32, 160 + 4 * r) for r in range(2)]
    m["q"] = [sb(f"q{h}", [P, S], F32R, 128 + 4 * h) for h in range(2)]
    m["k_hi"] = [sb(f"k_hi{h}", [P, S], F32R, 136 + 4 * h) for h in range(2)]
    m["k_lo"] = [sb(f"k_lo{h}", [P, S], F32R, 144 + 4 * h) for h in range(2)]
    m["v"] = [sb(f"v{h}", [P, NT, P], F32R, 152 + 4 * h) for h in range(2)]
    m["a"] = [sb(f"a{r}", [P, S], F32, 160 + 4 * r) for r in range(3)]
    m["b"] = [sb(f"b{r}", [P, S], F32, 172 + 4 * r) for r in range(2)]
    m["stick"] = [sb(f"stick{r}", [P, S + 1], F32, 180 + 4.0625 * r) for r in range(2)]
    m["bias"] = sb("bias", [P, S], F32, 180)
    m["sub_sq"] = [sb(f"sub_sq{r}", [P, GW], F32, 184 + r) for r in range(2)]
    m["sub_rs"] = [sb(f"sub_rs{r}", [P, GW], F32, 186 + r) for r in range(2)]
    m["dist"] = sb("dist", [P, S], I32, 172)
    m["wt_hi"] = sb("wt_hi", [P, NT, GW], F32R, 188.125)
    m["wt_lo"] = sb("wt_lo", [P, NT, GW], F32R, 196.125)
    at = [204.125]

    def small(name, shape, dtype, nbytes):
        t = sb(name, shape, dtype, at[0])
        at[0] += (nbytes + 31) // 32 * 32 / KB
        return t

    m["o_part"] = small("o_part", [P, GW], F32, 4 * GW)
    m["ident"] = small("ident", [P, P], F32, 4 * P)
    m["ones"] = small("ones", [P, P], F32, 4 * P)
    m["ident_b"] = small("ident_b", [P, P], BF16, 2 * P)
    m["mask_b"] = small("mask_b", [P, P], BF16, 2 * P)
    m["mul_col"] = [small(f"mul_col{l}", [P, KT], F32, 4 * KT) for l in range(DEPTH)]
    m["add_col"] = [small(f"add_col{l}", [P, KT], F32, 4 * KT) for l in range(DEPTH)]
    m["ada_sum"] = small("ada_sum", [P, P], F32, 4 * P)
    m["lam"] = small("lam", [P, 8], F32, 32)
    m["cond"] = small("cond_act", [P, KT], F32, 4 * KT)
    m["ada_cols"] = small("ada_cols", [P, DEPTH, 3 * KT], F32, 12 * KT * DEPTH)
    m["g_cols"] = small("g_cols", [P, DEPTH, 2 * KT], F32, 8 * KT * DEPTH)
    m["gate_col"] = small("gate_col", [P, DEPTH * KT], F32, 4 * KT * DEPTH)
    m["eps"] = small("eps", [P, 1], F32, 4)
    m["stat"] = small("stat", [P, 32], F32, 128)
    m["pm"] = [nc.alloc_psum_tensor(f"bank{i}", [P, HALF], F32) for i in range(8)]
    assert base + at[0] * KB <= nc.sbuf_usable_end, (base + at[0] * KB, nc.sbuf_usable_end)

    proj = [Projection(nc, m, w_in[layer], "sd"[layer]) for layer in range(DEPTH)]
    prepare(nc, m, sb, x, c, w_ada, b_ada, g_pre, g_post, diff_lambda, diff_subln, proj[0])
    stick_breaking(nc, m, proj[0], w_out[0], w_ada, gate_rows)
    project_out(nc, m, sb, 0, x, x1, gate_rows, proj[1])
    differential(nc, m, proj[1], w_out[1])
    project_out(nc, m, sb, 1, x1, out, gate_rows, None)


def prepare(nc, m, sb, x, c, w_ada, b_ada, g_pre, g_post, diff_lambda, diff_subln, proj):
    def sem(name):
        return nc.alloc_semaphore("p_" + name)

    PIECE = 4 * P
    PIECES = 2 * D // PIECE
    R = 4
    ROUNDS = NT // R
    cond_in = sb("cond_in", [P, KT], F32, 176)
    cond_sig = sb("cond_sig", [P, KT], F32, 176.25)
    lam_in = sb("lam_in", [P, 4, HD], F32, 177)
    lam_prod = sb("lam_prod", [P, 2, HD], F32, 178)
    lam_sums = sb("lam_sums", [P, 4], F32, 179)
    scale1 = sb("scale1", [P, KT], F32, 179.25)
    xt = [sb(f"p_x{s}", [P, D], F32, 128 + 4 * s) for s in range(R)]
    xn = [sb(f"p_xn{s}", [P, D], F32, 144 + 4 * s) for s in range(R)]
    st = m["stat"]
    T = [m["pm"][1:3], m["pm"][3:5]]
    cols = m["pm"][0]

    small_in = sem("small_loaded")
    ada_row = sb("ada_row", [1, 2 * D], F32, 160)
    rows = m["pm"][5:7]
    ada_in = [sem(f"ada_loaded{i}") for i in range(PIECES)]
    row_done, row_kept = sem("row_done"), sem("row_kept")
    loaded = [sem(f"x_loaded{s}") for s in range(R)]
    cond_sig_done, cond_done, cols_done = sem("cond_sig_done"), sem("cond_done"), sem("cols_done")
    zeroed, consts, chain = sem("zeroed"), sem("consts"), sem("vector_chain")
    lam_exp, lam_sum = sem("lam_exp"), sem("lam_sum")
    squares, mean_done, root_done, rstd_done = sem("squares"), sem("mean_done"), sem("root_done"), sem("rstd_done")
    scaled, turned, left_kept, right_kept = sem("scaled"), sem("turned"), sem("left_kept"), sem("right_kept")
    lam_init = 0.8 - 0.6 * math.exp(-0.3 * 1)

    with nc.Block() as block:

        @block.sync
        def _(sp):
            for s in range(R):
                sp.dma_start(xt[s][:, :], x[s * P:(s + 1) * P, :]).then_inc(loaded[s], 16)
            for s in range(R):
                sp.wait_ge(scaled, done(s))
                sp.dma_start(xt[s][:, :], x[(R + s) * P:(R + s + 1) * P, :]).then_inc(loaded[s], 16)
            proj.first_loads(sp)
            for i in range(PIECES):
                sp.dma_start(m["ada_w"][:, :, i * PIECE:(i + 1) * PIECE],
                             w_ada[0, :, i * PIECE:(i + 1) * PIECE]
                             .rearrange("(k p) f -> p k f", p=P)).then_inc(ada_in[i], 16)

        @block.gpsimd
        def _(pool):
            nc.gpsimd.memset(m["ident"][:, :], 0.0).then_inc(zeroed, 1)
            nc.gpsimd.memset(m["mask_b"][:, :], 0.0).then_inc(zeroed, 1)
            nc.gpsimd.memset(m["ones"][:, :], 1.0).then_inc(zeroed, 1)
            nc.gpsimd.memset(m["ident_b"][:, :], 0.0).then_inc(zeroed, 1)
            nc.gpsimd.memset(m["eps"][:, :], EPS).then_inc(zeroed, 1)
            pool.wait_ge(zeroed, 5)
            for t in (m["ident"], m["ident_b"]):
                nc.gpsimd.affine_select(out=t[:, :], in_=t[:, :], compare_op=ALU.not_equal, fill=1.0, base=0,
                                        pattern=[[-1, P]], channel_multiplier=1).then_inc(consts, 1)
            nc.gpsimd.affine_select(out=m["mask_b"][:, :], in_=m["mask_b"][:, :], compare_op=ALU.is_gt, fill=NEG,
                                    base=0, pattern=[[-1, P]], channel_multiplier=1).then_inc(consts, 1)

        @block.scalar
        def _(act):
            with nc.allow_non_contiguous_dma(reason="small vectors, feature on the partition"):
                act.dma_start(cond_in[:, :], c.rearrange("b (k p) -> p (b k)", p=P)).then_inc(small_in, 16)
                for layer in range(DEPTH):
                    act.dma_start(m["ada_cols"][:, layer, :],
                                  b_ada[layer, :].rearrange("(k p) -> p k", p=P)).then_inc(small_in, 16)
                    act.dma_start(m["g_cols"][:, layer, 0:KT],
                                  g_pre[layer, :].rearrange("(k p) -> p k", p=P)).then_inc(small_in, 16)
                    act.dma_start(m["g_cols"][:, layer, KT:2 * KT],
                                  g_post[layer, :].rearrange("(k p) -> p k", p=P)).then_inc(small_in, 16)
                act.dma_start(lam_in[:, :, :], diff_lambda[0:1, :, :].broadcast_to([P, 4, HD])).then_inc(small_in, 16)
                act.dma_start(m["lam"][:, 1:2], diff_subln.rearrange("a d -> d a")).then_inc(small_in, 16)
            for q in (squares, root_done, left_kept, proj.hi_done):
                act.sem_inc(q, CREDIT)

            def statistics(r, s):
                act.wait_ge(loaded[s], 16 * r + 16)
                act.wait_ge(turned, done(R * r + s - R))
                nc.scalar.activation(xn[s][:, :], xt[s][:, :], ACT.Square,
                                     accum_out=st[:, 4 * s:4 * s + 1]).then_inc(squares, 1)
                act.wait_ge(mean_done, done(R * r + s))
                nc.scalar.activation(st[:, 4 * s + 2:4 * s + 3], st[:, 4 * s + 1:4 * s + 2],
                                     ACT.Sqrt).then_inc(root_done, 1)

            def keep_left(r, s):
                act.wait_ge(turned, done(R * r + s))
                t4 = T[s % 2][0][:, :].rearrange("p (k t) -> p k t", t=P)
                nc.scalar.activation(m["y"][:, 0:4, bass.ds((R * r + s) * P, P)], t4, ACT.Copy).then_inc(left_kept, 1)

            for r in range(ROUNDS):
                for s in range(R):
                    statistics(r, s)
                    if s:
                        keep_left(r, s - 1)
                keep_left(r, R - 1)
                if r == 0:
                    act.wait_ge(small_in, 16 * (3 + 3 * DEPTH))
                    act.wait_ge(lam_sum, 2)
                    nc.scalar.activation(lam_sums[:, 2:4], lam_sums[:, 0:2], ACT.Exp).then_inc(lam_exp, 1)
            nc.scalar.activation(cond_sig[:, :], cond_in[:, :], ACT.Sigmoid).then_inc(cond_sig_done, 1)
            proj.first_hi(act)

        @block.vector
        def _(dve):
            def link(instruction, n=[0]):
                n[0] += 1
                instruction.then_inc(chain, 1)
                dve.wait_ge(chain, n[0])

            for q in (scaled, mean_done, rstd_done, right_kept, proj.lo_done):
                dve.sem_inc(q, CREDIT)

            def normalise(r, s):
                t = R * r + s
                dve.wait_ge(squares, done(t))
                nc.vector.tensor_scalar(st[:, 4 * s + 1:4 * s + 2], st[:, 4 * s:4 * s + 1], 1.0 / D, EPS,
                                        ALU.mult, ALU.add).then_inc(mean_done, 1)
                dve.wait_ge(root_done, done(t))
                nc.vector.reciprocal(st[:, 4 * s + 3:4 * s + 4], st[:, 4 * s + 2:4 * s + 3]).then_inc(rstd_done, 1)
                dve.wait_ge(rstd_done, done(t))
                nc.vector.tensor_scalar(xn[s][:, :], xt[s][:, :], st[:, 4 * s + 3:4 * s + 4], None,
                                        ALU.mult).then_inc(scaled, 1)

            def keep_right(r, s):
                dve.wait_ge(turned, done(R * r + s))
                t4 = T[s % 2][1][:, :].rearrange("p (k t) -> p k t", t=P)
                nc.vector.tensor_copy(m["y"][:, 4:8, bass.ds((R * r + s) * P, P)], t4).then_inc(right_kept, 1)

            for r in range(ROUNDS):
                for s in range(R):
                    normalise(r, s)
                    if s:
                        keep_right(r, s - 1)
                keep_right(r, R - 1)
                if r == 0:
                    dve.wait_ge(small_in, 16 * (3 + 3 * DEPTH))
                    for j in range(2):
                        nc.vector.tensor_tensor_reduce(out=lam_prod[:, j, :], in0=lam_in[:, 2 * j, :],
                                                       in1=lam_in[:, 2 * j + 1, :], scale=1.0, scalar=0.0,
                                                       op0=ALU.mult, op1=ALU.add,
                                                       accum_out=lam_sums[:, j:j + 1]).then_inc(lam_sum, 1)
                    dve.wait_ge(lam_exp, 1)
                    link(nc.vector.tensor_tensor(m["lam"][:, 0:1], lam_sums[:, 3:4], lam_sums[:, 2:3], ALU.subtract))
                    link(nc.vector.tensor_scalar(m["lam"][:, 2:3], m["lam"][:, 0:1], -lam_init, None, ALU.add))
                    link(nc.vector.tensor_scalar(m["lam"][:, 3:4], m["lam"][:, 1:2], 1.0 - lam_init, None, ALU.mult))
            dve.wait_ge(cond_sig_done, 1)
            nc.vector.tensor_tensor(m["cond"][:, :], cond_in[:, :], cond_sig[:, :], ALU.mult).then_inc(cond_done, 1)
            proj.first_lo(dve)
            for i in range(PIECES):
                dve.wait_ge(row_done, i + 1)
                nc.vector.tensor_copy(ada_row[0:1, i * PIECE:(i + 1) * PIECE], rows[i % 2][0:1, :]).then_inc(row_kept, 1)
            dve.wait_ge(cols_done, 1)
            link(nc.vector.tensor_tensor(m["add_col"][0][:, :], cols[:, 0:KT], m["ada_cols"][:, 0, 0:KT], ALU.add))
            link(nc.vector.tensor_tensor(scale1[:, :], cols[:, KT:2 * KT], m["ada_cols"][:, 0, KT:2 * KT], ALU.add))
            nc.vector.scalar_tensor_tensor(out=m["mul_col"][0][:, :], in0=scale1[:, :], scalar=1.0,
                                           in1=m["g_cols"][:, 0, 0:KT], op0=ALU.add, op1=ALU.mult)

        @block.tensor
        def _(pe):
            pe.sem_inc(turned, CREDIT)
            pe.wait_ge(consts, 3)
            for r in range(ROUNDS):
                for s in range(R):
                    t = R * r + s
                    pe.wait_ge(scaled, done(t))
                    pe.wait_ge(left_kept, done(t - 2))
                    pe.wait_ge(right_kept, done(t - 2))
                    for k in range(KT):
                        mm = nc.tensor.transpose(T[s % 2][k // 4][:, k % 4 * P:(k % 4 + 1) * P],
                                                 xn[s][:, k * P:(k + 1) * P], m["ident"][:, :])
                    mm.then_inc(turned, 1)
            pe.wait_ge(cond_done, 1)

            def columns(i):
                pe.wait_ge(row_kept, i + 1)
                for f in range(i * PIECE // P, (i + 1) * PIECE // P):
                    mm = nc.tensor.matmul(cols[:, f:f + 1], ada_row[0:1, f * P:(f + 1) * P], m["ones"][0:1, 0:1],
                                          start=True, stop=True)
                return mm

            for i in range(PIECES):
                pe.wait_ge(ada_in[i], 16)
                if i >= 2:
                    pe.wait_ge(row_kept, i - 1)
                for k in range(KT):
                    mm = nc.tensor.matmul(rows[i % 2][0:1, :], m["cond"][:, k:k + 1],
                                          m["ada_w"][:, k, i * PIECE:(i + 1) * PIECE],
                                          start=(k == 0), stop=(k == KT - 1))
                mm.then_inc(row_done, 1)
                if i:
                    columns(i - 1)
            columns(PIECES - 1).then_inc(cols_done, 1)


class Modulation:

    def __init__(self, nc, m, layer, tag):
        self.nc, self.m, self.layer = nc, m, layer
        self.hi_done = nc.alloc_semaphore(f"{tag}_h_hi_done")
        self.full_done = nc.alloc_semaphore(f"{tag}_h_full_done")
        self.even_done = nc.alloc_semaphore(f"{tag}_h_lo_even_done")
        self.odd_done = nc.alloc_semaphore(f"{tag}_h_lo_odd_done")

    def columns(self, k):
        return self.m["mul_col"][self.layer][:, k:k + 1], self.m["add_col"][self.layer][:, k:k + 1]

    def scalar(self, act):
        for k in range(KT):
            mul, add = self.columns(k)
            self.nc.scalar.activation(self.m["h_hi"][:, k, :], self.m["y"][:, k, :], ACT.Identity, bias=add,
                                      scale=mul).then_inc(self.hi_done, 1)

    def vector(self, dve):
        for k in range(KT):
            mul, add = self.columns(k)
            h32 = self.m["h32"][k % 2][:, :]
            if k >= 3 and k % 2:
                dve.wait_ge(self.odd_done, k // 2)
            self.nc.vector.tensor_scalar(h32, self.m["y"][:, k, :], mul, add, ALU.mult,
                                         ALU.add).then_inc(self.full_done, 1)
            if k % 2 == 0:
                dve.wait_ge(self.full_done, k + 1)
                dve.wait_ge(self.hi_done, k + 1)
                self.nc.vector.tensor_tensor(self.m["h_lo"][:, k, :], h32, self.m["h_hi"][:, k, :].bitcast(F32),
                                             ALU.subtract).then_inc(self.even_done, 1)
                dve.wait_ge(self.even_done, k // 2 + 1)

    def gpsimd(self, pool):
        for k in range(1, KT, 2):
            pool.wait_ge(self.full_done, k + 1)
            pool.wait_ge(self.hi_done, k + 1)
            self.nc.gpsimd.tensor_tensor(self.m["h_lo"][:, k, :], self.m["h32"][1][:, :],
                                         self.m["h_hi"][:, k, :].bitcast(F32), ALU.subtract).then_inc(self.odd_done, 1)

    def ready(self, pe, k):
        pe.wait_ge(self.hi_done, k + 1)
        pe.wait_ge((self.even_done, self.odd_done)[k % 2], k // 2 + 1)


class Projection:

    def __init__(self, nc, m, w_in, tag):
        self.nc, self.m, self.w_in = nc, m, w_in
        self.bank = m["pm"][6:8]
        self.loaded = [nc.alloc_semaphore(f"{tag}_w_loaded{s}") for s in range(2)]
        self.hi_done = nc.alloc_semaphore(f"{tag}_w_hi_done")
        self.lo_done = nc.alloc_semaphore(f"{tag}_w_lo_done")
        self.group_done = nc.alloc_semaphore(f"{tag}_group_done")
        self.u_done = nc.alloc_semaphore(f"{tag}_u_done")
        self.sz_done = nc.alloc_semaphore(f"{tag}_sz_done")

    def first_loads(self, sp):
        for kind in range(2):
            self.nc.sync.dma_start(self.m["w_raw"][kind][:, :, :],
                                   self.w_in[:, kind * D:kind * D + P].rearrange("(k p) f -> p k f", p=P)
                                   ).then_inc(self.loaded[kind], 16)

    def first_hi(self, act):
        for kind in range(2):
            act.wait_ge(self.loaded[kind], 16)
            self.nc.scalar.activation(self.m["w_hi"][kind][:, :, :], self.m["w_raw"][kind][:, :, :],
                                      ACT.Copy).then_inc(self.hi_done, 1)

    def first_lo(self, dve):
        for kind in range(2):
            dve.wait_ge(self.hi_done, done(kind))
            self.nc.vector.tensor_tensor(self.m["w_lo"][kind][:, :, :], self.m["w_raw"][kind][:, :, :],
                                         self.m["w_hi"][kind][:, :, :].bitcast(F32),
                                         ALU.subtract).then_inc(self.lo_done, 1)

    def load(self, sp, pair, kind):
        s = kind % 2
        sp.wait_ge(self.group_done, done(8 * pair + 2 * (kind - 2) + 1))
        sp.dma_start(self.m["w_raw"][s][:, :, :],
                     self.w_in[:, bass.ds(kind * D + pair * P, P)].rearrange("(k p) f -> p k f", p=P)
                     ).then_inc(self.loaded[s], 16)

    def split_hi(self, act, pair, kind):
        s = kind % 2
        act.wait_ge(self.loaded[s], 32 * pair + 16 * (kind // 2) + 16)
        act.wait_ge(self.group_done, done(8 * pair + 2 * (kind - 2) + 1))
        self.nc.scalar.activation(self.m["w_hi"][s][:, :, :], self.m["w_raw"][s][:, :, :],
                                  ACT.Copy).then_inc(self.hi_done, 1)

    def split_lo(self, pool, pair, kind):
        s = kind % 2
        pool.wait_ge(self.hi_done, done(4 * pair + kind))
        self.nc.gpsimd.tensor_tensor(self.m["w_lo"][s][:, :, :], self.m["w_raw"][s][:, :, :],
                                     self.m["w_hi"][s][:, :, :].bitcast(F32), ALU.subtract).then_inc(self.lo_done, 1)

    def multiply(self, pe, pair, first, last, modulation=None):
        m, nc = self.m, self.nc
        for n in range(first, last):
            group, i = divmod(n, GROUP)
            kind, half = divmod(group, 2)
            k, part = divmod(i, MULS)
            s = kind % 2
            if i == 0:
                if half == 0:
                    pe.wait_ge(self.hi_done, done(4 * pair + kind))
                    pe.wait_ge(self.lo_done, done(4 * pair + kind))
                if kind == 0:
                    pe.wait_ge(self.sz_done, done(2 * (pair - 1) + half))
                else:
                    pe.wait_ge(self.u_done, done(6 * pair + 2 * (kind - 1) + half))
            if modulation and group == 0 and part == 0:
                modulation.ready(pe, k)
            w = (m["w_hi"], m["w_hi"], m["w_lo"])[part][s]
            h = (m["h_hi"], m["h_lo"], m["h_hi"])[part]
            mm = nc.tensor.matmul(self.bank[half][:, :], w[:, k, :], h[:, k, half * HALF:(half + 1) * HALF],
                                  start=(i == 0), stop=(i == GROUP - 1))
            if i == GROUP - 1:
                mm.then_inc(self.group_done, 1)

    def keep(self, engine, pair, kind, half, pack):
        if kind == 0:
            engine.wait_ge(pack.lo_done, done(4 * pair - 1))
            engine.wait_ge(pack.hi_done, done(6 * pair - 1))
            engine.wait_ge(pack.key_lo_done, done(2 * pair - 1))
        engine.wait_ge(self.group_done, done(8 * pair + 2 * kind + half))
        dst = (self.m["uq"], self.m["uk"], self.m["uv"])[kind][:, half * HALF:(half + 1) * HALF]
        if engine is self.nc.vector:
            ins = self.nc.vector.tensor_copy(dst, self.bank[half][:, :])
        else:
            ins = self.nc.scalar.activation(dst, self.bank[half][:, :], ACT.Copy)
        ins.then_inc(self.u_done, 1)


class Packing:

    def __init__(self, nc, m, tag):
        self.nc, self.m = nc, m
        self.hi_done = nc.alloc_semaphore(f"{tag}_pack_hi_done")
        self.lo_done = nc.alloc_semaphore(f"{tag}_pack_lo_done")
        self.key_lo_done = nc.alloc_semaphore(f"{tag}_key_lo_done")

    def rows(self, h):
        return slice(HD * h, HD * h + HD), slice(HD - HD * h, 2 * HD - HD * h)

    def hi(self, act, n):
        own, other = self.rows(n % 2)
        src = self.m["uq" if n < 2 else "uk"]
        dst = self.m["q" if n < 2 else "k_hi"][n % 2]
        self.nc.scalar.activation(dst[other if n >= 4 else own, :], src[own, :], ACT.Copy).then_inc(self.hi_done, 1)

    def key_lo(self, dve, pair, h):
        own, _ = self.rows(h)
        dve.wait_ge(self.hi_done, done(6 * pair + 2 + h))
        self.nc.vector.tensor_tensor(self.m["k_lo"][h][own, :], self.m["uk"][own, :],
                                     self.m["k_hi"][h][own, :].bitcast(F32),
                                     ALU.subtract).then_inc(self.key_lo_done, 1)

    def lo(self, dve, pair, n):
        h = n % 2
        own, other = self.rows(h)
        m, v = self.m, self.nc.vector
        if n < 2:
            dve.wait_ge(self.hi_done, done(6 * pair + n))
            v.tensor_tensor(m["q"][h][other, :], m["uq"][own, :], m["q"][h][own, :].bitcast(F32),
                            ALU.subtract).then_inc(self.lo_done, 1)
        else:
            self.key_lo(dve, pair, h)
            dve.wait_ge(self.key_lo_done, done(2 * pair + h))
            v.tensor_copy(m["k_lo"][h][other, :], m["k_lo"][h][own, :].bitcast(F32)).then_inc(self.lo_done, 1)

    def ready(self, pe, pair):
        pe.wait_ge(self.hi_done, done(6 * pair + 5))
        pe.wait_ge(self.lo_done, done(4 * pair + 3))


def load_out_weights(sp, m, w_out, loaded):
    for k in range(0, KT, 2):
        sp.dma_start(m["wo_raw"][:, k:k + 2, :],
                     w_out[k * P:(k + 2) * P, :].rearrange("(k p) f -> p k f", p=P)).then_inc(loaded[k // 2], 16)


def stick_breaking(nc, m, proj, w_out, w_ada, gate_rows):
    TILES = 2 * NT
    CH = [len(widths(t % NT)) for t in range(TILES)]
    CAT = [sum(CH[:t]) for t in range(TILES)]
    NCH = sum(CH)
    NB = NCH + 2
    LAG = 2
    STEPS = TILES + LAG + 1
    GROUPS = 2 * NG
    L, T, O = m["pm"][0:3], m["pm"][3:5], m["pm"][5]
    assert NCH % 3 == 0 and NB % 2 == 0
    RA = 3

    def ring(t):
        return t % RA

    EARLY = 3
    Z = shares(2 * GROUP, [1] * EARLY + [0] * (STEPS - EARLY))
    QK = shares(4 * GROUP, [0] * EARLY + [2 + t % NT for t in range(EARLY, TILES)] + [0] * (STEPS - TILES))
    V = shares(2 * GROUP, [0] * TILES + [1] * (STEPS - TILES))
    Z_AT, U_AT, SPLIT_AT = schedule(Z, QK, V, 2)
    OUT = shares(KT, [0] * (EARLY + 2) + [1] * (STEPS - EARLY - 2))

    def sem(name):
        return nc.alloc_semaphore("s_" + name)

    logits, gates, scanned, weighted = sem("logits"), sem("gates"), sem("scanned"), sem("weighted")
    turned, hi_done, lo_done = sem("turned"), sem("hi_done"), sem("lo_done")
    o_done, part_done, y_done = sem("o_done"), sem("part_done"), sem("y_done")
    zsig, one_set, summed = sem("zsig"), sem("one_set"), sem("summed")
    ada_in, ada_done, ada_kept = sem("ada_loaded"), sem("ada_done"), sem("ada_kept")
    ada_scaled, ada_summed = sem("ada_scaled"), sem("ada_summed")
    chain, gate_turned, gate_kept, gate_stored = sem("chain"), sem("gate_turned"), sem("gate_kept"), sem("gate_stored")
    gate_rows_sb = m["o_part"]
    ADA = 4
    wo_in = [sem(f"wo_loaded{k}") for k in range(KT // 2)]
    wo_hi_done = sem("wo_hi_done")
    pack = Packing(nc, m, "s")
    modulation = Modulation(nc, m, 0, "s")

    def last_batch_before(p, t):
        if t >= RA:
            return NB * p + 2 + CAT[t - RA] + CH[t - RA] - 1
        prev = max(u for u in range(TILES) if ring(u) == ring(t))
        return NB * (p - 1) + 2 + CAT[prev] + CH[prev] - 1

    with nc.Block() as block:

        @block.sync
        def _(sp):
            for kind in range(2, 4):
                proj.load(sp, 0, kind)
            def ada(p, i):
                layer, at = (1, (3 * p + i) * P) if i < 3 else (0, 2 * D + p * P)
                sp.wait_ge(ada_summed, done(ADA * p + i - 1))
                sp.dma_start(m["ada_piece"][:, :, :], w_ada[layer, :, bass.ds(at, P)]
                             .rearrange("(k p) f -> p k f", p=P)).then_inc(ada_in, 16)

            with sp.Fori(0, PAIRS - 1) as p:
                proj.load(sp, p + 1, 0)
                ada(p, 0)
                proj.load(sp, p + 1, 1)
                ada(p, 1)
                ada(p, 2)
                proj.load(sp, p + 1, 2)
                ada(p, 3)
                proj.load(sp, p + 1, 3)
            ada(PAIRS - 1, 0)
            sp.wait_ge(proj.group_done, done(8 * PAIRS - 1))
            load_out_weights(sp, m, w_out, wo_in)
            for i in range(1, ADA):
                ada(PAIRS - 1, i)
            sp.wait_ge(gate_kept, 1)
            sp.dma_start(gate_rows.rearrange("l (k f) -> (l k) f", f=P),
                         gate_rows_sb[0:DEPTH * KT, 0:P]).then_inc(gate_stored, 16)
            sp.wait_ge(gate_stored, 16)

        @block.tensor
        def _(pe):
            for q in (proj.group_done, logits, turned, o_done, ada_done):
                pe.sem_inc(q, CREDIT)

            def score(p, t):
                h, i = divmod(t, NT)
                qs = m["q"][h][:, i * P:(i + 1) * P]
                if t == 0:
                    pack.ready(pe, p)
                for n, (k0, w) in enumerate(widths(i)):
                    ch = CAT[t] + n
                    bank = L[ch % 3]
                    pe.wait_ge(gates, done(NCH * p + ch - 3))
                    diag = k0 + w == P * (i + 1)
                    nc.tensor.matmul(bank[:, 0:w], qs, m["k_hi"][h][:, k0:k0 + w], start=True, stop=False)
                    mm = nc.tensor.matmul(bank[:, 0:w], qs, m["k_lo"][h][:, k0:k0 + w], start=False, stop=not diag)
                    if diag:
                        mm = nc.tensor.matmul(bank[:, w - P:w], m["ident_b"][:, :], m["mask_b"][:, :],
                                              start=False, stop=True)
                    mm.then_inc(logits, 1)

            def turn(p, t):
                i = t % NT
                pe.wait_ge(weighted, done(TILES * p + t))
                a = m["a"][ring(t)]
                for n, (k0, w) in enumerate(widths(i)):
                    b = 2 + CAT[t] + n
                    pe.wait_ge(lo_done, done(NB * p + b - 2))
                    for j in range(w // P):
                        at = S - P * (i + 1) + k0 + j * P
                        mm = nc.tensor.transpose(T[b % 2][:, j * P:(j + 1) * P], a[:, at:at + P], m["ident"][:, :])
                    mm.then_inc(turned, 1)

            def values(p, g):
                h, gg = divmod(g, NG)
                pe.wait_ge(lo_done, done(NB * p + 2 + CAT[2 * g + 1] + CH[2 * g + 1] - 1))
                pe.wait_ge(summed, done(GROUPS * p + g - 1))
                if g % 2:
                    i = g // 2
                    pe.wait_ge(ada_summed, done(ADA * p + i))
                    pe.wait_ge(ada_kept, done(ADA * p + i - 1))
                    nc.tensor.matmul(O[:, GW:GW + 1], m["ada_sum"][:, :], m["ones"][:, 0:1], start=True,
                                     stop=True).then_inc(ada_done, 1)
                tiles = 2 * gg + 2
                for j in range(tiles):
                    c0 = P if j == tiles - 1 else 0
                    for w in (m["wt_hi"], m["wt_lo"]):
                        mm = nc.tensor.matmul(O[:, c0:GW], m["v"][h][:, j, :], w[:, j, c0:GW],
                                              start=(j == 0 and w is m["wt_hi"]),
                                              stop=(j == tiles - 1 and w is m["wt_lo"]))
                mm.then_inc(o_done, 1)

            def turn_values(p):
                for b in range(2):
                    pe.wait_ge(proj.u_done, done(6 * p + 4 + b))
                    pe.wait_ge(lo_done, done(NB * p + b - 2))
                    for j in range(4):
                        at = (4 * b + j) * P
                        mm = nc.tensor.transpose(T[b][:, j * P:(j + 1) * P], m["uv"][:, at:at + P], m["ident"][:, :])
                    mm.then_inc(turned, 1)

            def project_share(p, s, project, half):
                for of, (f, l), at in ((p, Z[s], 6 * GROUP), (p + 1, QK[s], 0), (p + 1, V[s], 4 * GROUP)):
                    if project or at == 6 * GROUP:
                        mid = f + (l - f) // 2
                        proj.multiply(pe, of, at + (f, mid)[half], at + (mid, l)[half])

            def pair(p, project):
                for s in range(STEPS):
                    if s == 1:
                        turn_values(p)
                    if s < TILES:
                        score(p, s)
                    project_share(p, s, project, 0)
                    if s >= 4 and s % 2 == 0:
                        values(p, s // 2 - 2)
                    if LAG <= s < TILES + LAG:
                        turn(p, s - LAG)
                    project_share(p, s, project, 1)

            proj.multiply(pe, 0, 0, 6 * GROUP, modulation)
            with pe.Fori(0, PAIRS - 1) as p:
                pair(p, True)
            pair(PAIRS - 1, False)
            pe.wait_ge(chain, 4)
            nc.tensor.transpose(T[0][0:DEPTH * KT, 0:P], m["gate_col"][:, :], m["ident"][:, :]).then_inc(gate_turned, 1)

        @block.scalar
        def _(act):
            for q in (pack.hi_done, gates, hi_done, part_done, zsig):
                act.sem_inc(q, CREDIT)

            def sigmoids(p, t):
                i = t % NT
                for n, (k0, w) in enumerate(widths(i)):
                    ch = CAT[t] + n
                    at = S - P * (i + 1) + k0
                    act.wait_ge(logits, done(NCH * p + ch))
                    if n == 0:
                        act.wait_ge(turned, done(last_batch_before(p, t)))
                        act.wait_ge(scanned, done(TILES * p + t - 2))
                    nc.scalar.activation(m["a"][ring(t)][:, at:at + w], L[ch % 3][:, 0:w], ACT.Sigmoid, scale=SCALE)
                    nc.scalar.activation(m["b"][t % 2][:, at:at + w], L[ch % 3][:, 0:w], ACT.Sigmoid,
                                         scale=-SCALE).then_inc(gates, 1)

            def weights_hi(p, t):
                i = t % NT
                for n, (k0, w) in enumerate(widths(i)):
                    b = 2 + CAT[t] + n
                    act.wait_ge(turned, done(NB * p + b))
                    if n == 0:
                        act.wait_ge(o_done, done(GROUPS * p + t // 2 - 1))
                    c0 = (t % 2) * P
                    dst = m["wt_hi"][:, k0 // P:(k0 + w) // P, c0:c0 + P]
                    nc.scalar.activation(dst, T[b % 2][:, 0:w].rearrange("p (j q) -> p j q", q=P),
                                         ACT.Copy).then_inc(hi_done, 1)

            def other_part(p, g):
                h = g // NG
                own, other = slice(HD * h, HD * h + HD), slice(HD - HD * h, 2 * HD - HD * h)
                act.wait_ge(o_done, done(GROUPS * p + g))
                act.wait_ge(y_done, done(GROUPS * p + g - 1))
                nc.scalar.activation(m["o_part"][own, :], O[other, 0:GW], ACT.Copy).then_inc(part_done, 1)

            def z_gate(p, half):
                y = m["y"][:, :, :].rearrange("r k t -> r (k t)")
                act.wait_ge(proj.group_done, done(8 * p + 6 + half))
                nc.scalar.activation(y[:, bass.ds(p * S + half * HALF, HALF)], proj.bank[half][:, :],
                                     ACT.Sigmoid).then_inc(zsig, 1)

            def values_hi(p):
                for b in range(2):
                    act.wait_ge(turned, done(NB * p + b))
                    act.wait_ge(o_done, done(GROUPS * p - 1))
                    t3 = T[b][:, :].rearrange("p (j d) -> p j d", d=P)
                    nc.scalar.activation(m["v"][0][:, 4 * b:4 * b + 4, 0:HD], t3[:, :, 0:HD], ACT.Copy)
                    nc.scalar.activation(m["v"][1][:, 4 * b:4 * b + 4, HD:P], t3[:, :, HD:P],
                                         ACT.Copy).then_inc(hi_done, 1)

            def pack_hi(p, n):
                if n in (0, 2):
                    act.wait_ge(proj.u_done, done(6 * p + n + 1))
                if n == 0:
                    act.wait_ge(logits, done(NCH * p - 1))
                pack.hi(act, n)

            def pair(p, project):
                for s in range(STEPS):
                    if s < TILES:
                        sigmoids(p, s)
                    if project:
                        for kind in SPLIT_AT[s]:
                            proj.split_hi(act, p + 1, kind)
                    if s == 1:
                        values_hi(p)
                    if s >= 4 and s % 2 == 0:
                        other_part(p, s // 2 - 2)
                    if LAG <= s < TILES + LAG:
                        weights_hi(p, s - LAG)
                    if s >= TILES and project:
                        for n in ((0, 1, 2, 3), (4, 5), ())[s - TILES]:
                            pack_hi(p + 1, n)
                    for half in Z_AT[s]:
                        z_gate(p, half)

            modulation.scalar(act)
            for kind in range(2):
                proj.split_hi(act, 0, 2 + kind)
                for n in range(2):
                    pack_hi(0, 2 * kind + n)
            for n in range(4, 6):
                pack_hi(0, n)
            with act.Fori(0, PAIRS - 1) as p:
                pair(p, True)
            pair(PAIRS - 1, False)

        @block.vector
        def _(dve):
            for q in (proj.u_done, proj.sz_done, pack.lo_done, pack.key_lo_done, scanned, lo_done, summed,
                      ada_kept, ada_summed, y_done):
                dve.sem_inc(q, CREDIT)
            for r in range(2):
                nc.vector.memset(m["stick"][r][:, S:S + 1], 1.0).then_inc(one_set, 1)
            modulation.vector(dve)

            def scan(p, t):
                i = t % NT
                at = S - P * (i + 1)
                dve.wait_ge(gates, done(NCH * p + CAT[t] + CH[t] - 1))
                dve.wait_ge(weighted, done(TILES * p + t - 2))
                keep = m["b"][t % 2][:, at:S][:, ::-1]
                nc.vector.tensor_tensor_scan(m["stick"][t % 2][:, at:S][:, ::-1], keep, keep, 1.0, ALU.mult,
                                             ALU.bypass).then_inc(scanned, 1)

            def weights_lo(p, t):
                i = t % NT
                for n, (k0, w) in enumerate(widths(i)):
                    b = 2 + CAT[t] + n
                    dve.wait_ge(hi_done, done(NB * p + b))
                    c0 = (t % 2) * P
                    js = slice(k0 // P, (k0 + w) // P)
                    nc.vector.tensor_tensor(m["wt_lo"][:, js, c0:c0 + P],
                                            T[b % 2][:, 0:w].rearrange("p (j q) -> p j q", q=P),
                                            m["wt_hi"][:, js, c0:c0 + P].bitcast(F32),
                                            ALU.subtract).then_inc(lo_done, 1)

            def add_parts(p, g):
                h, gg = divmod(g, NG)
                own = slice(HD * h, HD * h + HD)
                dve.wait_ge(part_done, done(GROUPS * p + g))
                if g % 2:
                    i = g // 2
                    at = 3 * KT + 3 * p + i if i < 3 else 2 * KT + p
                    dve.wait_ge(ada_done, done(ADA * p + i))
                    col = m["ada_cols"][:, :, :].rearrange("p l f -> p (l f)")[:, bass.ds(at, 1)]
                    nc.vector.tensor_tensor(col, O[:, GW:GW + 1], col, ALU.add).then_inc(ada_kept, 1)
                nc.vector.tensor_tensor(m["o_part"][own, :], O[own, 0:GW], m["o_part"][own, :],
                                        ALU.add).then_inc(summed, 1)
                dve.wait_ge(summed, done(GROUPS * p + g))
                y = m["y"][own, :, :].rearrange("r k t -> r (k t)")[:, bass.ds(p * S + gg * GW, GW)]
                nc.vector.tensor_tensor(y, m["o_part"][own, :], y, ALU.mult).then_inc(y_done, 1)

            def z_gate(p, half):
                y = m["y"][:, :, :].rearrange("r k t -> r (k t)")
                dve.wait_ge(zsig, done(2 * p + half))
                sz = y[:, bass.ds(p * S + half * HALF, HALF)]
                nc.vector.tensor_tensor(sz, proj.bank[half][:, :], sz, ALU.mult).then_inc(proj.sz_done, 1)

            def sum_ada(p, i):
                dve.wait_ge(ada_scaled, done(ADA * p + i))
                dve.wait_ge(ada_done, done(ADA * p + i - 1))
                nc.vector.tensor_reduce(m["ada_sum"][:, :], m["ada_piece"][:, :, :].rearrange("p k f -> p f k"),
                                        axis=AX.X, op=ALU.add).then_inc(ada_summed, 1)

            def finish_ada():
                g, ada = m["g_cols"], m["ada_cols"][:, :, :].rearrange("p l f -> p (l f)")
                n = 0

                def link(ins):
                    nonlocal n
                    n += 1
                    ins.then_inc(chain, 1)
                    dve.wait_ge(chain, n)

                tt = nc.vector.tensor_tensor
                dve.wait_ge(ada_kept, done(ADA * PAIRS - 1))
                link(nc.vector.scalar_tensor_tensor(out=m["mul_col"][1][:, :], in0=ada[:, 4 * KT:5 * KT], scalar=1.0,
                                                    in1=g[:, 1, 0:KT], op0=ALU.add, op1=ALU.mult))
                link(nc.vector.tensor_copy(m["add_col"][1][:, :], ada[:, 3 * KT:4 * KT]))
                for layer in range(DEPTH):
                    cols = slice((3 * layer + 2) * KT, (3 * layer + 3) * KT)
                    link(tt(m["gate_col"][:, layer * KT:(layer + 1) * KT], ada[:, cols], g[:, layer, KT:2 * KT],
                            ALU.mult))
                dve.wait_ge(gate_turned, 1)
                dve.wait_ge(y_done, done(GROUPS * PAIRS - 1))
                nc.vector.tensor_copy(gate_rows_sb[0:DEPTH * KT, 0:P], T[0][0:DEPTH * KT, 0:P]).then_inc(gate_kept, 1)

            def values_lo(p):
                for b in range(2):
                    dve.wait_ge(hi_done, done(NB * p + b))
                    t3 = T[b][:, :].rearrange("p (j d) -> p j d", d=P)
                    js = slice(4 * b, 4 * b + 4)
                    nc.vector.tensor_tensor(m["v"][0][:, js, HD:P], t3[:, :, 0:HD],
                                            m["v"][0][:, js, 0:HD].bitcast(F32), ALU.subtract)
                    nc.vector.tensor_tensor(m["v"][1][:, js, 0:HD], t3[:, :, HD:P],
                                            m["v"][1][:, js, HD:P].bitcast(F32), ALU.subtract).then_inc(lo_done, 1)

            def keep_u(p, kind, half):
                if kind == 2:
                    dve.wait_ge(turned, done(NB * (p - 1) + half))
                proj.keep(dve, p, kind, half, pack)

            def out_weights_hi(k):
                dve.wait_ge(wo_in[k // 2], 16)
                nc.vector.tensor_copy(m["wo_hi"][:, k, :], m["wo_raw"][:, k, :]).then_inc(wo_hi_done, 1)

            def out_weights_lo(k):
                dve.wait_ge(wo_hi_done, k + 1)
                nc.vector.tensor_tensor(m["wo_lo"][:, k, :], m["wo_raw"][:, k, :],
                                        m["wo_hi"][:, k, :].bitcast(F32), ALU.subtract)

            def pair(p, project):
                for s in range(STEPS):
                    if s >= 4 and s % 2 == 0:
                        add_parts(p, s // 2 - 2)
                    if LAG <= s < TILES + LAG:
                        weights_lo(p, s - LAG)
                    if s < TILES:
                        scan(p, s)
                    if s % 4 == 3 and s // 4 < ADA:
                        sum_ada(p, s // 4)
                    for half in Z_AT[s]:
                        z_gate(p, half)
                    if s == 1:
                        values_lo(p)
                    if project:
                        if s >= TILES:
                            for n in ((0, 1, 2), (3,), ())[s - TILES]:
                                pack.lo(dve, p + 1, n)
                        for kind, half in U_AT[s]:
                            keep_u(p + 1, kind, half)
                    for k in () if project else range(*OUT[s]):
                        out_weights_hi(k)
                        if k % 2 == 0:
                            out_weights_lo(k)

            for kind in range(2):
                for half in range(2):
                    keep_u(0, kind, half)
            for n in range(4):
                pack.lo(dve, 0, n)
            for half in range(2):
                keep_u(0, 2, half)
            with dve.Fori(0, PAIRS - 1) as p:
                pair(p, True)
            pair(PAIRS - 1, False)
            finish_ada()

        @block.gpsimd
        def _(pool):
            for q in (weighted, ada_scaled):
                pool.sem_inc(q, CREDIT)
            pool.wait_ge(one_set, 2)

            def weigh(p, t):
                i = t % NT
                at = S - P * (i + 1)
                pool.wait_ge(scanned, done(TILES * p + t))
                a = m["a"][ring(t)]
                nc.gpsimd.tensor_tensor(a[:, at:S], a[:, at:S], m["stick"][t % 2][:, at + 1:S + 1],
                                        ALU.mult).then_inc(weighted, 1)

            def scale_ada(p, i):
                pool.wait_ge(ada_in, 16 * (ADA * p + i) + 16)
                cond = m["cond"][:, :].rearrange("p (k o) -> p k o", o=1).broadcast_to([P, KT, P])
                nc.gpsimd.tensor_tensor(m["ada_piece"][:, :, :], m["ada_piece"][:, :, :], cond,
                                        ALU.mult).then_inc(ada_scaled, 1)

            def pair(p, project):
                for s in range(STEPS):
                    if s < TILES:
                        weigh(p, s)
                    for kind in SPLIT_AT[s] if project else ():
                        proj.split_lo(pool, p + 1, kind)
                    if s % 4 == 1 and s // 4 < ADA:
                        scale_ada(p, s // 4)
                    for k in () if project else range(*OUT[s]):
                        if k % 2:
                            out_weights_lo(k)

            def out_weights_lo(k):
                pool.wait_ge(wo_hi_done, k + 1)
                nc.gpsimd.tensor_tensor(m["wo_lo"][:, k, :], m["wo_raw"][:, k, :],
                                        m["wo_hi"][:, k, :].bitcast(F32), ALU.subtract)

            modulation.gpsimd(pool)
            for kind in range(2, 4):
                proj.split_lo(pool, 0, kind)
            with pool.Fori(0, PAIRS - 1) as p:
                pair(p, True)
            pair(PAIRS - 1, False)

def differential(nc, m, proj, w_out):
    MAPS = 2
    BCH = [len(widths(t)) for t in range(NT)]
    BAT = [sum(BCH[:t]) for t in range(NT)]
    CAT = [MAPS * b for b in BAT]
    NCH = MAPS * sum(BCH)
    NB = sum(BCH) + 2
    LAG = 2
    STEPS = NT + LAG + 1
    L, T, O = m["pm"][0:3], m["pm"][3:5], m["pm"][5]
    RA = 3
    assert NCH % 3 == 0 and NB % 2 == 0

    def ring(t):
        return t % RA

    EARLY = 2
    Z = shares(2 * GROUP, [1] * EARLY + [0] * (STEPS - EARLY))
    QK = shares(4 * GROUP, [0] * EARLY + [2 + t for t in range(EARLY, NT)] + [0] * (STEPS - NT))
    V = shares(2 * GROUP, [0] * NT + [1] * (STEPS - NT))
    Z_AT, U_AT, SPLIT_AT = schedule(Z, QK, V, 1)
    OUT = shares(KT, [0] * (EARLY + 2) + [1] * (STEPS - EARLY - 2))

    def sem(name):
        return nc.alloc_semaphore("d_" + name)

    logits, biased, negmax, expd = sem("logits"), sem("biased"), sem("negmax"), sem("expd")
    inverse, inverse_lam, weighted = sem("inverse"), sem("inverse_lam"), sem("weighted")
    turned, hi_done, lo_done = sem("turned"), sem("hi_done"), sem("lo_done")
    o_done, o_kept, o_squared, sum_done = sem("o_done"), sem("o_kept"), sem("o_squared"), sem("sum_done")
    log_done, rs_done, normed, y_done = sem("log_done"), sem("rs_done"), sem("normed"), sem("y_done")
    zsig, z_gated, b_scaled = sem("zsig"), sem("z_gated"), sem("b_scaled")
    dist_done, table = sem("dist_done"), sem("table")
    halved, seen = sem("halved"), sem("seen")
    wo_in = [sem(f"wo_loaded{k}") for k in range(KT // 2)]
    wo_hi_done = sem("wo_hi_done")
    pack = Packing(nc, m, "d")
    modulation = Modulation(nc, m, 1, "d")
    dist = m["dist"]
    st = m["stat"]

    def col(t, name, n=0):
        at = {"max": 0, "neg": 4, "sum": 6, "inv": 8, "lam": 10}[name]
        return 16 * (t % 2) + at + n

    def last_batch_before(p, t):
        if t >= RA:
            return NB * p + 2 + BAT[t - RA] + BCH[t - RA] - 1
        prev = max(u for u in range(NT) if ring(u) == ring(t))
        return NB * (p - 1) + 2 + BAT[prev] + BCH[prev] - 1

    with nc.Block() as block:

        @block.sync
        def _(sp):
            for kind in range(2, 4):
                proj.load(sp, 0, kind)
            with sp.Fori(0, PAIRS - 1) as p:
                for kind in range(4):
                    proj.load(sp, p + 1, kind)
            sp.wait_ge(proj.group_done, done(8 * PAIRS - 1))
            load_out_weights(sp, m, w_out, wo_in)

        @block.tensor
        def _(pe):
            for q in (proj.group_done, logits, turned, o_done, sum_done):
                pe.sem_inc(q, CREDIT)

            def score(p, t, n):
                if t == 0 and n == 0:
                    pack.ready(pe, p)
                qs = m["q"][n][:, t * P:(t + 1) * P]
                for c, (k0, w) in enumerate(widths(t)):
                    ch = CAT[t] + n * BCH[t] + c
                    bank = L[ch % 3]
                    pe.wait_ge(biased, done(NCH * p + ch - 3))
                    nc.tensor.matmul(bank[:, 0:w], qs, m["k_hi"][n][:, k0:k0 + w], start=True, stop=False)
                    nc.tensor.matmul(bank[:, 0:w], qs, m["k_lo"][n][:, k0:k0 + w], start=False,
                                     stop=True).then_inc(logits, 1)

            def turn(p, t):
                pe.wait_ge(weighted, done(NT * p + t))
                a = m["a"][ring(t)]
                for n, (k0, w) in enumerate(widths(t)):
                    b = 2 + BAT[t] + n
                    pe.wait_ge(lo_done, done(NB * p + b - 2))
                    for j in range(w // P):
                        at = S - P * (t + 1) + k0 + j * P
                        mm = nc.tensor.transpose(T[b % 2][:, j * P:(j + 1) * P], a[:, at:at + P], m["ident"][:, :])
                    mm.then_inc(turned, 1)

            def values(p, g):
                pe.wait_ge(lo_done, done(NB * p + 2 + BAT[2 * g + 1] + BCH[2 * g + 1] - 1))
                pe.wait_ge(log_done, done(NG * p + g - 1))
                tiles = 2 * g + 2
                for j in range(tiles):
                    c0 = P if j == tiles - 1 else 0
                    for i, (v, w) in enumerate(((0, "wt_hi"), (0, "wt_lo"), (1, "wt_hi"))):
                        mm = nc.tensor.matmul(O[:, c0:GW], m["v"][v][:, j, :], m[w][:, j, c0:GW],
                                              start=(j == 0 and i == 0), stop=(j == tiles - 1 and i == MULS - 1))
                mm.then_inc(o_done, 1)

            def sum_squares(p, g):
                pe.wait_ge(o_squared, done(NG * p + g))
                pe.wait_ge(o_kept, done(NG * p + g))
                nc.tensor.matmul(O[:, GW:2 * GW], m["ones"][:, :], m["sub_sq"][g % 2][:, :], start=True,
                                 stop=True).then_inc(sum_done, 1)

            def turn_values(p):
                for b in range(2):
                    pe.wait_ge(proj.u_done, done(6 * p + 4 + b))
                    pe.wait_ge(lo_done, done(NB * p + b - 2))
                    for j in range(4):
                        at = (4 * b + j) * P
                        mm = nc.tensor.transpose(T[b][:, j * P:(j + 1) * P], m["uv"][:, at:at + P], m["ident"][:, :])
                    mm.then_inc(turned, 1)

            def project_share(p, s, project, half):
                for of, (f, l), at in ((p, Z[s], 6 * GROUP), (p + 1, QK[s], 0), (p + 1, V[s], 4 * GROUP)):
                    if project or at == 6 * GROUP:
                        mid = f + (l - f) // 2
                        proj.multiply(pe, of, at + (f, mid)[half], at + (mid, l)[half])

            def pair(p, project):
                for s in range(STEPS):
                    if s == 1:
                        turn_values(p)
                    if s < NT:
                        score(p, s, 0)
                    project_share(p, s, project, 0)
                    if s < NT:
                        score(p, s, 1)
                    if s >= 4 and s % 2 == 0:
                        values(p, s // 2 - 2)
                    if LAG <= s < NT + LAG:
                        turn(p, s - LAG)
                    project_share(p, s, project, 1)
                    if s >= 4 and s % 2 == 0:
                        sum_squares(p, s // 2 - 2)

            proj.multiply(pe, 0, 0, 6 * GROUP, modulation)
            with pe.Fori(0, PAIRS - 1) as p:
                pair(p, True)
            pair(PAIRS - 1, False)

        @block.scalar
        def _(act):
            for q in (pack.hi_done, expd, hi_done, o_kept, o_squared, log_done, rs_done, zsig, b_scaled,
                      proj.u_done):
                act.sem_inc(q, CREDIT)
            act.preload_act_table_set("natural_log_exp_and_others")

            def exponentials(p, t):
                at = S - P * (t + 1)
                for n in range(MAPS):
                    e = (m["a"][ring(t)], m["b"][t % 2])[n]
                    neg, total = col(t, "neg", n), col(t, "sum", n)
                    act.wait_ge(negmax, done(MAPS * (NT * p + t) + n))
                    nc.scalar.activation(e[:, at:S], e[:, at:S], ACT.Exp, bias=st[:, neg:neg + 1], scale=SCALE,
                                         accum_out=st[:, total:total + 1]).then_inc(expd, 1)

            def scale_second(p, t):
                at, lam = S - P * (t + 1), col(t, "lam")
                b = m["b"][t % 2][:, at:S]
                act.wait_ge(inverse_lam, done(NT * p + t))
                nc.scalar.activation(b, b, ACT.Copy, scale=st[:, lam:lam + 1]).then_inc(b_scaled, 1)

            def keep_u(p, kind, half):
                if kind == 2:
                    act.wait_ge(turned, done(NB * (p - 1) + half))
                proj.keep(act, p, kind, half, pack)

            def weights_hi(p, t):
                for n, (k0, w) in enumerate(widths(t)):
                    b = 2 + BAT[t] + n
                    act.wait_ge(turned, done(NB * p + b))
                    if n == 0:
                        act.wait_ge(o_done, done(NG * p + t // 2 - 1))
                    c0 = (t % 2) * P
                    dst = m["wt_hi"][:, k0 // P:(k0 + w) // P, c0:c0 + P]
                    nc.scalar.activation(dst, T[b % 2][:, 0:w].rearrange("p (j q) -> p j q", q=P),
                                         ACT.Copy).then_inc(hi_done, 1)

            def keep_output(p, g):
                act.wait_ge(o_done, done(NG * p + g))
                act.wait_ge(sum_done, done(NG * p + g - 2))
                if g == 0:
                    act.wait_ge(z_gated, done(p))
                else:
                    act.wait_ge(y_done, done(NG * p + g - 2))
                nc.scalar.activation(m["sub_sq"][g % 2][:, :], O[:, 0:GW], ACT.Square).then_inc(o_squared, 1)
                nc.scalar.activation(m["sub_o"][g % 2][:, :], O[:, 0:GW], ACT.Copy).then_inc(o_kept, 1)

            def inverse_root(p, g):
                act.wait_ge(sum_done, done(NG * p + g))
                nc.scalar.activation(m["sub_rs"][0][:, :], O[:, GW:2 * GW], ACT.Ln, scale=1.0 / P,
                                     bias=m["eps"][:, 0:1]).then_inc(log_done, 1)
                act.wait_ge(log_done, done(NG * p + g))
                act.wait_ge(normed, done(NG * p + g - 1))
                nc.scalar.activation(m["sub_rs"][1][:, :], m["sub_rs"][0][:, :], ACT.Exp,
                                     scale=-0.5).then_inc(rs_done, 1)

            def z_gate(p):
                y = m["y"][:, :, :].rearrange("r k t -> r (k t)")[:, bass.ds(p * S, S)]
                act.wait_ge(proj.sz_done, done(2 * p + 1))
                act.wait_ge(y_done, done(NG * p - 1))
                nc.scalar.activation(m["z_sig"][:, :], y, ACT.Sigmoid).then_inc(zsig, 1)
                act.preload_act_table_set("natural_log_exp_and_others")

            def values_hi(p):
                for b in range(2):
                    act.wait_ge(turned, done(NB * p + b))
                    act.wait_ge(o_done, done(NG * p - 1))
                    t3 = T[b][:, :].rearrange("p (j d) -> p j d", d=P)
                    nc.scalar.activation(m["v"][0][:, 4 * b:4 * b + 4, :], t3, ACT.Copy).then_inc(hi_done, 1)

            def pack_hi(p, n):
                if n in (0, 2):
                    act.wait_ge(proj.u_done, done(6 * p + n + 1))
                if n == 0:
                    act.wait_ge(logits, done(NCH * p - 1))
                pack.hi(act, n)

            def pair(p, project):
                for s in range(STEPS):
                    if s >= 5 and s % 2 == 1:
                        inverse_root(p, (s - 5) // 2)
                    if 1 <= s <= NT:
                        scale_second(p, s - 1)
                    if s < NT:
                        exponentials(p, s)
                    if project:
                        for kind in SPLIT_AT[s]:
                            proj.split_hi(act, p + 1, kind)
                    if s == 1:
                        values_hi(p)
                    if s == EARLY:
                        z_gate(p)
                    if s >= 4 and s % 2 == 0:
                        keep_output(p, s // 2 - 2)
                    if LAG <= s < NT + LAG:
                        weights_hi(p, s - LAG)
                    if s >= NT and project:
                        for n in ((0, 1, 2, 3), (4, 5), ())[s - NT]:
                            pack_hi(p + 1, n)
                    for kind, half in U_AT[s] if project else ():
                        keep_u(p + 1, kind, half)
                inverse_root(p, NG - 1)

            modulation.scalar(act)
            for kind in range(2):
                for half in range(2):
                    keep_u(0, kind, half)
                proj.split_hi(act, 0, 2 + kind)
                for n in range(2):
                    pack_hi(0, 2 * kind + n)
            for n in range(4, 6):
                pack_hi(0, n)
            for half in range(2):
                keep_u(0, 2, half)
            with act.Fori(0, PAIRS - 1) as p:
                pair(p, True)
            pair(PAIRS - 1, False)

        @block.vector
        def _(dve):
            for q in (proj.sz_done, z_gated, pack.lo_done, pack.key_lo_done, biased, negmax, inverse, inverse_lam,
                      weighted, lo_done, halved):
                dve.sem_inc(q, CREDIT)
            modulation.vector(dve)
            slope8 = 8.0 * 2.0 ** (-8.0 / PAIRS)
            dve.wait_ge(dist_done, 1)
            nc.vector.tensor_scalar(m["bias"][:, :], dist[:, :], -slope8, None, ALU.mult).then_inc(table, 1)
            nc.vector.tensor_scalar(m["b"][1][:, :], dist[:, :], slope8, None, ALU.mult).then_inc(table, 1)
            dve.wait_ge(table, 2)
            nc.vector.tensor_tensor(m["bias"][:, :], m["bias"][:, :], m["b"][1][:, :], ALU.min).then_inc(table, 1)
            dve.wait_ge(table, 3)
            nc.vector.memset(m["bias"][0:CHUNK, S - CHUNK:S], NEG).then_inc(table, 1)
            dve.wait_ge(table, 4)

            def add_bias(p, t):
                if t == 0:
                    dve.wait_ge(halved, done(p - 1))
                for n in range(MAPS):
                    x = (m["a"][ring(t)], m["b"][t % 2])[n]
                    if n == 0:
                        dve.wait_ge(turned, done(last_batch_before(p, t)))
                    for c, (k0, w) in enumerate(widths(t)):
                        ch = CAT[t] + n * BCH[t] + c
                        at = S - P * (t + 1) + k0
                        mx = col(t, "max", 2 * n + c)
                        dve.wait_ge(logits, done(NCH * p + ch))
                        dve.sem_inc(seen, 1)
                        nc.vector.tensor_tensor_reduce(
                            out=x[:, at:at + w], in0=L[ch % 3][:, 0:w], in1=m["bias"][:, at:at + w], scale=1.0,
                            scalar=-3e38, op0=ALU.add, op1=ALU.max, accum_out=st[:, mx:mx + 1]).then_inc(biased, 1)
                    dve.wait_ge(biased, done(NCH * p + ch))
                    mx, neg = col(t, "max", 2 * n), col(t, "neg", n)
                    if BCH[t] == 2:
                        ins = nc.vector.tensor_scalar(st[:, neg:neg + 1], st[:, mx:mx + 1], st[:, mx + 1:mx + 2],
                                                      -SCALE, ALU.max, ALU.mult)
                    else:
                        ins = nc.vector.tensor_scalar(st[:, neg:neg + 1], st[:, mx:mx + 1], -SCALE, None, ALU.mult)
                    ins.then_inc(negmax, 1)
                if t == NT - 1:
                    nc.vector.tensor_scalar(m["bias"][:, :], m["bias"][:, :], 0.5, None, ALU.mult).then_inc(halved, 1)

            def invert(p, t):
                total, inv, lam = col(t, "sum"), col(t, "inv"), col(t, "lam")
                dve.wait_ge(expd, done(MAPS * (NT * p + t) + 1))
                nc.vector.reciprocal(st[:, inv:inv + 2], st[:, total:total + 2]).then_inc(inverse, 1)
                dve.wait_ge(inverse, done(NT * p + t))
                nc.vector.tensor_scalar(st[:, lam:lam + 1], st[:, inv + 1:inv + 2], m["lam"][:, 2:3], None,
                                        ALU.mult).then_inc(inverse_lam, 1)

            def combine(p, t):
                at, inv = S - P * (t + 1), col(t, "inv")
                a, b = m["a"][ring(t)], m["b"][t % 2]
                dve.wait_ge(b_scaled, done(NT * p + t))
                nc.vector.scalar_tensor_tensor(out=a[:, at:S], in0=a[:, at:S], scalar=st[:, inv:inv + 1],
                                               in1=b[:, at:S], op0=ALU.mult, op1=ALU.add).then_inc(weighted, 1)

            def weights_lo(p, t):
                for n, (k0, w) in enumerate(widths(t)):
                    b = 2 + BAT[t] + n
                    dve.wait_ge(hi_done, done(NB * p + b))
                    c0 = (t % 2) * P
                    js = slice(k0 // P, (k0 + w) // P)
                    nc.vector.tensor_tensor(m["wt_lo"][:, js, c0:c0 + P],
                                            T[b % 2][:, 0:w].rearrange("p (j q) -> p j q", q=P),
                                            m["wt_hi"][:, js, c0:c0 + P].bitcast(F32),
                                            ALU.subtract).then_inc(lo_done, 1)

            def keep_z(p, half):
                y = m["y"][:, :, :].rearrange("r k t -> r (k t)")[:, bass.ds(p * S + half * HALF, HALF)]
                dve.wait_ge(proj.group_done, done(8 * p + 6 + half))
                nc.vector.tensor_copy(y, proj.bank[half][:, :]).then_inc(proj.sz_done, 1)

            def z_gate(p):
                y = m["y"][:, :, :].rearrange("r k t -> r (k t)")[:, bass.ds(p * S, S)]
                dve.wait_ge(zsig, done(p))
                nc.vector.scalar_tensor_tensor(out=y, in0=y, scalar=m["lam"][:, 3:4], in1=m["z_sig"][:, :],
                                               op0=ALU.mult, op1=ALU.mult).then_inc(z_gated, 1)

            def values_lo(p):
                for b in range(2):
                    dve.wait_ge(hi_done, done(NB * p + b))
                    t3 = T[b][:, :].rearrange("p (j d) -> p j d", d=P)
                    js = slice(4 * b, 4 * b + 4)
                    nc.vector.tensor_tensor(m["v"][1][:, js, :], t3, m["v"][0][:, js, :].bitcast(F32),
                                            ALU.subtract).then_inc(lo_done, 1)

            def out_weights_hi(k):
                dve.wait_ge(wo_in[k // 2], 16)
                nc.vector.tensor_copy(m["wo_hi"][:, k, :], m["wo_raw"][:, k, :]).then_inc(wo_hi_done, 1)

            def out_weights_lo(k):
                dve.wait_ge(wo_hi_done, k + 1)
                nc.vector.tensor_tensor(m["wo_lo"][:, k, :], m["wo_raw"][:, k, :],
                                        m["wo_hi"][:, k, :].bitcast(F32), ALU.subtract)

            def pair(p, project):
                for s in range(STEPS):
                    if 1 <= s <= NT:
                        invert(p, s - 1)
                    if s < NT:
                        add_bias(p, s)
                    if 1 <= s <= NT:
                        combine(p, s - 1)
                    for half in Z_AT[s]:
                        keep_z(p, half)
                    if s == 1:
                        values_lo(p)
                    if s == EARLY + 1:
                        z_gate(p)
                    if LAG <= s < NT + LAG:
                        weights_lo(p, s - LAG)
                    if project:
                        if s >= NT:
                            for n in ((0, 1), (2, 3), ())[s - NT]:
                                pack.lo(dve, p + 1, n)
                    for k in () if project else range(*OUT[s]):
                        out_weights_hi(k)
                        if k % 2 == 0:
                            out_weights_lo(k)

            for n in range(4):
                pack.lo(dve, 0, n)
            with dve.Fori(0, PAIRS - 1) as p:
                pair(p, True)
            pair(PAIRS - 1, False)

        @block.gpsimd
        def _(pool):
            for q in (normed, y_done):
                pool.sem_inc(q, CREDIT)
            nc.gpsimd.iota(dist[:, :], pattern=[[-1, S]], base=S - P, channel_multiplier=1).then_inc(dist_done, 1)

            def norm_output(p, g):
                o = m["sub_o"][g % 2][:, :]
                pool.wait_ge(rs_done, done(NG * p + g))
                pool.wait_ge(o_kept, done(NG * p + g))
                nc.gpsimd.tensor_tensor(o, o, m["sub_rs"][1][:, :], ALU.mult).then_inc(normed, 1)
                pool.wait_ge(normed, done(NG * p + g))
                if g == 0:
                    pool.wait_ge(z_gated, done(p))
                y = m["y"][:, :, :].rearrange("r k t -> r (k t)")[:, bass.ds(p * S + g * GW, GW)]
                nc.gpsimd.tensor_tensor(y, o, y, ALU.mult).then_inc(y_done, 1)

            def pair(p, project):
                for s in range(STEPS):
                    for kind in SPLIT_AT[s] if project else ():
                        proj.split_lo(pool, p + 1, kind)
                    if s >= 5 and s % 2 == 1:
                        norm_output(p, (s - 5) // 2)
                    for k in () if project else range(*OUT[s]):
                        if k % 2:
                            out_weights_lo(k)
                norm_output(p, NG - 1)

            def out_weights_lo(k):
                pool.wait_ge(wo_hi_done, k + 1)
                nc.gpsimd.tensor_tensor(m["wo_lo"][:, k, :], m["wo_raw"][:, k, :],
                                        m["wo_hi"][:, k, :].bitcast(F32), ALU.subtract)

            modulation.gpsimd(pool)
            for kind in range(2, 4):
                proj.split_lo(pool, 0, kind)
            with pool.Fori(0, PAIRS - 1) as p:
                pair(p, True)
            pair(PAIRS - 1, False)


def project_out(nc, m, sb, layer, source, target, gate_rows, next_proj):
    def sem(name):
        return nc.alloc_semaphore(f"o{layer}_{name}")

    y_hi = [sb(f"o{layer}_y_hi{s}", [P, KT, P], F32R, 112 + 4 * s) for s in range(2)]
    y_lo = [sb(f"o{layer}_y_lo{s}", [P, KT, P], F32R, 120 + 4 * s) for s in range(2)]
    xt = [sb(f"o{layer}_x{s}", [P, D], F32, 128 + 4 * s) for s in range(2)]
    res = [sb(f"o{layer}_res{s}", [P, D], F32, 136 + 4 * s) for s in range(2)]
    gate = sb(f"o{layer}_gate", [P, D], F32, 144)
    xn = [sb(f"o{layer}_xn{s}", [P, D], F32, 148 + 4 * s) for s in range(2)]
    st = m["stat"]
    bank = m["pm"][0:4]
    T = [m["pm"][4:6], m["pm"][6:8]]
    gate_in = sem("gate_loaded")
    loaded = [sem(f"x_loaded{s}") for s in range(2)]
    stored = [sem(f"stored{s}") for s in range(2)]
    hi_done, lo_done, product = sem("hi_done"), sem("lo_done"), sem("product")
    squares, summed, mean_done, root_done, rstd_done = (sem("squares"), sem("summed"), sem("mean_done"),
                                                        sem("root_done"), sem("rstd_done"))
    scaled, added = sem("scaled"), sem("added")
    if next_proj:
        squares2, mean2, root2, rstd2 = sem("next_squares"), sem("next_mean"), sem("next_root"), sem("next_rstd")
        scaled2, turned, left_kept, right_kept = sem("next_scaled"), sem("turned"), sem("left_kept"), sem("right_kept")
    SQ, SUM, MEAN, ROOT, RSTD, SQ2, MEAN2, ROOT2, RSTD2 = 0, 2, 3, 4, 5, 6, 7, 8, 9

    def col(s, n):
        return st[:, 16 * s + n:16 * s + n + 1]

    with nc.Block() as block:

        @block.sync
        def _(sp):
            sp.dma_start(gate[:, :], gate_rows[layer:layer + 1, :].broadcast_to([P, D])).then_inc(gate_in, 16)
            for s in range(2):
                sp.dma_start(xt[s][:, :], source[s * P:(s + 1) * P, :]).then_inc(loaded[s], 16)
            if next_proj:
                next_proj.first_loads(sp)

            def store(t, s):
                sp.wait_ge(added, done(t))
                sp.dma_start(target[bass.ds(t * P, P), :], res[s][:, :]).then_inc(stored[s], 16)

            with sp.Fori(0, NT // 2 - 1) as r:
                for s in range(2):
                    store(2 * r + s, s)
                    sp.dma_start(xt[s][:, :], source[bass.ds((2 * r + s + 2) * P, P), :]).then_inc(loaded[s], 16)
            for s in range(2):
                store(NT - 2 + s, s)
            for s in range(2):
                sp.wait_ge(stored[s], 16 + 16 * (NT // 2))

        @block.scalar
        def _(act):
            for q in (hi_done, squares, root_done) + ((squares2, root2, left_kept) if next_proj else ()):
                act.sem_inc(q, CREDIT)
            for s in range(2):
                act.sem_inc(stored[s], 16)
            if next_proj:
                act.sem_inc(next_proj.hi_done, CREDIT)

            def split(t, s):
                act.wait_ge(product, done(2 * (t - 2) + 1))
                nc.scalar.activation(y_hi[s][:, :, :], m["y"][:, :, bass.ds(t * P, P)], ACT.Copy).then_inc(hi_done, 1)

            def finish(t, s, r):
                act.wait_ge(stored[s], 16 + 16 * r)
                for h in range(2):
                    act.wait_ge(product, done(2 * t + h))
                    if h == 0 and next_proj:
                        act.wait_ge(scaled2, done(t - 2))
                    nc.scalar.activation(res[s][:, h * HALF:(h + 1) * HALF], bank[2 * s + h][:, :], ACT.Square,
                                         accum_out=col(s, SQ + h)).then_inc(squares, 1)
                act.wait_ge(mean_done, done(t))
                nc.scalar.activation(col(s, ROOT), col(s, MEAN), ACT.Sqrt).then_inc(root_done, 1)

            def renormalise(t, s):
                if not next_proj:
                    return
                act.wait_ge(added, done(t))
                act.wait_ge(turned, done(t - 2))
                nc.scalar.activation(xn[s][:, :], res[s][:, :], ACT.Square, accum_out=col(s, SQ2)).then_inc(squares2, 1)
                act.wait_ge(mean2, done(t))
                nc.scalar.activation(col(s, ROOT2), col(s, MEAN2), ACT.Sqrt).then_inc(root2, 1)

            def keep_left(t, s):
                if not next_proj:
                    return
                act.wait_ge(turned, done(t))
                t4 = T[s][0][:, :].rearrange("p (k t) -> p k t", t=P)
                nc.scalar.activation(m["y"][:, 0:4, bass.ds(t * P, P)], t4, ACT.Copy).then_inc(left_kept, 1)

            def tile(t, s, r):
                split(t + 1, 1 - s)
                finish(t, s, r)
                renormalise(t, s)

            split(0, 0)
            tile(0, 0, 0)
            with act.Fori(0, NT // 2 - 1) as r:
                tile(2 * r + 1, 1, r)
                keep_left(2 * r, 0)
                tile(2 * r + 2, 0, r + 1)
                keep_left(2 * r + 1, 1)
            finish(NT - 1, 1, NT // 2 - 1)
            renormalise(NT - 1, 1)
            keep_left(NT - 2, 0)
            keep_left(NT - 1, 1)
            if next_proj:
                next_proj.first_hi(act)

        @block.vector
        def _(dve):
            next_sems = (mean2, rstd2, scaled2, right_kept) if next_proj else ()
            for q in (lo_done, summed, mean_done, rstd_done, scaled) + next_sems:
                dve.sem_inc(q, CREDIT)
            if next_proj:
                dve.sem_inc(next_proj.lo_done, CREDIT)
            dve.wait_ge(gate_in, 16)

            def split(t, s):
                dve.wait_ge(hi_done, done(t))
                nc.vector.tensor_tensor(y_lo[s][:, :, :], m["y"][:, :, bass.ds(t * P, P)],
                                        y_hi[s][:, :, :].bitcast(F32), ALU.subtract).then_inc(lo_done, 1)

            def finish(t, s):
                dve.wait_ge(squares, done(2 * t + 1))
                nc.vector.tensor_tensor(col(s, SUM), col(s, SQ), col(s, SQ + 1), ALU.add).then_inc(summed, 1)
                dve.wait_ge(summed, done(t))
                nc.vector.tensor_scalar(col(s, MEAN), col(s, SUM), 1.0 / D, EPS, ALU.mult,
                                        ALU.add).then_inc(mean_done, 1)
                dve.wait_ge(root_done, done(t))
                nc.vector.reciprocal(col(s, RSTD), col(s, ROOT)).then_inc(rstd_done, 1)
                dve.wait_ge(rstd_done, done(t))
                for h in range(2):
                    cols = slice(h * HALF, (h + 1) * HALF)
                    nc.vector.scalar_tensor_tensor(out=res[s][:, cols], in0=bank[2 * s + h][:, :],
                                                   scalar=col(s, RSTD), in1=gate[:, cols], op0=ALU.mult,
                                                   op1=ALU.mult).then_inc(scaled, 1)

            def renormalise(t, s):
                if not next_proj:
                    return
                dve.wait_ge(squares2, done(t))
                nc.vector.tensor_scalar(col(s, MEAN2), col(s, SQ2), 1.0 / D, EPS, ALU.mult, ALU.add).then_inc(mean2, 1)
                dve.wait_ge(root2, done(t))
                nc.vector.reciprocal(col(s, RSTD2), col(s, ROOT2)).then_inc(rstd2, 1)
                dve.wait_ge(rstd2, done(t))
                nc.vector.tensor_scalar(xn[s][:, :], res[s][:, :], col(s, RSTD2), None, ALU.mult).then_inc(scaled2, 1)

            def keep_right(t, s):
                if not next_proj:
                    return
                dve.wait_ge(turned, done(t))
                t4 = T[s][1][:, :].rearrange("p (k t) -> p k t", t=P)
                nc.vector.tensor_copy(m["y"][:, 4:8, bass.ds(t * P, P)], t4).then_inc(right_kept, 1)

            def tile(t, s):
                split(t + 1, 1 - s)
                finish(t, s)
                renormalise(t, s)

            split(0, 0)
            tile(0, 0)
            with dve.Fori(0, NT // 2 - 1) as r:
                tile(2 * r + 1, 1)
                keep_right(2 * r, 0)
                tile(2 * r + 2, 0)
                keep_right(2 * r + 1, 1)
            finish(NT - 1, 1)
            renormalise(NT - 1, 1)
            keep_right(NT - 2, 0)
            keep_right(NT - 1, 1)
            if next_proj:
                next_proj.first_lo(dve)

        @block.gpsimd
        def _(pool):
            pool.sem_inc(added, CREDIT)
            with pool.Fori(0, NT // 2) as r:
                for s in range(2):
                    pool.wait_ge(scaled, done(2 * (2 * r + s) + 1))
                    pool.wait_ge(loaded[s], 16 * r + 16)
                    nc.gpsimd.tensor_tensor(res[s][:, :], res[s][:, :], xt[s][:, :], ALU.add).then_inc(added, 1)

        @block.tensor
        def _(pe):
            for q in (product,) + ((turned,) if next_proj else ()):
                pe.sem_inc(q, CREDIT)

            def multiply(t, s):
                pe.wait_ge(lo_done, done(t))
                for h in range(2):
                    pe.wait_ge(scaled, done(2 * (t - 2) + h))
                    for k in range(KT):
                        for i, (y, w) in enumerate(((y_hi, "wo_hi"), (y_hi, "wo_lo"), (y_lo, "wo_hi"))):
                            mm = nc.tensor.matmul(bank[2 * s + h][:, :], y[s][:, k, :],
                                                  m[w][:, k, h * HALF:(h + 1) * HALF],
                                                  start=(k == 0 and i == 0), stop=(k == KT - 1 and i == MULS - 1))
                    mm.then_inc(product, 1)

            def turn(t, s):
                if not next_proj:
                    return
                pe.wait_ge(scaled2, done(t))
                pe.wait_ge(left_kept, done(t - 2))
                pe.wait_ge(right_kept, done(t - 2))
                for k in range(KT):
                    mm = nc.tensor.transpose(T[s][k // 4][:, k % 4 * P:(k % 4 + 1) * P],
                                             xn[s][:, k * P:(k + 1) * P], m["ident"][:, :])
                mm.then_inc(turned, 1)

            multiply(0, 0)
            with pe.Fori(0, NT // 2 - 1) as r:
                multiply(2 * r + 1, 1)
                turn(2 * r, 0)
                multiply(2 * r + 2, 0)
                turn(2 * r + 1, 1)
            multiply(NT - 1, 1)
            turn(NT - 2, 0)
            turn(NT - 1, 1)


_INS = ["x", "c", "w_ada", "b_ada", "g_pre", "g_post", "w_in", "w_out", "diff_lambda", "diff_subln"]


def kernel(**inputs):
    import numpy as np
    import concourse.bacc as bacc
    from concourse.bass_utils import run_bass_kernel_spmd

    nc = bacc.Bacc("TRN2", target_bir_lowering=False, num_devices=1)
    arrays, args = {}, {}
    for name in _INS:
        a = np.ascontiguousarray(inputs[name])
        if name == "x":
            a = a.reshape(S, D)
        arrays[f"in_{name}_dram"] = a
        args[name] = nc.dram_tensor(f"in_{name}_dram", a.shape, mybir.dt.from_np(a.dtype), kind="ExternalInput").ap()
    args["out"] = nc.dram_tensor("out_dram", [S, D], F32, kind="ExternalOutput").ap()
    trunk(nc, **args)
    r = run_bass_kernel_spmd(nc, [arrays], core_ids=[0])
    return r.results[0]["out_dram"].reshape(1, S, D)
```

```python
import math

import concourse.bass as bass
from concourse import mybir

F32 = mybir.dt.float32
F32R = mybir.dt.float32r
BF16 = mybir.dt.bfloat16
I32 = mybir.dt.int32
ALU = mybir.AluOpType
ACT = mybir.ActivationFunctionType
AX = mybir.AxisListType

P = 128
D = 1024
S = 1024
KT = D // P
NT = S // P
HALF = 512
PAIRS = D // P
HD = 64
GW = 2 * P
NG = NT // 2
SCALE = HD ** -0.5
CHUNK = 64
EPS = 1e-6
NEG = -1e30
DEPTH = 2
CREDIT = 32
AHEAD = NT // 2
MULS = 3
GROUP = MULS * KT
KB = 1024


def done(n):
    return CREDIT + 1 + n


def widths(i):
    w = P * (i + 1)
    return [(c, min(HALF, w - c)) for c in range(0, w, HALF)]


def shares(total, weights):
    whole, acc, cut = sum(weights), 0, [0]
    for w in weights:
        acc += w
        cut.append(round(total * acc / whole))
    return list(zip(cut[:-1], cut[1:]))


def schedule(z, qk, v, lags):
    steps = range(len(z))

    def end(parts, group):
        return next(s for s in steps if parts[s][1] >= (group + 1) * GROUP)

    z_end = [end(z, half) for half in range(2)]
    u_end = [end(qk, g) for g in range(4)] + [end(v, half) for half in range(2)]
    split = [0] + [e + lag for e, lag in zip((z_end[1], u_end[1], u_end[3]), lags)]
    return ([[half for half in range(2) if z_end[half] == s] for s in steps],
            [[divmod(g, 2) for g in range(6) if u_end[g] == s] for s in steps],
            [[kind for kind in range(4) if split[kind] == s] for s in steps])


def trunk(nc, x, c, w_ada, b_ada, g_pre, g_post, w_in, w_out, diff_lambda, diff_subln, out):
    base = (nc.sbuf_base + 63) // 64 * 64

    def sb(name, shape, dtype, kb):
        return nc.alloc_sbuf_tensor_at(name, shape, dtype, offset=base + int(kb * KB))

    x1 = nc.dram_tensor("x_between", [S, D], F32, kind="Internal").ap()
    gate_rows = nc.dram_tensor("gate_rows", [DEPTH, D], F32, kind="Internal").ap()

    m = {}
    m["h_hi"] = sb("h_hi", [P, KT, S], F32R, 0)
    m["h_lo"] = sb("h_lo", [P, KT, S], F32R, 32)
    m["ada_w"] = sb("ada_w", [P, KT, 2 * D], F32, 0)
    m["wo_hi"] = sb("wo_hi", [P, KT, D], F32R, 0)
    m["wo_raw"] = sb("wo_raw", [P, KT, D], F32, 32)
    m["wo_lo"] = sb("wo_lo", [P, KT, D], F32R, 32)
    m["y"] = sb("y", [P, KT, S], F32, 64)
    m["w_hi"] = [sb(f"w_hi{s}", [P, KT, P], F32R, 96 + 8 * s) for s in range(2)]
    m["w_raw"] = [sb(f"w_raw{s}", [P, KT, P], F32, 100 + 8 * s) for s in range(2)]
    m["w_lo"] = [sb(f"w_lo{s}", [P, KT, P], F32R, 100 + 8 * s) for s in range(2)]
    m["uq"] = sb("uq", [P, S], F32, 112)
    m["uk"] = sb("uk", [P, S], F32, 116)
    m["uv"] = sb("uv", [P, S], F32, 120)
    m["ada_piece"] = sb("ada_piece", [P, KT, P], F32, 124)
    m["z_sig"] = sb("z_sig", [P, S], F32, 124)
    m["sub_o"] = [sb(f"sub_o{r}", [P, GW], F32, 124 + r) for r in range(2)]
    m["h32"] = [sb(f"h32_{r}", [P, S], F32, 160 + 4 * r) for r in range(2)]
    m["q"] = [sb(f"q{h}", [P, S], F32R, 128 + 4 * h) for h in range(2)]
    m["k_hi"] = [sb(f"k_hi{h}", [P, S], F32R, 136 + 4 * h) for h in range(2)]
    m["k_lo"] = [sb(f"k_lo{h}", [P, S], F32R, 144 + 4 * h) for h in range(2)]
    m["v"] = [sb(f"v{h}", [P, NT, P], F32R, 152 + 4 * h) for h in range(2)]
    m["a"] = [sb(f"a{r}", [P, S], F32, 160 + 4 * r) for r in range(3)]
    m["b"] = [sb(f"b{r}", [P, S], F32, 172 + 4 * r) for r in range(2)]
    m["stick"] = [sb(f"stick{r}", [P, S + 1], F32, 180 + 4.0625 * r) for r in range(2)]
    m["bias"] = sb("bias", [P, S], F32, 180)
    m["sub_sq"] = [sb(f"sub_sq{r}", [P, GW], F32, 184 + r) for r in range(2)]
    m["sub_rs"] = [sb(f"sub_rs{r}", [P, GW], F32, 186 + r) for r in range(2)]
    m["dist"] = sb("dist", [P, S], I32, 172)
    m["wt_hi"] = sb("wt_hi", [P, NT, GW], F32R, 188.125)
    m["wt_lo"] = sb("wt_lo", [P, NT, GW], F32R, 196.125)
    at = [204.125]

    def small(name, shape, dtype, nbytes):
        t = sb(name, shape, dtype, at[0])
        at[0] += (nbytes + 31) // 32 * 32 / KB
        return t

    m["o_part"] = small("o_part", [P, GW], F32, 4 * GW)
    m["ident"] = small("ident", [P, P], F32, 4 * P)
    m["ones"] = small("ones", [P, P], F32, 4 * P)
    m["ident_b"] = small("ident_b", [P, P], BF16, 2 * P)
    m["mask_b"] = small("mask_b", [P, P], BF16, 2 * P)
    m["mul_col"] = [small(f"mul_col{l}", [P, KT], F32, 4 * KT) for l in range(DEPTH)]
    m["add_col"] = [small(f"add_col{l}", [P, KT], F32, 4 * KT) for l in range(DEPTH)]
    m["ada_sum"] = small("ada_sum", [P, P], F32, 4 * P)
    m["lam"] = small("lam", [P, 8], F32, 32)
    m["cond"] = small("cond_act", [P, KT], F32, 4 * KT)
    m["ada_cols"] = small("ada_cols", [P, DEPTH, 3 * KT], F32, 12 * KT * DEPTH)
    m["g_cols"] = small("g_cols", [P, DEPTH, 2 * KT], F32, 8 * KT * DEPTH)
    m["gate_col"] = small("gate_col", [P, DEPTH * KT], F32, 4 * KT * DEPTH)
    m["eps"] = small("eps", [P, 1], F32, 4)
    m["stat"] = small("stat", [P, 32], F32, 128)
    m["pm"] = [nc.alloc_psum_tensor(f"bank{i}", [P, HALF], F32) for i in range(8)]
    assert base + at[0] * KB <= nc.sbuf_usable_end, (base + at[0] * KB, nc.sbuf_usable_end)

    proj = [Projection(nc, m, w_in[layer], "sd"[layer]) for layer in range(DEPTH)]
    prepare(nc, m, sb, x, c, w_ada, b_ada, g_pre, g_post, diff_lambda, diff_subln, proj[0])
    outp = [OutProjection(nc, m, sb, layer) for layer in range(DEPTH)]
    stick_breaking(nc, m, proj[0], outp[0], w_out[0], w_ada, gate_rows)
    project_out(nc, m, sb, 0, outp[0], x, x1, gate_rows, proj[1])
    differential(nc, m, proj[1], outp[1], w_out[1])
    project_out(nc, m, sb, 1, outp[1], x1, out, gate_rows, None)


def prepare(nc, m, sb, x, c, w_ada, b_ada, g_pre, g_post, diff_lambda, diff_subln, proj):
    def sem(name):
        return nc.alloc_semaphore("p_" + name)

    PIECE = 4 * P
    PIECES = 2 * D // PIECE
    R = 4
    ROUNDS = NT // R
    cond_in = sb("cond_in", [P, KT], F32, 176)
    cond_sig = sb("cond_sig", [P, KT], F32, 176.25)
    lam_in = sb("lam_in", [P, 4, HD], F32, 179)
    lam_prod = sb("lam_prod", [P, 2, HD], F32, 180)
    lam_sums = sb("lam_sums", [P, 4], F32, 181)
    scale1 = sb("scale1", [P, KT], F32, 181.25)
    xt = [sb(f"p_x{s}", [P, D], F32, 128 + 4 * s) for s in range(R)]
    xn = [sb(f"p_xn{s}", [P, D], F32, 144 + 4 * s) for s in range(R)]
    st = m["stat"]
    T = [m["pm"][1:3], m["pm"][3:5]]
    cols = m["pm"][0]

    small_in = sem("small_loaded")
    BY_ROW, BY_SUM = 1, (0, 2, 3)
    assert PIECES == 4
    ada_row = sb("ada_row", [1, PIECE], F32, 176.5)
    row = m["pm"][5]
    row_done, row_kept = sem("row_done"), sem("row_kept")
    acc = [sb(f"ada_acc{e}", [P, 2 * D], F32, 160 + 8 * e) for e in range(2)]
    OPS = KT + 1
    ada_in = [sem(f"ada_loaded{i}") for i in range(PIECES)]
    acc_done = sem("acc_done")
    loaded = [sem(f"x_loaded{s}") for s in range(R)]
    cond_loaded = sem("cond_loaded")
    cond_sig_done, cond_done, cols_done = sem("cond_sig_done"), sem("cond_done"), sem("cols_done")
    zeroed, consts, chain = sem("zeroed"), sem("consts"), sem("vector_chain")
    lam_exp, lam_sum = sem("lam_exp"), sem("lam_sum")
    squares, mean_done, root_done, rstd_done = sem("squares"), sem("mean_done"), sem("root_done"), sem("rstd_done")
    scaled, turned, left_kept, right_kept = sem("scaled"), sem("turned"), sem("left_kept"), sem("right_kept")
    lam_init = 0.8 - 0.6 * math.exp(-0.3 * 1)

    with nc.Block() as block:

        @block.sync
        def _(sp):
            for s in range(R):
                sp.dma_start(xt[s][:, :], x[s * P:(s + 1) * P, :]).then_inc(loaded[s], 16)

            def ada(i):
                sp.dma_start(m["ada_w"][:, :, i * PIECE:(i + 1) * PIECE],
                             w_ada[0, :, i * PIECE:(i + 1) * PIECE]
                             .rearrange("(k p) f -> p k f", p=P)).then_inc(ada_in[i], 16)

            ada(0)
            for s in range(R):
                sp.wait_ge(scaled, done(s))
                sp.dma_start(xt[s][:, :], x[(R + s) * P:(R + s + 1) * P, :]).then_inc(loaded[s], 16)
            for i in range(1, PIECES):
                ada(i)
            proj.first_loads(sp)

        @block.gpsimd
        def _(pool):
            nc.gpsimd.memset(m["ident"][:, :], 0.0).then_inc(zeroed, 1)
            nc.gpsimd.memset(m["mask_b"][:, :], 0.0).then_inc(zeroed, 1)
            nc.gpsimd.memset(m["ones"][:, :], 1.0).then_inc(zeroed, 1)
            nc.gpsimd.memset(m["ident_b"][:, :], 0.0).then_inc(zeroed, 1)
            nc.gpsimd.memset(m["eps"][:, :], EPS).then_inc(zeroed, 1)
            pool.wait_ge(zeroed, 5)
            for t in (m["ident"], m["ident_b"]):
                nc.gpsimd.affine_select(out=t[:, :], in_=t[:, :], compare_op=ALU.not_equal, fill=1.0, base=0,
                                        pattern=[[-1, P]], channel_multiplier=1).then_inc(consts, 1)
            nc.gpsimd.affine_select(out=m["mask_b"][:, :], in_=m["mask_b"][:, :], compare_op=ALU.is_gt, fill=NEG,
                                    base=0, pattern=[[-1, P]], channel_multiplier=1).then_inc(consts, 1)

        @block.scalar
        def _(act):
            with nc.allow_non_contiguous_dma(reason="small vectors, feature on the partition"):
                act.dma_start(cond_in[:, :], c.rearrange("b (k p) -> p (b k)", p=P)).then_inc(cond_loaded, 16)
                for layer in range(DEPTH):
                    act.dma_start(m["ada_cols"][:, layer, :],
                                  b_ada[layer, :].rearrange("(k p) -> p k", p=P)).then_inc(small_in, 16)
                    act.dma_start(m["g_cols"][:, layer, 0:KT],
                                  g_pre[layer, :].rearrange("(k p) -> p k", p=P)).then_inc(small_in, 16)
                    act.dma_start(m["g_cols"][:, layer, KT:2 * KT],
                                  g_post[layer, :].rearrange("(k p) -> p k", p=P)).then_inc(small_in, 16)
                act.dma_start(lam_in[:, :, :], diff_lambda[0:1, :, :].broadcast_to([P, 4, HD])).then_inc(small_in, 16)
                act.dma_start(m["lam"][:, 1:2], diff_subln.rearrange("a d -> d a")).then_inc(small_in, 16)
            for q in (squares, root_done, left_kept, proj.hi_done):
                act.sem_inc(q, CREDIT)

            act.wait_ge(cond_loaded, 16)
            nc.scalar.activation(cond_sig[:, :], cond_in[:, :], ACT.Sigmoid).then_inc(cond_sig_done, 1)

            def statistics(r, s):
                act.wait_ge(loaded[s], 16 * r + 16)
                act.wait_ge(turned, done(R * r + s - R))
                nc.scalar.activation(xn[s][:, :], xt[s][:, :], ACT.Square,
                                     accum_out=st[:, 4 * s:4 * s + 1]).then_inc(squares, 1)
                act.wait_ge(mean_done, done(R * r + s))
                nc.scalar.activation(st[:, 4 * s + 2:4 * s + 3], st[:, 4 * s + 1:4 * s + 2],
                                     ACT.Sqrt).then_inc(root_done, 1)

            def keep_left(r, s):
                act.wait_ge(turned, done(R * r + s))
                t4 = T[s % 2][0][:, :].rearrange("p (k t) -> p k t", t=P)
                nc.scalar.activation(m["y"][:, 0:4, bass.ds((R * r + s) * P, P)], t4, ACT.Copy).then_inc(left_kept, 1)

            for r in range(ROUNDS):
                for s in range(R):
                    statistics(r, s)
                    if s:
                        keep_left(r, s - 1)
                keep_left(r, R - 1)
            act.wait_ge(row_done, 1)
            nc.scalar.activation(ada_row[:, :], row[0:1, :], ACT.Copy).then_inc(row_kept, 1)
            act.wait_ge(lam_sum, 2)
            nc.scalar.activation(lam_sums[:, 2:4], lam_sums[:, 0:2], ACT.Exp).then_inc(lam_exp, 1)
            proj.first_hi(act)

        @block.vector
        def _(dve):
            def link(instruction, n=[0]):
                n[0] += 1
                instruction.then_inc(chain, 1)
                dve.wait_ge(chain, n[0])

            for q in (scaled, mean_done, rstd_done, right_kept, proj.lo_done):
                dve.sem_inc(q, CREDIT)

            def normalise(r, s):
                t = R * r + s
                dve.wait_ge(squares, done(t))
                nc.vector.tensor_scalar(st[:, 4 * s + 1:4 * s + 2], st[:, 4 * s:4 * s + 1], 1.0 / D, EPS,
                                        ALU.mult, ALU.add).then_inc(mean_done, 1)
                dve.wait_ge(root_done, done(t))
                nc.vector.reciprocal(st[:, 4 * s + 3:4 * s + 4], st[:, 4 * s + 2:4 * s + 3]).then_inc(rstd_done, 1)
                dve.wait_ge(rstd_done, done(t))
                nc.vector.tensor_scalar(xn[s][:, :], xt[s][:, :], st[:, 4 * s + 3:4 * s + 4], None,
                                        ALU.mult).then_inc(scaled, 1)

            def keep_right(r, s):
                dve.wait_ge(turned, done(R * r + s))
                t4 = T[s % 2][1][:, :].rearrange("p (k t) -> p k t", t=P)
                nc.vector.tensor_copy(m["y"][:, 4:8, bass.ds((R * r + s) * P, P)], t4).then_inc(right_kept, 1)

            def accumulate(i):
                cols_i = slice(i * PIECE, (i + 1) * PIECE)
                first = OPS * BY_SUM.index(i)
                if first == 0:
                    dve.wait_ge(cond_done, 1)
                dve.wait_ge(ada_in[i], 16)
                for k in range(KT):
                    a, w, cond = acc[k % 2][:, cols_i], m["ada_w"][:, k, cols_i], m["cond"][:, k:k + 1]
                    if k < 2:
                        ins = nc.vector.tensor_scalar(a, w, cond, None, ALU.mult)
                    else:
                        dve.wait_ge(acc_done, first + k - 1)
                        ins = nc.vector.scalar_tensor_tensor(out=a, in0=w, scalar=cond, in1=a, op0=ALU.mult,
                                                             op1=ALU.add)
                    ins.then_inc(acc_done, 1)
                dve.wait_ge(acc_done, first + KT)
                nc.vector.tensor_tensor(acc[0][:, cols_i], acc[0][:, cols_i], acc[1][:, cols_i],
                                        ALU.add).then_inc(acc_done, 1)

            dve.wait_ge(cond_sig_done, 1)
            nc.vector.tensor_tensor(m["cond"][:, :], cond_in[:, :], cond_sig[:, :], ALU.mult).then_inc(cond_done, 1)
            for r in range(ROUNDS):
                for s in range(R):
                    normalise(r, s)
                    if s:
                        keep_right(r, s - 1)
                keep_right(r, R - 1)
                if r == 0:
                    accumulate(BY_SUM[0])
            dve.wait_ge(small_in, 16 * (2 + 3 * DEPTH))
            for j in range(2):
                nc.vector.tensor_tensor_reduce(out=lam_prod[:, j, :], in0=lam_in[:, 2 * j, :],
                                               in1=lam_in[:, 2 * j + 1, :], scale=1.0, scalar=0.0,
                                               op0=ALU.mult, op1=ALU.add,
                                               accum_out=lam_sums[:, j:j + 1]).then_inc(lam_sum, 1)
            for i in BY_SUM[1:]:
                accumulate(i)
            for kind in range(2):
                proj.first_lo(dve, kind)
            dve.wait_ge(lam_exp, 1)
            link(nc.vector.tensor_tensor(m["lam"][:, 0:1], lam_sums[:, 3:4], lam_sums[:, 2:3], ALU.subtract))
            link(nc.vector.tensor_scalar(m["lam"][:, 2:3], m["lam"][:, 0:1], -lam_init, None, ALU.add))
            link(nc.vector.tensor_scalar(m["lam"][:, 3:4], m["lam"][:, 1:2], 1.0 - lam_init, None, ALU.mult))
            dve.wait_ge(cols_done, 1)
            link(nc.vector.tensor_tensor(m["add_col"][0][:, :], cols[:, 0:KT], m["ada_cols"][:, 0, 0:KT], ALU.add))
            link(nc.vector.tensor_tensor(scale1[:, :], cols[:, KT:2 * KT], m["ada_cols"][:, 0, KT:2 * KT], ALU.add))
            nc.vector.scalar_tensor_tensor(out=m["mul_col"][0][:, :], in0=scale1[:, :], scalar=1.0,
                                           in1=m["g_cols"][:, 0, 0:KT], op0=ALU.add, op1=ALU.mult)

        @block.tensor
        def _(pe):
            pe.sem_inc(turned, CREDIT)
            pe.wait_ge(consts, 3)
            for r in range(ROUNDS):
                for s in range(R):
                    t = R * r + s
                    pe.wait_ge(scaled, done(t))
                    pe.wait_ge(left_kept, done(t - 2))
                    pe.wait_ge(right_kept, done(t - 2))
                    for k in range(KT):
                        mm = nc.tensor.transpose(T[s % 2][k // 4][:, k % 4 * P:(k % 4 + 1) * P],
                                                 xn[s][:, k * P:(k + 1) * P], m["ident"][:, :])
                    mm.then_inc(turned, 1)
            pe.wait_ge(cond_done, 1)
            pe.wait_ge(ada_in[BY_ROW], 16)
            for k in range(KT):
                mm = nc.tensor.matmul(row[0:1, :], m["cond"][:, k:k + 1],
                                      m["ada_w"][:, k, BY_ROW * PIECE:(BY_ROW + 1) * PIECE],
                                      start=(k == 0), stop=(k == KT - 1))
            mm.then_inc(row_done, 1)
            for i in range(PIECES):
                if i == BY_ROW:
                    pe.wait_ge(row_kept, 1)
                else:
                    pe.wait_ge(acc_done, OPS * (BY_SUM.index(i) + 1))
                for j in range(PIECE // P):
                    f = i * PIECE // P + j
                    if i == BY_ROW:
                        w, one = ada_row[0:1, j * P:(j + 1) * P], m["ones"][0:1, 0:1]
                    else:
                        w, one = acc[0][:, f * P:(f + 1) * P], m["ones"][:, 0:1]
                    mm = nc.tensor.matmul(cols[:, f:f + 1], w, one, start=True, stop=True)
            mm.then_inc(cols_done, 1)


class Modulation:

    def __init__(self, nc, m, layer, tag):
        self.nc, self.m, self.layer = nc, m, layer
        self.hi_done = nc.alloc_semaphore(f"{tag}_h_hi_done")
        self.full_done = nc.alloc_semaphore(f"{tag}_h_full_done")
        self.even_done = nc.alloc_semaphore(f"{tag}_h_lo_even_done")
        self.odd_done = nc.alloc_semaphore(f"{tag}_h_lo_odd_done")

    def columns(self, k):
        return self.m["mul_col"][self.layer][:, k:k + 1], self.m["add_col"][self.layer][:, k:k + 1]

    def scalar(self, act):
        for k in range(KT):
            mul, add = self.columns(k)
            self.nc.scalar.activation(self.m["h_hi"][:, k, :], self.m["y"][:, k, :], ACT.Identity, bias=add,
                                      scale=mul).then_inc(self.hi_done, 1)

    def vector(self, dve):
        for k in range(KT):
            mul, add = self.columns(k)
            h32 = self.m["h32"][k % 2][:, :]
            if k >= 3 and k % 2:
                dve.wait_ge(self.odd_done, k // 2)
            self.nc.vector.tensor_scalar(h32, self.m["y"][:, k, :], mul, add, ALU.mult,
                                         ALU.add).then_inc(self.full_done, 1)
            if k % 2 == 0:
                dve.wait_ge(self.full_done, k + 1)
                dve.wait_ge(self.hi_done, k + 1)
                self.nc.vector.tensor_tensor(self.m["h_lo"][:, k, :], h32, self.m["h_hi"][:, k, :].bitcast(F32),
                                             ALU.subtract).then_inc(self.even_done, 1)
                dve.wait_ge(self.even_done, k // 2 + 1)

    def gpsimd(self, pool):
        for k in range(1, KT, 2):
            pool.wait_ge(self.full_done, k + 1)
            pool.wait_ge(self.hi_done, k + 1)
            self.nc.gpsimd.tensor_tensor(self.m["h_lo"][:, k, :], self.m["h32"][1][:, :],
                                         self.m["h_hi"][:, k, :].bitcast(F32), ALU.subtract).then_inc(self.odd_done, 1)

    def ready(self, pe, k):
        pe.wait_ge(self.hi_done, k + 1)
        pe.wait_ge((self.even_done, self.odd_done)[k % 2], k // 2 + 1)


class Projection:

    def __init__(self, nc, m, w_in, tag):
        self.nc, self.m, self.w_in = nc, m, w_in
        self.bank = m["pm"][6:8]
        self.loaded = [nc.alloc_semaphore(f"{tag}_w_loaded{s}") for s in range(2)]
        self.hi_done = nc.alloc_semaphore(f"{tag}_w_hi_done")
        self.lo_done = nc.alloc_semaphore(f"{tag}_w_lo_done")
        self.group_done = nc.alloc_semaphore(f"{tag}_group_done")
        self.u_done = nc.alloc_semaphore(f"{tag}_u_done")
        self.sz_done = nc.alloc_semaphore(f"{tag}_sz_done")

    def first_loads(self, sp):
        for kind in range(2):
            self.nc.sync.dma_start(self.m["w_raw"][kind][:, :, :],
                                   self.w_in[:, kind * D:kind * D + P].rearrange("(k p) f -> p k f", p=P)
                                   ).then_inc(self.loaded[kind], 16)

    def first_hi(self, act):
        for kind in range(2):
            act.wait_ge(self.loaded[kind], 16)
            self.nc.scalar.activation(self.m["w_hi"][kind][:, :, :], self.m["w_raw"][kind][:, :, :],
                                      ACT.Copy).then_inc(self.hi_done, 1)

    def first_lo(self, dve, kind):
        dve.wait_ge(self.hi_done, done(kind))
        self.nc.vector.tensor_tensor(self.m["w_lo"][kind][:, :, :], self.m["w_raw"][kind][:, :, :],
                                     self.m["w_hi"][kind][:, :, :].bitcast(F32), ALU.subtract).then_inc(self.lo_done, 1)

    def load(self, sp, pair, kind):
        s = kind % 2
        sp.wait_ge(self.group_done, done(8 * pair + 2 * (kind - 2) + 1))
        sp.dma_start(self.m["w_raw"][s][:, :, :],
                     self.w_in[:, bass.ds(kind * D + pair * P, P)].rearrange("(k p) f -> p k f", p=P)
                     ).then_inc(self.loaded[s], 16)

    def split_hi(self, act, pair, kind):
        s = kind % 2
        act.wait_ge(self.loaded[s], 32 * pair + 16 * (kind // 2) + 16)
        act.wait_ge(self.group_done, done(8 * pair + 2 * (kind - 2) + 1))
        self.nc.scalar.activation(self.m["w_hi"][s][:, :, :], self.m["w_raw"][s][:, :, :],
                                  ACT.Copy).then_inc(self.hi_done, 1)

    def split_lo(self, pool, pair, kind):
        s = kind % 2
        pool.wait_ge(self.hi_done, done(4 * pair + kind))
        self.nc.gpsimd.tensor_tensor(self.m["w_lo"][s][:, :, :], self.m["w_raw"][s][:, :, :],
                                     self.m["w_hi"][s][:, :, :].bitcast(F32), ALU.subtract).then_inc(self.lo_done, 1)

    def multiply(self, pe, pair, first, last, modulation=None):
        m, nc = self.m, self.nc
        for n in range(first, last):
            group, i = divmod(n, GROUP)
            kind, half = divmod(group, 2)
            k, part = divmod(i, MULS)
            if modulation and kind == 0:
                k, j = divmod(n, 2 * MULS)
                half, part = divmod(j, MULS)
                i = k * MULS + part
            s = kind % 2
            if i == 0:
                if half == 0:
                    pe.wait_ge(self.hi_done, done(4 * pair + kind))
                    pe.wait_ge(self.lo_done, done(4 * pair + kind))
                if kind == 0:
                    pe.wait_ge(self.sz_done, done(2 * (pair - 1) + half))
                else:
                    pe.wait_ge(self.u_done, done(6 * pair + 2 * (kind - 1) + half))
            if modulation and kind == 0 and part == 0:
                modulation.ready(pe, k)
            w = (m["w_hi"], m["w_hi"], m["w_lo"])[part][s]
            h = (m["h_hi"], m["h_lo"], m["h_hi"])[part]
            mm = nc.tensor.matmul(self.bank[half][:, :], w[:, k, :], h[:, k, half * HALF:(half + 1) * HALF],
                                  start=(i == 0), stop=(i == GROUP - 1))
            if i == GROUP - 1:
                mm.then_inc(self.group_done, 1)

    def keep(self, engine, pair, kind, half, pack):
        if kind == 0:
            engine.wait_ge(pack.lo_done, done(4 * pair - 1))
            engine.wait_ge(pack.hi_done, done(6 * pair - 1))
            engine.wait_ge(pack.key_lo_done, done(2 * pair - 1))
        engine.wait_ge(self.group_done, done(8 * pair + 2 * kind + half))
        dst = (self.m["uq"], self.m["uk"], self.m["uv"])[kind][:, half * HALF:(half + 1) * HALF]
        if engine is self.nc.vector:
            ins = self.nc.vector.tensor_copy(dst, self.bank[half][:, :])
        else:
            ins = self.nc.scalar.activation(dst, self.bank[half][:, :], ACT.Copy)
        ins.then_inc(self.u_done, 1)


class Packing:

    def __init__(self, nc, m, tag):
        self.nc, self.m = nc, m
        self.hi_done = nc.alloc_semaphore(f"{tag}_pack_hi_done")
        self.lo_done = nc.alloc_semaphore(f"{tag}_pack_lo_done")
        self.key_lo_done = nc.alloc_semaphore(f"{tag}_key_lo_done")

    def rows(self, h):
        return slice(HD * h, HD * h + HD), slice(HD - HD * h, 2 * HD - HD * h)

    def hi(self, act, n):
        own, other = self.rows(n % 2)
        src = self.m["uq" if n < 2 else "uk"]
        dst = self.m["q" if n < 2 else "k_hi"][n % 2]
        self.nc.scalar.activation(dst[other if n >= 4 else own, :], src[own, :], ACT.Copy).then_inc(self.hi_done, 1)

    def key_lo(self, dve, pair, h):
        own, _ = self.rows(h)
        dve.wait_ge(self.hi_done, done(6 * pair + 2 + h))
        self.nc.vector.tensor_tensor(self.m["k_lo"][h][own, :], self.m["uk"][own, :],
                                     self.m["k_hi"][h][own, :].bitcast(F32),
                                     ALU.subtract).then_inc(self.key_lo_done, 1)

    def lo(self, dve, pair, n):
        h = n % 2
        own, other = self.rows(h)
        m, v = self.m, self.nc.vector
        if n < 2:
            dve.wait_ge(self.hi_done, done(6 * pair + n))
            v.tensor_tensor(m["q"][h][other, :], m["uq"][own, :], m["q"][h][own, :].bitcast(F32),
                            ALU.subtract).then_inc(self.lo_done, 1)
        else:
            self.key_lo(dve, pair, h)
            dve.wait_ge(self.key_lo_done, done(2 * pair + h))
            v.tensor_copy(m["k_lo"][h][other, :], m["k_lo"][h][own, :].bitcast(F32)).then_inc(self.lo_done, 1)

    def ready(self, pe, pair):
        pe.wait_ge(self.hi_done, done(6 * pair + 5))
        pe.wait_ge(self.lo_done, done(4 * pair + 3))


class OutProjection:

    def __init__(self, nc, m, sb, layer):
        self.nc, self.m = nc, m
        self.parked = [sb(f"o{layer}_parked{t}", [P, D], F32, 96 + 4 * t) for t in range(AHEAD)]
        self.y_hi = [sb(f"o{layer}_ahead_hi{s}", [P, KT, P], F32R, 112 + 8 * s) for s in range(2)]
        self.y_lo = [sb(f"o{layer}_ahead_lo{s}", [P, KT, P], F32R, 116 - 8 * s) for s in range(2)]
        self.bank = m["pm"][6:8]

        def sem(name):
            return nc.alloc_semaphore(f"o{layer}_{name}")

        self.gate_stored = sem("gate_stored")
        self.weights_in = [sem(f"w_loaded{k}") for k in range(KT // 2)]
        self.weights_hi_done, self.weights_lo_done = sem("w_hi_done"), sem("w_lo_done")
        self.hi_done, self.lo_done = sem("hi_done"), sem("lo_done")
        self.product, self.kept = sem("product"), sem("kept")

    def load_weights(self, sp, w_out):
        for k in range(0, KT, 2):
            sp.dma_start(self.m["wo_raw"][:, k:k + 2, :], w_out[k * P:(k + 2) * P, :]
                         .rearrange("(k p) f -> p k f", p=P)).then_inc(self.weights_in[k // 2], 16)

    def weights_hi(self, act, k):
        act.wait_ge(self.weights_in[k // 2], 16)
        self.nc.scalar.activation(self.m["wo_hi"][:, k, :], self.m["wo_raw"][:, k, :],
                                  ACT.Copy).then_inc(self.weights_hi_done, 1)

    def weights_lo(self, engine, k):
        engine.wait_ge(self.weights_hi_done, k + 1)
        engine.tensor_tensor(self.m["wo_lo"][:, k, :], self.m["wo_raw"][:, k, :],
                             self.m["wo_hi"][:, k, :].bitcast(F32), ALU.subtract).then_inc(self.weights_lo_done, 1)

    def split_hi(self, act, t):
        if t >= 2:
            act.wait_ge(self.product, done(2 * (t - 2) + 1))
        self.nc.scalar.activation(self.y_hi[t % 2][:, :, :], self.m["y"][:, :, t * P:(t + 1) * P],
                                  ACT.Copy).then_inc(self.hi_done, 1)

    def split_lo(self, dve, t):
        dve.wait_ge(self.hi_done, done(t))
        self.nc.vector.tensor_tensor(self.y_lo[t % 2][:, :, :], self.m["y"][:, :, t * P:(t + 1) * P],
                                     self.y_hi[t % 2][:, :, :].bitcast(F32), ALU.subtract).then_inc(self.lo_done, 1)

    def multiply(self, pe, first, last, proj):
        for n in range(first, last):
            group, i = divmod(n, GROUP)
            t, h = divmod(group, 2)
            k, part = (i // 2, (0, 2)[i % 2]) if i < 2 * KT else (i - 2 * KT, 1)
            if n == 0:
                pe.wait_ge(self.weights_hi_done, KT)
            if n == 2 * KT:
                pe.wait_ge(self.weights_lo_done, KT)
            if i == 0:
                if h == 0:
                    pe.wait_ge(self.lo_done, done(t))
                if t == 0:
                    pe.wait_ge(proj.sz_done, done(2 * (PAIRS - 1) + h))
                else:
                    pe.wait_ge(self.kept, 2 * (t - 1) + h + 1)
            y, w = ((self.y_hi, "wo_hi"), (self.y_hi, "wo_lo"), (self.y_lo, "wo_hi"))[part]
            mm = self.nc.tensor.matmul(self.bank[h][:, :], y[t % 2][:, k, :],
                                       self.m[w][:, k, h * HALF:(h + 1) * HALF], start=(i == 0), stop=(i == GROUP - 1))
            if i == GROUP - 1:
                mm.then_inc(self.product, 1)

    def keep(self, act, t, h):
        act.wait_ge(self.product, done(2 * t + (h if t < AHEAD - 1 else 1)))
        self.nc.scalar.activation(self.parked[t][:, h * HALF:(h + 1) * HALF], self.bank[h][:, :],
                                  ACT.Copy).then_inc(self.kept, 1)


def ahead(multiplies):
    return [[divmod(g, 2) for g in range(2 * AHEAD) if f < (g + 1) * GROUP <= l] for f, l in multiplies]


def stick_breaking(nc, m, proj, outp, w_out, w_ada, gate_rows):
    TILES = 2 * NT
    ORDER = [(t // 2 % 2, t // 4 * 2 + t % 2) for t in range(TILES)]
    CH = [len(widths(i)) for _, i in ORDER]
    CAT = [sum(CH[:t]) for t in range(TILES)]
    NCH = sum(CH)
    NB = NCH + 2
    LAG = 2
    STEPS = TILES + LAG + 1
    GROUPS = 2 * NG
    L, T, O = m["pm"][0:3], m["pm"][3:5], m["pm"][5]
    assert NCH % 3 == 0 and NB % 2 == 0
    RA = 3

    def ring(t):
        return t % RA

    EARLY = 3
    Z = shares(2 * GROUP, [1] * EARLY + [0] * (STEPS - EARLY))
    QK = shares(4 * GROUP, [0] * EARLY + [7 + ORDER[t][1] for t in range(EARLY, TILES)] + [0] * (STEPS - TILES))
    V = shares(2 * GROUP, [0] * TILES + [1] * (STEPS - TILES))
    Z_AT, U_AT, SPLIT_AT = schedule(Z, QK, V, (2, 2, 2))
    OUT = shares(KT, [0] * 7 + [1] * 5 + [0] * (STEPS - 12))
    MULTIPLY = shares(AHEAD * 2 * GROUP, [0] * 12 + [1] * (STEPS - 12))
    AHEAD_AT = [{10: (0, 1), 14: (2,), 16: (3,), STEPS - 1: (AHEAD,)}.get(s, ()) for s in range(STEPS)]

    def sem(name):
        return nc.alloc_semaphore("s_" + name)

    logits, gates, scanned, weighted = sem("logits"), sem("gates"), sem("scanned"), sem("weighted")
    turned, hi_done, lo_done = sem("turned"), sem("hi_done"), sem("lo_done")
    o_done, part_done, y_done = sem("o_done"), sem("part_done"), sem("y_done")
    zsig, one_set, summed = sem("zsig"), sem("one_set"), sem("summed")
    ada_in, ada_done, ada_kept = sem("ada_loaded"), sem("ada_done"), sem("ada_kept")
    ada_scaled, ada_summed = sem("ada_scaled"), sem("ada_summed")
    chain, gate_turned, gate_kept = sem("chain"), sem("gate_turned"), sem("gate_kept")
    gate_rows_sb = m["o_part"]
    ADA = 4
    pack = Packing(nc, m, "s")
    modulation = Modulation(nc, m, 0, "s")

    def last_batch_before(p, t):
        if t >= RA:
            return NB * p + 2 + CAT[t - RA] + CH[t - RA] - 1
        prev = max(u for u in range(TILES) if ring(u) == ring(t))
        return NB * (p - 1) + 2 + CAT[prev] + CH[prev] - 1

    with nc.Block() as block:

        @block.sync
        def _(sp):
            for kind in range(2, 4):
                proj.load(sp, 0, kind)

            def ada(p, i):
                layer, at = (1, (3 * p + i) * P) if i < 3 else (0, 2 * D + p * P)
                sp.wait_ge(ada_summed, done(ADA * p + i - 1))
                sp.dma_start(m["ada_piece"][:, :, :], w_ada[layer, :, bass.ds(at, P)]
                             .rearrange("(k p) f -> p k f", p=P)).then_inc(ada_in, 16)

            with sp.Fori(0, PAIRS - 1) as p:
                proj.load(sp, p + 1, 0)
                ada(p, 0)
                proj.load(sp, p + 1, 1)
                ada(p, 1)
                ada(p, 2)
                proj.load(sp, p + 1, 2)
                ada(p, 3)
                proj.load(sp, p + 1, 3)
            for i in range(2):
                ada(PAIRS - 1, i)
            sp.wait_ge(proj.group_done, done(8 * PAIRS - 1))
            outp.load_weights(sp, w_out)
            for i in range(2, ADA):
                ada(PAIRS - 1, i)
            sp.wait_ge(gate_kept, 1)
            sp.dma_start(gate_rows.rearrange("l (k f) -> (l k) f", f=P),
                         gate_rows_sb[0:DEPTH * KT, 0:P]).then_inc(outp.gate_stored, 16)

        @block.tensor
        def _(pe):
            for q in (outp.product, proj.group_done, logits, turned, o_done, ada_done):
                pe.sem_inc(q, CREDIT)

            def score(p, t):
                h, i = ORDER[t]
                qs = m["q"][h][:, i * P:(i + 1) * P]
                if t == 0:
                    pack.ready(pe, p)
                for n, (k0, w) in enumerate(widths(i)):
                    ch = CAT[t] + n
                    bank = L[ch % 3]
                    pe.wait_ge(gates, done(NCH * p + ch - 3))
                    diag = k0 + w == P * (i + 1)
                    nc.tensor.matmul(bank[:, 0:w], qs, m["k_hi"][h][:, k0:k0 + w], start=True, stop=False)
                    mm = nc.tensor.matmul(bank[:, 0:w], qs, m["k_lo"][h][:, k0:k0 + w], start=False, stop=not diag)
                    if diag:
                        mm = nc.tensor.matmul(bank[:, w - P:w], m["ident_b"][:, :], m["mask_b"][:, :],
                                              start=False, stop=True)
                    mm.then_inc(logits, 1)

            def turn(p, t):
                i = ORDER[t][1]
                pe.wait_ge(weighted, done(TILES * p + t))
                a = m["a"][ring(t)]
                for n, (k0, w) in enumerate(widths(i)):
                    b = 2 + CAT[t] + n
                    pe.wait_ge(lo_done, done(NB * p + b - 2))
                    for j in range(w // P):
                        at = S - P * (i + 1) + k0 + j * P
                        mm = nc.tensor.transpose(T[b % 2][:, j * P:(j + 1) * P], a[:, at:at + P], m["ident"][:, :])
                    mm.then_inc(turned, 1)

            def values(p, g):
                h, gg = g % 2, g // 2
                pe.wait_ge(lo_done, done(NB * p + 2 + CAT[2 * g + 1] + CH[2 * g + 1] - 1))
                pe.wait_ge(summed, done(GROUPS * p + g - 1))
                if g % 2:
                    i = g // 2
                    pe.wait_ge(ada_summed, done(ADA * p + i))
                    pe.wait_ge(ada_kept, done(ADA * p + i - 1))
                    nc.tensor.matmul(O[:, GW:GW + 1], m["ada_sum"][:, :], m["ones"][:, 0:1], start=True,
                                     stop=True).then_inc(ada_done, 1)
                tiles = 2 * gg + 2
                for j in range(tiles):
                    c0 = P if j == tiles - 1 else 0
                    for w in (m["wt_hi"], m["wt_lo"]):
                        mm = nc.tensor.matmul(O[:, c0:GW], m["v"][h][:, j, :], w[:, j, c0:GW],
                                              start=(j == 0 and w is m["wt_hi"]),
                                              stop=(j == tiles - 1 and w is m["wt_lo"]))
                mm.then_inc(o_done, 1)

            def turn_values(p):
                for b in range(2):
                    pe.wait_ge(proj.u_done, done(6 * p + 4 + b))
                    pe.wait_ge(lo_done, done(NB * p + b - 2))
                    for j in range(4):
                        at = (4 * b + j) * P
                        mm = nc.tensor.transpose(T[b][:, j * P:(j + 1) * P], m["uv"][:, at:at + P], m["ident"][:, :])
                    mm.then_inc(turned, 1)

            def project_share(p, s, project, half):
                for of, (f, l), at in ((p, Z[s], 6 * GROUP), (p + 1, QK[s], 0), (p + 1, V[s], 4 * GROUP)):
                    if project or at == 6 * GROUP:
                        mid = f + (l - f) // 2
                        proj.multiply(pe, of, at + (f, mid)[half], at + (mid, l)[half])

            def pair(p, project):
                for s in range(STEPS):
                    if s == 1:
                        turn_values(p)
                    if s < TILES:
                        score(p, s)
                    project_share(p, s, project, 0)
                    if not project:
                        outp.multiply(pe, MULTIPLY[s][0], sum(MULTIPLY[s]) // 2, proj)
                    if s >= 4 and s % 2 == 0:
                        values(p, s // 2 - 2)
                    if LAG <= s < TILES + LAG:
                        turn(p, s - LAG)
                    project_share(p, s, project, 1)
                    if not project:
                        outp.multiply(pe, sum(MULTIPLY[s]) // 2, MULTIPLY[s][1], proj)

            proj.multiply(pe, 0, 0, 6 * GROUP, modulation)
            with pe.Fori(0, PAIRS - 1) as p:
                pair(p, True)
            pair(PAIRS - 1, False)
            pe.wait_ge(chain, 4)
            nc.tensor.transpose(T[0][0:DEPTH * KT, 0:P], m["gate_col"][:, :], m["ident"][:, :]).then_inc(gate_turned, 1)

        @block.scalar
        def _(act):
            for q in (outp.hi_done, pack.hi_done, gates, hi_done, part_done, zsig):
                act.sem_inc(q, CREDIT)

            def sigmoids(p, t):
                i = ORDER[t][1]
                for n, (k0, w) in enumerate(widths(i)):
                    ch = CAT[t] + n
                    at = S - P * (i + 1) + k0
                    act.wait_ge(logits, done(NCH * p + ch))
                    if n == 0:
                        act.wait_ge(turned, done(last_batch_before(p, t)))
                        act.wait_ge(scanned, done(TILES * p + t - 2))
                    nc.scalar.activation(m["a"][ring(t)][:, at:at + w], L[ch % 3][:, 0:w], ACT.Sigmoid, scale=SCALE)
                    nc.scalar.activation(m["b"][t % 2][:, at:at + w], L[ch % 3][:, 0:w], ACT.Sigmoid,
                                         scale=-SCALE).then_inc(gates, 1)

            def weights_hi(p, t):
                i = ORDER[t][1]
                for n, (k0, w) in enumerate(widths(i)):
                    b = 2 + CAT[t] + n
                    act.wait_ge(turned, done(NB * p + b))
                    if n == 0:
                        act.wait_ge(o_done, done(GROUPS * p + t // 2 - 1))
                    c0 = (t % 2) * P
                    dst = m["wt_hi"][:, k0 // P:(k0 + w) // P, c0:c0 + P]
                    nc.scalar.activation(dst, T[b % 2][:, 0:w].rearrange("p (j q) -> p j q", q=P),
                                         ACT.Copy).then_inc(hi_done, 1)

            def other_part(p, g):
                h = g % 2
                own, other = slice(HD * h, HD * h + HD), slice(HD - HD * h, 2 * HD - HD * h)
                act.wait_ge(o_done, done(GROUPS * p + g))
                act.wait_ge(y_done, done(GROUPS * p + g - 1))
                nc.scalar.activation(m["o_part"][own, :], O[other, 0:GW], ACT.Copy).then_inc(part_done, 1)

            def z_gate(p, half):
                y = m["y"][:, :, :].rearrange("r k t -> r (k t)")
                act.wait_ge(proj.group_done, done(8 * p + 6 + half))
                nc.scalar.activation(y[:, bass.ds(p * S + half * HALF, HALF)], proj.bank[half][:, :],
                                     ACT.Sigmoid).then_inc(zsig, 1)

            def values_hi(p):
                for b in range(2):
                    act.wait_ge(turned, done(NB * p + b))
                    act.wait_ge(o_done, done(GROUPS * p - 1))
                    t3 = T[b][:, :].rearrange("p (j d) -> p j d", d=P)
                    nc.scalar.activation(m["v"][0][:, 4 * b:4 * b + 4, 0:HD], t3[:, :, 0:HD], ACT.Copy)
                    nc.scalar.activation(m["v"][1][:, 4 * b:4 * b + 4, HD:P], t3[:, :, HD:P],
                                         ACT.Copy).then_inc(hi_done, 1)

            def pack_hi(p, n):
                if n in (0, 2):
                    act.wait_ge(proj.u_done, done(6 * p + n + 1))
                if n == 0:
                    act.wait_ge(logits, done(NCH * p - 1))
                pack.hi(act, n)

            def pair(p, project):
                for s in range(STEPS):
                    for t in () if project else AHEAD_AT[s]:
                        act.wait_ge(y_done, done(GROUPS * p + 2 * (t // 2) + 1))
                        outp.split_hi(act, t)
                    if s < TILES:
                        sigmoids(p, s)
                    if project:
                        for kind in SPLIT_AT[s]:
                            proj.split_hi(act, p + 1, kind)
                    if s == 1:
                        values_hi(p)
                    if s >= 4 and s % 2 == 0:
                        other_part(p, s // 2 - 2)
                    if LAG <= s < TILES + LAG:
                        weights_hi(p, s - LAG)
                    if s >= TILES and project:
                        for n in ((0, 1, 2, 3), (4, 5), ())[s - TILES]:
                            pack_hi(p + 1, n)
                    for half in Z_AT[s]:
                        z_gate(p, half)
                    for t, h in () if project else ahead(MULTIPLY)[s]:
                        outp.keep(act, t, h)
                    for k in () if project else range(*OUT[s]):
                        outp.weights_hi(act, k)

            modulation.scalar(act)
            for kind in range(2):
                proj.split_hi(act, 0, 2 + kind)
                for n in range(2):
                    pack_hi(0, 2 * kind + n)
            for n in range(4, 6):
                pack_hi(0, n)
            with act.Fori(0, PAIRS - 1) as p:
                pair(p, True)
            pair(PAIRS - 1, False)

        @block.vector
        def _(dve):
            for q in (outp.lo_done, proj.u_done, proj.sz_done, pack.lo_done, pack.key_lo_done, scanned, lo_done, summed,
                      ada_kept, ada_summed, y_done):
                dve.sem_inc(q, CREDIT)
            for r in range(2):
                nc.vector.memset(m["stick"][r][:, S:S + 1], 1.0).then_inc(one_set, 1)
            modulation.vector(dve)

            def scan(p, t):
                i = ORDER[t][1]
                at = S - P * (i + 1)
                dve.wait_ge(gates, done(NCH * p + CAT[t] + CH[t] - 1))
                dve.wait_ge(weighted, done(TILES * p + t - 2))
                keep = m["b"][t % 2][:, at:S][:, ::-1]
                nc.vector.tensor_tensor_scan(m["stick"][t % 2][:, at:S][:, ::-1], keep, keep, 1.0, ALU.mult,
                                             ALU.bypass).then_inc(scanned, 1)

            def weights_lo(p, t):
                i = ORDER[t][1]
                for n, (k0, w) in enumerate(widths(i)):
                    b = 2 + CAT[t] + n
                    dve.wait_ge(hi_done, done(NB * p + b))
                    c0 = (t % 2) * P
                    js = slice(k0 // P, (k0 + w) // P)
                    nc.vector.tensor_tensor(m["wt_lo"][:, js, c0:c0 + P],
                                            T[b % 2][:, 0:w].rearrange("p (j q) -> p j q", q=P),
                                            m["wt_hi"][:, js, c0:c0 + P].bitcast(F32),
                                            ALU.subtract).then_inc(lo_done, 1)

            def add_parts(p, g):
                h, gg = g % 2, g // 2
                own = slice(HD * h, HD * h + HD)
                dve.wait_ge(part_done, done(GROUPS * p + g))
                if g % 2:
                    i = g // 2
                    at = 3 * KT + 3 * p + i if i < 3 else 2 * KT + p
                    dve.wait_ge(ada_done, done(ADA * p + i))
                    col = m["ada_cols"][:, :, :].rearrange("p l f -> p (l f)")[:, bass.ds(at, 1)]
                    nc.vector.tensor_tensor(col, O[:, GW:GW + 1], col, ALU.add).then_inc(ada_kept, 1)
                nc.vector.tensor_tensor(m["o_part"][own, :], O[own, 0:GW], m["o_part"][own, :],
                                        ALU.add).then_inc(summed, 1)
                dve.wait_ge(summed, done(GROUPS * p + g))
                y = m["y"][own, :, :].rearrange("r k t -> r (k t)")[:, bass.ds(p * S + gg * GW, GW)]
                nc.vector.tensor_tensor(y, m["o_part"][own, :], y, ALU.mult).then_inc(y_done, 1)

            def z_gate(p, half):
                y = m["y"][:, :, :].rearrange("r k t -> r (k t)")
                dve.wait_ge(zsig, done(2 * p + half))
                sz = y[:, bass.ds(p * S + half * HALF, HALF)]
                nc.vector.tensor_tensor(sz, proj.bank[half][:, :], sz, ALU.mult).then_inc(proj.sz_done, 1)

            def sum_ada(p, i):
                dve.wait_ge(ada_scaled, done(ADA * p + i))
                dve.wait_ge(ada_done, done(ADA * p + i - 1))
                nc.vector.tensor_reduce(m["ada_sum"][:, :], m["ada_piece"][:, :, :].rearrange("p k f -> p f k"),
                                        axis=AX.X, op=ALU.add).then_inc(ada_summed, 1)

            def finish_ada():
                g, ada = m["g_cols"], m["ada_cols"][:, :, :].rearrange("p l f -> p (l f)")
                n = 0

                def link(ins):
                    nonlocal n
                    n += 1
                    ins.then_inc(chain, 1)
                    dve.wait_ge(chain, n)

                tt = nc.vector.tensor_tensor
                dve.wait_ge(ada_kept, done(ADA * PAIRS - 1))
                link(nc.vector.scalar_tensor_tensor(out=m["mul_col"][1][:, :], in0=ada[:, 4 * KT:5 * KT], scalar=1.0,
                                                    in1=g[:, 1, 0:KT], op0=ALU.add, op1=ALU.mult))
                link(nc.vector.tensor_copy(m["add_col"][1][:, :], ada[:, 3 * KT:4 * KT]))
                for layer in range(DEPTH):
                    cols = slice((3 * layer + 2) * KT, (3 * layer + 3) * KT)
                    link(tt(m["gate_col"][:, layer * KT:(layer + 1) * KT], ada[:, cols], g[:, layer, KT:2 * KT],
                            ALU.mult))
                dve.wait_ge(gate_turned, 1)
                dve.wait_ge(y_done, done(GROUPS * PAIRS - 1))
                nc.vector.tensor_copy(gate_rows_sb[0:DEPTH * KT, 0:P], T[0][0:DEPTH * KT, 0:P]).then_inc(gate_kept, 1)

            def values_lo(p):
                for b in range(2):
                    dve.wait_ge(hi_done, done(NB * p + b))
                    t3 = T[b][:, :].rearrange("p (j d) -> p j d", d=P)
                    js = slice(4 * b, 4 * b + 4)
                    nc.vector.tensor_tensor(m["v"][0][:, js, HD:P], t3[:, :, 0:HD],
                                            m["v"][0][:, js, 0:HD].bitcast(F32), ALU.subtract)
                    nc.vector.tensor_tensor(m["v"][1][:, js, 0:HD], t3[:, :, HD:P],
                                            m["v"][1][:, js, HD:P].bitcast(F32), ALU.subtract).then_inc(lo_done, 1)

            def keep_u(p, kind, half):
                if kind == 2:
                    dve.wait_ge(turned, done(NB * (p - 1) + half))
                proj.keep(dve, p, kind, half, pack)

            def pair(p, project):
                for s in range(STEPS):
                    for t in () if project else AHEAD_AT[s]:
                        outp.split_lo(dve, t)
                    if s >= 4 and s % 2 == 0:
                        add_parts(p, s // 2 - 2)
                    if LAG <= s < TILES + LAG:
                        weights_lo(p, s - LAG)
                    if s < TILES:
                        scan(p, s)
                    if s % 4 == 3 and s // 4 < ADA:
                        sum_ada(p, s // 4)
                    for half in Z_AT[s]:
                        z_gate(p, half)
                    if s == 1:
                        values_lo(p)
                    if project:
                        if s >= TILES:
                            for n in ((0, 1, 2), (3,), ())[s - TILES]:
                                pack.lo(dve, p + 1, n)
                        for kind, half in U_AT[s]:
                            keep_u(p + 1, kind, half)
                    for k in () if project else range(*OUT[s]):
                        if k % 2 == 0:
                            outp.weights_lo(dve, k)

            for kind in range(2):
                for half in range(2):
                    keep_u(0, kind, half)
            for n in range(4):
                pack.lo(dve, 0, n)
            for half in range(2):
                keep_u(0, 2, half)
            with dve.Fori(0, PAIRS - 1) as p:
                pair(p, True)
            pair(PAIRS - 1, False)
            finish_ada()

        @block.gpsimd
        def _(pool):
            for q in (weighted, ada_scaled):
                pool.sem_inc(q, CREDIT)
            pool.wait_ge(one_set, 2)

            def weigh(p, t):
                i = ORDER[t][1]
                at = S - P * (i + 1)
                pool.wait_ge(scanned, done(TILES * p + t))
                a = m["a"][ring(t)]
                nc.gpsimd.tensor_tensor(a[:, at:S], a[:, at:S], m["stick"][t % 2][:, at + 1:S + 1],
                                        ALU.mult).then_inc(weighted, 1)

            def scale_ada(p, i):
                pool.wait_ge(ada_in, 16 * (ADA * p + i) + 16)
                cond = m["cond"][:, :].rearrange("p (k o) -> p k o", o=1).broadcast_to([P, KT, P])
                nc.gpsimd.tensor_tensor(m["ada_piece"][:, :, :], m["ada_piece"][:, :, :], cond,
                                        ALU.mult).then_inc(ada_scaled, 1)

            def pair(p, project):
                for s in range(STEPS):
                    if s < TILES:
                        weigh(p, s)
                    for kind in SPLIT_AT[s] if project else ():
                        proj.split_lo(pool, p + 1, kind)
                    if s % 4 == 1 and s // 4 < ADA:
                        scale_ada(p, s // 4)
                    for k in () if project else range(*OUT[s]):
                        if k % 2:
                            outp.weights_lo(pool, k)

            modulation.gpsimd(pool)
            for kind in range(2, 4):
                proj.split_lo(pool, 0, kind)
            with pool.Fori(0, PAIRS - 1) as p:
                pair(p, True)
            pair(PAIRS - 1, False)

def differential(nc, m, proj, outp, w_out):
    MAPS = 2
    BCH = [len(widths(t)) for t in range(NT)]
    BAT = [sum(BCH[:t]) for t in range(NT)]
    CAT = [MAPS * b for b in BAT]
    NCH = MAPS * sum(BCH)
    NB = sum(BCH) + 2
    LAG = 2
    STEPS = NT + LAG + 1
    L, T, O = m["pm"][0:3], m["pm"][3:5], m["pm"][5]
    RA = 3
    assert NCH % 3 == 0 and NB % 2 == 0

    def ring(t):
        return t % RA

    EARLY = 2
    Z = shares(2 * GROUP, [1] * EARLY + [0] * (STEPS - EARLY))
    QK = shares(4 * GROUP, [0] * EARLY + [14] + [4 + t for t in range(EARLY + 1, NT)] + [0] * (STEPS - NT))
    V = shares(2 * GROUP, [0] * NT + [1] * (STEPS - NT))
    Z_AT, U_AT, SPLIT_AT = schedule(Z, QK, V, (2, 1, 1))
    OUT = shares(KT, [0] * 4 + [1] * 3 + [0] * (STEPS - 7))
    MULTIPLY = shares(AHEAD * 2 * GROUP, [0] * 7 + [1] * (STEPS - 7))
    AHEAD_AT = [{7: (0, 1), 8: (2,), 9: (3,), STEPS - 1: (AHEAD,)}.get(s, ()) for s in range(STEPS)]

    def sem(name):
        return nc.alloc_semaphore("d_" + name)

    logits, biased, negmax, expd = sem("logits"), sem("biased"), sem("negmax"), sem("expd")
    inverse, inverse_lam, weighted = sem("inverse"), sem("inverse_lam"), sem("weighted")
    turned, hi_done, lo_done = sem("turned"), sem("hi_done"), sem("lo_done")
    o_done, o_kept, o_squared, sum_done = sem("o_done"), sem("o_kept"), sem("o_squared"), sem("sum_done")
    log_done, rs_done, normed, y_done = sem("log_done"), sem("rs_done"), sem("normed"), sem("y_done")
    zsig, z_gated, b_scaled = sem("zsig"), sem("z_gated"), sem("b_scaled")
    dist_done, table = sem("dist_done"), sem("table")
    halved, seen = sem("halved"), sem("seen")
    pack = Packing(nc, m, "d")
    modulation = Modulation(nc, m, 1, "d")
    dist = m["dist"]
    st = m["stat"]

    def col(t, name, n=0):
        at = {"max": 0, "neg": 4, "sum": 6, "inv": 8, "lam": 10}[name]
        return 16 * (t % 2) + at + n

    def last_batch_before(p, t):
        if t >= RA:
            return NB * p + 2 + BAT[t - RA] + BCH[t - RA] - 1
        prev = max(u for u in range(NT) if ring(u) == ring(t))
        return NB * (p - 1) + 2 + BAT[prev] + BCH[prev] - 1

    with nc.Block() as block:

        @block.sync
        def _(sp):
            for kind in range(2, 4):
                proj.load(sp, 0, kind)
            with sp.Fori(0, PAIRS - 1) as p:
                for kind in range(4):
                    proj.load(sp, p + 1, kind)
            sp.wait_ge(proj.group_done, done(8 * PAIRS - 1))
            outp.load_weights(sp, w_out)

        @block.tensor
        def _(pe):
            for q in (outp.product, proj.group_done, logits, turned, o_done, sum_done):
                pe.sem_inc(q, CREDIT)

            def score(p, t, n):
                if t == 0 and n == 0:
                    pack.ready(pe, p)
                qs = m["q"][n][:, t * P:(t + 1) * P]
                for c, (k0, w) in enumerate(widths(t)):
                    ch = CAT[t] + n * BCH[t] + c
                    bank = L[ch % 3]
                    pe.wait_ge(biased, done(NCH * p + ch - 3))
                    nc.tensor.matmul(bank[:, 0:w], qs, m["k_hi"][n][:, k0:k0 + w], start=True, stop=False)
                    nc.tensor.matmul(bank[:, 0:w], qs, m["k_lo"][n][:, k0:k0 + w], start=False,
                                     stop=True).then_inc(logits, 1)

            def turn(p, t):
                pe.wait_ge(weighted, done(NT * p + t))
                a = m["a"][ring(t)]
                for n, (k0, w) in enumerate(widths(t)):
                    b = 2 + BAT[t] + n
                    pe.wait_ge(lo_done, done(NB * p + b - 2))
                    for j in range(w // P):
                        at = S - P * (t + 1) + k0 + j * P
                        mm = nc.tensor.transpose(T[b % 2][:, j * P:(j + 1) * P], a[:, at:at + P], m["ident"][:, :])
                    mm.then_inc(turned, 1)

            def values(p, g):
                pe.wait_ge(lo_done, done(NB * p + 2 + BAT[2 * g + 1] + BCH[2 * g + 1] - 1))
                pe.wait_ge(log_done, done(NG * p + g - 1))
                tiles = 2 * g + 2
                for j in range(tiles):
                    c0 = P if j == tiles - 1 else 0
                    for i, (v, w) in enumerate(((0, "wt_hi"), (0, "wt_lo"), (1, "wt_hi"))):
                        mm = nc.tensor.matmul(O[:, c0:GW], m["v"][v][:, j, :], m[w][:, j, c0:GW],
                                              start=(j == 0 and i == 0), stop=(j == tiles - 1 and i == MULS - 1))
                mm.then_inc(o_done, 1)

            def sum_squares(p, g):
                pe.wait_ge(o_squared, done(NG * p + g))
                pe.wait_ge(o_kept, done(NG * p + g))
                nc.tensor.matmul(O[:, GW:2 * GW], m["ones"][:, :], m["sub_sq"][g % 2][:, :], start=True,
                                 stop=True).then_inc(sum_done, 1)

            def turn_values(p):
                for b in range(2):
                    pe.wait_ge(proj.u_done, done(6 * p + 4 + b))
                    pe.wait_ge(lo_done, done(NB * p + b - 2))
                    for j in range(4):
                        at = (4 * b + j) * P
                        mm = nc.tensor.transpose(T[b][:, j * P:(j + 1) * P], m["uv"][:, at:at + P], m["ident"][:, :])
                    mm.then_inc(turned, 1)

            def project_share(p, s, project, half):
                for of, (f, l), at in ((p, Z[s], 6 * GROUP), (p + 1, QK[s], 0), (p + 1, V[s], 4 * GROUP)):
                    if project or at == 6 * GROUP:
                        mid = f + (l - f) // 2
                        proj.multiply(pe, of, at + (f, mid)[half], at + (mid, l)[half])

            def pair(p, project):
                for s in range(STEPS):
                    if s == 1:
                        turn_values(p)
                    if s < NT:
                        score(p, s, 0)
                    project_share(p, s, project, 0)
                    if not project:
                        outp.multiply(pe, MULTIPLY[s][0], sum(MULTIPLY[s]) // 2, proj)
                    if s < NT:
                        score(p, s, 1)
                    if s >= 4 and s % 2 == 0:
                        values(p, s // 2 - 2)
                    if LAG <= s < NT + LAG:
                        turn(p, s - LAG)
                    project_share(p, s, project, 1)
                    if not project:
                        outp.multiply(pe, sum(MULTIPLY[s]) // 2, MULTIPLY[s][1], proj)
                    if s >= 4 and s % 2 == 0:
                        sum_squares(p, s // 2 - 2)

            proj.multiply(pe, 0, 0, 6 * GROUP, modulation)
            with pe.Fori(0, PAIRS - 1) as p:
                pair(p, True)
            pair(PAIRS - 1, False)

        @block.scalar
        def _(act):
            for q in (outp.hi_done, pack.hi_done, expd, hi_done, o_kept, o_squared, log_done, rs_done, zsig, b_scaled,
                      proj.u_done):
                act.sem_inc(q, CREDIT)

            def exponentials(p, t):
                at = S - P * (t + 1)
                for n in range(MAPS):
                    e = (m["a"][ring(t)], m["b"][t % 2])[n]
                    neg, total = col(t, "neg", n), col(t, "sum", n)
                    act.wait_ge(negmax, done(MAPS * (NT * p + t) + n))
                    nc.scalar.activation(e[:, at:S], e[:, at:S], ACT.Exp, bias=st[:, neg:neg + 1], scale=SCALE,
                                         accum_out=st[:, total:total + 1]).then_inc(expd, 1)

            def scale_second(p, t):
                at, lam = S - P * (t + 1), col(t, "lam")
                b = m["b"][t % 2][:, at:S]
                act.wait_ge(inverse_lam, done(NT * p + t))
                nc.scalar.activation(b, b, ACT.Copy, scale=st[:, lam:lam + 1]).then_inc(b_scaled, 1)

            def keep_u(p, kind, half):
                if kind == 2:
                    act.wait_ge(turned, done(NB * (p - 1) + half))
                proj.keep(act, p, kind, half, pack)

            def weights_hi(p, t):
                for n, (k0, w) in enumerate(widths(t)):
                    b = 2 + BAT[t] + n
                    act.wait_ge(turned, done(NB * p + b))
                    if n == 0:
                        act.wait_ge(o_done, done(NG * p + t // 2 - 1))
                    c0 = (t % 2) * P
                    dst = m["wt_hi"][:, k0 // P:(k0 + w) // P, c0:c0 + P]
                    nc.scalar.activation(dst, T[b % 2][:, 0:w].rearrange("p (j q) -> p j q", q=P),
                                         ACT.Copy).then_inc(hi_done, 1)

            def keep_output(p, g):
                act.wait_ge(o_done, done(NG * p + g))
                act.wait_ge(sum_done, done(NG * p + g - 2))
                if g == 0:
                    act.wait_ge(z_gated, done(p))
                else:
                    act.wait_ge(y_done, done(NG * p + g - 2))
                nc.scalar.activation(m["sub_sq"][g % 2][:, :], O[:, 0:GW], ACT.Square).then_inc(o_squared, 1)
                nc.scalar.activation(m["sub_o"][g % 2][:, :], O[:, 0:GW], ACT.Copy).then_inc(o_kept, 1)

            def inverse_root(p, g):
                act.wait_ge(sum_done, done(NG * p + g))
                nc.scalar.activation(m["sub_rs"][0][:, :], O[:, GW:2 * GW], ACT.Ln, scale=1.0 / P,
                                     bias=m["eps"][:, 0:1]).then_inc(log_done, 1)
                act.wait_ge(log_done, done(NG * p + g))
                act.wait_ge(normed, done(NG * p + g - 1))
                nc.scalar.activation(m["sub_rs"][1][:, :], m["sub_rs"][0][:, :], ACT.Exp,
                                     scale=-0.5).then_inc(rs_done, 1)

            def z_gate(p):
                y = m["y"][:, :, :].rearrange("r k t -> r (k t)")[:, bass.ds(p * S, S)]
                act.wait_ge(proj.sz_done, done(2 * p + 1))
                act.wait_ge(y_done, done(NG * p - 1))
                nc.scalar.activation(m["z_sig"][:, :], y, ACT.Sigmoid).then_inc(zsig, 1)
                act.preload_act_table_set("natural_log_exp_and_others")

            def values_hi(p):
                for b in range(2):
                    act.wait_ge(turned, done(NB * p + b))
                    act.wait_ge(o_done, done(NG * p - 1))
                    t3 = T[b][:, :].rearrange("p (j d) -> p j d", d=P)
                    nc.scalar.activation(m["v"][0][:, 4 * b:4 * b + 4, :], t3, ACT.Copy).then_inc(hi_done, 1)

            def pack_hi(p, n):
                if n in (0, 2):
                    act.wait_ge(proj.u_done, done(6 * p + n + 1))
                if n == 0:
                    act.wait_ge(logits, done(NCH * p - 1))
                pack.hi(act, n)

            def pair(p, project):
                for s in range(STEPS):
                    for t in () if project else AHEAD_AT[s]:
                        act.wait_ge(y_done, done(NG * p + t // 2))
                        outp.split_hi(act, t)
                    if s >= 5 and s % 2 == 1:
                        inverse_root(p, (s - 5) // 2)
                    if 1 <= s <= NT:
                        scale_second(p, s - 1)
                    if s < NT:
                        exponentials(p, s)
                    if project:
                        for kind in SPLIT_AT[s]:
                            proj.split_hi(act, p + 1, kind)
                    if s == 1:
                        values_hi(p)
                    if s >= 4 and s % 2 == 0:
                        keep_output(p, s // 2 - 2)
                    if LAG <= s < NT + LAG:
                        weights_hi(p, s - LAG)
                    if s == EARLY:
                        z_gate(p)
                    if s >= NT and project:
                        for n in ((0, 1, 2, 3), (4, 5), ())[s - NT]:
                            pack_hi(p + 1, n)
                    for kind, half in U_AT[s] if project else ():
                        keep_u(p + 1, kind, half)
                    for t, h in () if project else ahead(MULTIPLY)[s]:
                        outp.keep(act, t, h)
                    for k in () if project else range(*OUT[s]):
                        outp.weights_hi(act, k)
                inverse_root(p, NG - 1)

            modulation.scalar(act)
            act.preload_act_table_set("natural_log_exp_and_others")
            for kind in range(2):
                for half in range(2):
                    keep_u(0, kind, half)
                proj.split_hi(act, 0, 2 + kind)
                for n in range(2):
                    pack_hi(0, 2 * kind + n)
            for n in range(4, 6):
                pack_hi(0, n)
            for half in range(2):
                keep_u(0, 2, half)
            with act.Fori(0, PAIRS - 1) as p:
                pair(p, True)
            pair(PAIRS - 1, False)

        @block.vector
        def _(dve):
            for q in (outp.lo_done, proj.sz_done, z_gated, pack.lo_done, pack.key_lo_done, biased, negmax,
                      inverse, inverse_lam, weighted, lo_done, halved):
                dve.sem_inc(q, CREDIT)
            modulation.vector(dve)
            slope8 = 8.0 * 2.0 ** (-8.0 / PAIRS)
            dve.wait_ge(dist_done, 1)
            nc.vector.tensor_scalar(m["bias"][:, :], dist[:, :], -slope8, None, ALU.mult).then_inc(table, 1)
            nc.vector.tensor_scalar(m["b"][1][:, :], dist[:, :], slope8, None, ALU.mult).then_inc(table, 1)
            dve.wait_ge(table, 2)
            nc.vector.tensor_tensor(m["bias"][:, :], m["bias"][:, :], m["b"][1][:, :], ALU.min).then_inc(table, 1)
            dve.wait_ge(table, 3)
            nc.vector.memset(m["bias"][0:CHUNK, S - CHUNK:S], NEG).then_inc(table, 1)
            dve.wait_ge(table, 4)

            def add_bias(p, t):
                if t == 0:
                    dve.wait_ge(halved, done(p - 1))
                for n in range(MAPS):
                    x = (m["a"][ring(t)], m["b"][t % 2])[n]
                    if n == 0:
                        dve.wait_ge(turned, done(last_batch_before(p, t)))
                    for c, (k0, w) in enumerate(widths(t)):
                        ch = CAT[t] + n * BCH[t] + c
                        at = S - P * (t + 1) + k0
                        mx = col(t, "max", 2 * n + c)
                        dve.wait_ge(logits, done(NCH * p + ch))
                        dve.sem_inc(seen, 1)
                        nc.vector.tensor_tensor_reduce(
                            out=x[:, at:at + w], in0=L[ch % 3][:, 0:w], in1=m["bias"][:, at:at + w], scale=1.0,
                            scalar=-3e38, op0=ALU.add, op1=ALU.max, accum_out=st[:, mx:mx + 1]).then_inc(biased, 1)
                    dve.wait_ge(biased, done(NCH * p + ch))
                    mx, neg = col(t, "max", 2 * n), col(t, "neg", n)
                    if BCH[t] == 2:
                        ins = nc.vector.tensor_scalar(st[:, neg:neg + 1], st[:, mx:mx + 1], st[:, mx + 1:mx + 2],
                                                      -SCALE, ALU.max, ALU.mult)
                    else:
                        ins = nc.vector.tensor_scalar(st[:, neg:neg + 1], st[:, mx:mx + 1], -SCALE, None, ALU.mult)
                    ins.then_inc(negmax, 1)
                if t == NT - 1:
                    nc.vector.tensor_scalar(m["bias"][:, :], m["bias"][:, :], 0.5, None, ALU.mult).then_inc(halved, 1)

            def invert(p, t):
                total, inv, lam = col(t, "sum"), col(t, "inv"), col(t, "lam")
                dve.wait_ge(expd, done(MAPS * (NT * p + t) + 1))
                nc.vector.reciprocal(st[:, inv:inv + 2], st[:, total:total + 2]).then_inc(inverse, 1)
                dve.wait_ge(inverse, done(NT * p + t))
                nc.vector.tensor_scalar(st[:, lam:lam + 1], st[:, inv + 1:inv + 2], m["lam"][:, 2:3], None,
                                        ALU.mult).then_inc(inverse_lam, 1)

            def combine(p, t):
                at, inv = S - P * (t + 1), col(t, "inv")
                a, b = m["a"][ring(t)], m["b"][t % 2]
                dve.wait_ge(b_scaled, done(NT * p + t))
                nc.vector.scalar_tensor_tensor(out=a[:, at:S], in0=a[:, at:S], scalar=st[:, inv:inv + 1],
                                               in1=b[:, at:S], op0=ALU.mult, op1=ALU.add).then_inc(weighted, 1)

            def weights_lo(p, t):
                for n, (k0, w) in enumerate(widths(t)):
                    b = 2 + BAT[t] + n
                    dve.wait_ge(hi_done, done(NB * p + b))
                    c0 = (t % 2) * P
                    js = slice(k0 // P, (k0 + w) // P)
                    nc.vector.tensor_tensor(m["wt_lo"][:, js, c0:c0 + P],
                                            T[b % 2][:, 0:w].rearrange("p (j q) -> p j q", q=P),
                                            m["wt_hi"][:, js, c0:c0 + P].bitcast(F32),
                                            ALU.subtract).then_inc(lo_done, 1)

            def keep_z(p, half):
                y = m["y"][:, :, :].rearrange("r k t -> r (k t)")[:, bass.ds(p * S + half * HALF, HALF)]
                dve.wait_ge(proj.group_done, done(8 * p + 6 + half))
                nc.vector.tensor_copy(y, proj.bank[half][:, :]).then_inc(proj.sz_done, 1)

            def z_gate(p):
                y = m["y"][:, :, :].rearrange("r k t -> r (k t)")[:, bass.ds(p * S, S)]
                dve.wait_ge(zsig, done(p))
                nc.vector.scalar_tensor_tensor(out=y, in0=y, scalar=m["lam"][:, 3:4], in1=m["z_sig"][:, :],
                                               op0=ALU.mult, op1=ALU.mult).then_inc(z_gated, 1)

            def values_lo(p):
                for b in range(2):
                    dve.wait_ge(hi_done, done(NB * p + b))
                    t3 = T[b][:, :].rearrange("p (j d) -> p j d", d=P)
                    js = slice(4 * b, 4 * b + 4)
                    nc.vector.tensor_tensor(m["v"][1][:, js, :], t3, m["v"][0][:, js, :].bitcast(F32),
                                            ALU.subtract).then_inc(lo_done, 1)

            def pair(p, project):
                for s in range(STEPS):
                    for t in () if project else AHEAD_AT[s]:
                        outp.split_lo(dve, t)
                    if 1 <= s <= NT:
                        invert(p, s - 1)
                    if s < NT:
                        add_bias(p, s)
                    if 1 <= s <= NT:
                        combine(p, s - 1)
                    for half in Z_AT[s]:
                        keep_z(p, half)
                    if s == 1:
                        values_lo(p)
                    if s == EARLY + 1:
                        z_gate(p)
                    if LAG <= s < NT + LAG:
                        weights_lo(p, s - LAG)
                    if project:
                        if s >= NT:
                            for n in ((0, 1), (2, 3), ())[s - NT]:
                                pack.lo(dve, p + 1, n)
                    for k in () if project else range(*OUT[s]):
                        if k % 2 == 0:
                            outp.weights_lo(dve, k)

            for n in range(4):
                pack.lo(dve, 0, n)
            with dve.Fori(0, PAIRS - 1) as p:
                pair(p, True)
            pair(PAIRS - 1, False)

        @block.gpsimd
        def _(pool):
            for q in (normed, y_done):
                pool.sem_inc(q, CREDIT)
            nc.gpsimd.iota(dist[:, :], pattern=[[-1, S]], base=S - P, channel_multiplier=1).then_inc(dist_done, 1)

            def norm_output(p, g):
                o = m["sub_o"][g % 2][:, :]
                pool.wait_ge(rs_done, done(NG * p + g))
                pool.wait_ge(o_kept, done(NG * p + g))
                nc.gpsimd.tensor_tensor(o, o, m["sub_rs"][1][:, :], ALU.mult).then_inc(normed, 1)
                pool.wait_ge(normed, done(NG * p + g))
                if g == 0:
                    pool.wait_ge(z_gated, done(p))
                y = m["y"][:, :, :].rearrange("r k t -> r (k t)")[:, bass.ds(p * S + g * GW, GW)]
                nc.gpsimd.tensor_tensor(y, o, y, ALU.mult).then_inc(y_done, 1)

            def pair(p, project):
                for s in range(STEPS):
                    for kind in SPLIT_AT[s] if project else ():
                        proj.split_lo(pool, p + 1, kind)
                    if s >= 5 and s % 2 == 1:
                        norm_output(p, (s - 5) // 2)
                    for k in () if project else range(*OUT[s]):
                        if k % 2:
                            outp.weights_lo(pool, k)
                norm_output(p, NG - 1)

            modulation.gpsimd(pool)
            for kind in range(2, 4):
                proj.split_lo(pool, 0, kind)
            with pool.Fori(0, PAIRS - 1) as p:
                pair(p, True)
            pair(PAIRS - 1, False)


def project_out(nc, m, sb, layer, outp, source, target, gate_rows, next_proj):
    def sem(name):
        return nc.alloc_semaphore(f"o{layer}_{name}")

    FRESH = NT - AHEAD
    y_hi = [outp.y_hi[0], sb(f"o{layer}_y_hi", [P, KT, P], F32R, 120)]
    y_lo = [outp.y_lo[0], sb(f"o{layer}_y_lo", [P, KT, P], F32R, 124)]
    xt = [sb(f"o{layer}_x{s}", [P, D], F32, 128 + 4 * s) for s in range(2)]
    res = [sb(f"o{layer}_res{s}", [P, D], F32, 136 + 4 * s) for s in range(2)]
    gate = sb(f"o{layer}_gate", [P, D], F32, 144)
    xn = [sb(f"o{layer}_xn{s}", [P, D], F32, 148 + 4 * s) for s in range(2)]
    st = m["stat"]
    bank = m["pm"][0:4]
    T = [m["pm"][4:6], m["pm"][6:8]]
    gate_in = sem("gate_loaded")
    loaded = [sem(f"x_loaded{s}") for s in range(2)]
    stored = [sem(f"stored{s}") for s in range(2)]
    hi_done, lo_done, product = outp.hi_done, outp.lo_done, outp.product
    squares, summed, mean_done, root_done, rstd_done = (sem("squares"), sem("summed"), sem("mean_done"),
                                                        sem("root_done"), sem("rstd_done"))
    scaled, added = sem("scaled"), sem("added")
    if next_proj:
        squares2, mean2, root2, rstd2 = sem("next_squares"), sem("next_mean"), sem("next_root"), sem("next_rstd")
        scaled2, turned, left_kept, right_kept = sem("next_scaled"), sem("turned"), sem("left_kept"), sem("right_kept")
    SQ, SUM, MEAN, ROOT, RSTD, SQ2, MEAN2, ROOT2, RSTD2 = 0, 2, 3, 4, 5, 6, 7, 8, 9

    def col(n, at):
        return st[:, 16 * (n % 2) + at:16 * (n % 2) + at + 1]

    def tokens(n):
        return (n // 2 + (AHEAD if n % 2 else 0)) * P

    def raw(n, h):
        if n % 2 == 0:
            return outp.parked[n // 2][:, h * HALF:(h + 1) * HALF]
        return bank[2 * (n // 2 % 2) + h][:, :]

    def rows(n):
        return slice(tokens(n), tokens(n) + P)

    def add(engine, n):
        engine.wait_ge(loaded[n % 2], 16 * (n // 2) + 16)
        engine.tensor_tensor(res[n % 2][:, :], res[n % 2][:, :], xt[n % 2][:, :], ALU.add).then_inc(added, 1)

    with nc.Block() as block:

        @block.sync
        def _(sp):
            for n in range(2):
                sp.dma_start(xt[n][:, :], source[rows(n), :]).then_inc(loaded[n], 16)
            if layer == 0:
                sp.wait_ge(outp.gate_stored, 16)
            sp.dma_start(gate[:, :], gate_rows[layer:layer + 1, :].broadcast_to([P, D])).then_inc(gate_in, 16)
            for n in range(NT):
                sp.wait_ge(added, n + 1)
                sp.dma_start(target[rows(n), :], res[n % 2][:, :]).then_inc(stored[n % 2], 16)
                if n + 2 < NT:
                    sp.dma_start(xt[n % 2][:, :], source[rows(n + 2), :]).then_inc(loaded[n % 2], 16)
                if n == NT - 2 and next_proj:
                    next_proj.first_loads(sp)
            for s in range(2):
                sp.wait_ge(stored[s], 16 * (NT // 2))

        @block.scalar
        def _(act):
            if next_proj:
                act.sem_inc(next_proj.hi_done, CREDIT)

            def split(j):
                t = AHEAD + j
                if j >= 2:
                    act.wait_ge(product, done(2 * (t - 2) + 1))
                nc.scalar.activation(y_hi[j % 2][:, :, :], m["y"][:, :, t * P:(t + 1) * P],
                                     ACT.Copy).then_inc(hi_done, 1)

            def finish(n):
                if n >= 2:
                    act.wait_ge(stored[n % 2], 16 * (n // 2))
                    if next_proj:
                        act.wait_ge(scaled2, n - 1)
                for h in range(2):
                    if n % 2:
                        act.wait_ge(product, done(2 * (AHEAD + n // 2) + h))
                    nc.scalar.activation(res[n % 2][:, h * HALF:(h + 1) * HALF], raw(n, h), ACT.Square,
                                         accum_out=col(n, SQ + h)).then_inc(squares, 1)
                act.wait_ge(mean_done, n + 1)
                nc.scalar.activation(col(n, ROOT), col(n, MEAN), ACT.Sqrt).then_inc(root_done, 1)

            def renormalise(n):
                if not next_proj:
                    return
                act.wait_ge(added, n + 1)
                if n >= 2:
                    act.wait_ge(turned, n - 1)
                nc.scalar.activation(xn[n % 2][:, :], res[n % 2][:, :], ACT.Square,
                                     accum_out=col(n, SQ2)).then_inc(squares2, 1)
                act.wait_ge(mean2, n + 1)
                nc.scalar.activation(col(n, ROOT2), col(n, MEAN2), ACT.Sqrt).then_inc(root2, 1)

            def keep_left(n):
                if not next_proj:
                    return
                act.wait_ge(turned, n + 1)
                t4 = T[n % 2][0][:, :].rearrange("p (k t) -> p k t", t=P)
                nc.scalar.activation(m["y"][:, 0:4, rows(n)], t4, ACT.Copy).then_inc(left_kept, 1)

            split(1)
            finish(0)
            renormalise(0)
            for j in range(FRESH):
                finish(2 * j + 1)
                if j + 2 < FRESH:
                    split(j + 2)
                if j + 1 < FRESH:
                    finish(2 * j + 2)
                elif next_proj:
                    next_proj.first_hi(act)
                renormalise(2 * j + 1)
                keep_left(2 * j)
                if j + 1 < FRESH:
                    renormalise(2 * j + 2)
                keep_left(2 * j + 1)

        @block.vector
        def _(dve):
            if next_proj:
                dve.sem_inc(next_proj.lo_done, CREDIT)

            def split(j):
                t = AHEAD + j
                dve.wait_ge(hi_done, done(t))
                nc.vector.tensor_tensor(y_lo[j % 2][:, :, :], m["y"][:, :, t * P:(t + 1) * P],
                                        y_hi[j % 2][:, :, :].bitcast(F32), ALU.subtract).then_inc(lo_done, 1)

            def finish(n):
                dve.wait_ge(squares, 2 * n + 2)
                nc.vector.tensor_tensor(col(n, SUM), col(n, SQ), col(n, SQ + 1), ALU.add).then_inc(summed, 1)
                dve.wait_ge(summed, n + 1)
                nc.vector.tensor_scalar(col(n, MEAN), col(n, SUM), 1.0 / D, EPS, ALU.mult,
                                        ALU.add).then_inc(mean_done, 1)
                dve.wait_ge(root_done, n + 1)
                nc.vector.reciprocal(col(n, RSTD), col(n, ROOT)).then_inc(rstd_done, 1)
                dve.wait_ge(rstd_done, n + 1)
                for h in range(2):
                    cols = slice(h * HALF, (h + 1) * HALF)
                    nc.vector.scalar_tensor_tensor(out=res[n % 2][:, cols], in0=raw(n, h), scalar=col(n, RSTD),
                                                   in1=gate[:, cols], op0=ALU.mult, op1=ALU.mult).then_inc(scaled, 1)
                if n == NT - 1:
                    dve.wait_ge(scaled, 2 * n + 2)
                    dve.wait_ge(added, n)
                    add(dve, n)

            def renormalise(n):
                if not next_proj:
                    return
                dve.wait_ge(squares2, n + 1)
                nc.vector.tensor_scalar(col(n, MEAN2), col(n, SQ2), 1.0 / D, EPS, ALU.mult, ALU.add).then_inc(mean2, 1)
                dve.wait_ge(root2, n + 1)
                nc.vector.reciprocal(col(n, RSTD2), col(n, ROOT2)).then_inc(rstd2, 1)
                dve.wait_ge(rstd2, n + 1)
                nc.vector.tensor_scalar(xn[n % 2][:, :], res[n % 2][:, :], col(n, RSTD2), None,
                                        ALU.mult).then_inc(scaled2, 1)

            def keep_right(n):
                if not next_proj:
                    return
                dve.wait_ge(turned, n + 1)
                t4 = T[n % 2][1][:, :].rearrange("p (k t) -> p k t", t=P)
                nc.vector.tensor_copy(m["y"][:, 4:8, rows(n)], t4).then_inc(right_kept, 1)

            split(1)
            dve.wait_ge(gate_in, 16)
            finish(0)
            renormalise(0)
            for j in range(FRESH):
                finish(2 * j + 1)
                if j + 2 < FRESH:
                    split(j + 2)
                if j + 1 < FRESH:
                    finish(2 * j + 2)
                elif next_proj:
                    next_proj.first_lo(dve, 0)
                renormalise(2 * j + 1)
                keep_right(2 * j)
                if j + 1 == FRESH and next_proj:
                    next_proj.first_lo(dve, 1)
                if j + 1 < FRESH:
                    renormalise(2 * j + 2)
                keep_right(2 * j + 1)

        @block.gpsimd
        def _(pool):
            for n in range(NT - 1):
                pool.wait_ge(scaled, 2 * n + 2)
                add(pool, n)

        @block.tensor
        def _(pe):
            def multiply(j):
                pe.wait_ge(lo_done, done(AHEAD + j))
                for h in range(2):
                    if j >= 2:
                        pe.wait_ge(scaled, 2 * (2 * (j - 2) + 1) + h + 1)
                    for k in range(KT):
                        for i, (y, w) in enumerate(((y_hi, "wo_hi"), (y_hi, "wo_lo"), (y_lo, "wo_hi"))):
                            mm = nc.tensor.matmul(bank[2 * (j % 2) + h][:, :], y[j % 2][:, k, :],
                                                  m[w][:, k, h * HALF:(h + 1) * HALF],
                                                  start=(k == 0 and i == 0), stop=(k == KT - 1 and i == MULS - 1))
                    mm.then_inc(product, 1)

            def turn(n):
                if not next_proj:
                    return
                pe.wait_ge(scaled2, n + 1)
                if n >= 2:
                    pe.wait_ge(left_kept, n - 1)
                    pe.wait_ge(right_kept, n - 1)
                for k in range(KT):
                    mm = nc.tensor.transpose(T[n % 2][k // 4][:, k % 4 * P:(k % 4 + 1) * P],
                                             xn[n % 2][:, k * P:(k + 1) * P], m["ident"][:, :])
                mm.then_inc(turned, 1)

            multiply(0)
            for j in range(FRESH):
                if j + 1 < FRESH:
                    multiply(j + 1)
                for n in range(2 * j, 2 * j + 2):
                    turn(n)


_INS = ["x", "c", "w_ada", "b_ada", "g_pre", "g_post", "w_in", "w_out", "diff_lambda", "diff_subln"]


def kernel(**inputs):
    import numpy as np
    import concourse.bacc as bacc
    from concourse.bass_utils import run_bass_kernel_spmd

    nc = bacc.Bacc("TRN2", target_bir_lowering=False, num_devices=1)
    arrays, args = {}, {}
    for name in _INS:
        a = np.ascontiguousarray(inputs[name])
        if name == "x":
            a = a.reshape(S, D)
        arrays[f"in_{name}_dram"] = a
        args[name] = nc.dram_tensor(f"in_{name}_dram", a.shape, mybir.dt.from_np(a.dtype), kind="ExternalInput").ap()
    args["out"] = nc.dram_tensor("out_dram", [S, D], F32, kind="ExternalOutput").ap()
    trunk(nc, **args)
    r = run_bass_kernel_spmd(nc, [arrays], core_ids=[0])
    return r.results[0]["out_dram"].reshape(1, S, D)
```
